# Optimizing a Trainium2 kernel written in Bass

```python
import jax
import jax.numpy as jnp
from jax import lax
import numpy as np

D_MODEL = 1024
BATCH = 1
SEQ = 256
DEPTH = 1
DEC_BATCH = 1
DEC_SEQ = 1024
PAST_LEN = 512

GRID_W = 64
HEAD_DIM = 64
N_Q_HEADS = 8
N_KV_HEADS = 2
Q_GROUP = N_Q_HEADS // N_KV_HEADS
ATTN_Q_W = N_Q_HEADS * HEAD_DIM
ATTN_KV_W = N_KV_HEADS * HEAD_DIM
Q_BLOCK = 128
ROPE_THETA = 10000.0
DN_HEADS = 8
DN_DK = 64
DN_DV = 64
DN_QK_W = DN_HEADS * DN_DK
DN_V_W = DN_HEADS * DN_DV
DN_CONV = 5
DN_CHUNK = 64
D_FF = -(-8 * D_MODEL // (3 * 256)) * 256
EPS = 1e-6
IN_WIDTHS = (ATTN_Q_W, ATTN_KV_W, ATTN_KV_W, DN_QK_W, DN_QK_W, DN_V_W, DN_V_W,
             2 * DN_HEADS, 2 * DN_HEADS, D_MODEL, D_MODEL)
IN_W = sum(IN_WIDTHS)

kernel_name = 'hybrid_gqa_gdn_prefix_diffusion_step'

def rms_norm(x, g):
    xf = x.astype(jnp.float32)
    y = xf * lax.rsqrt(jnp.mean(xf * xf, axis=-1, keepdims=True) + EPS)
    return (y * g.astype(jnp.float32)).astype(x.dtype)

def l2_norm(x):
    xf = x.astype(jnp.float32)
    return xf * lax.rsqrt(jnp.sum(xf * xf, axis=-1, keepdims=True) + EPS)

def rope_1d(x, pos):
    half = x.shape[-1] // 2
    inv = ROPE_THETA ** (-jnp.arange(half, dtype=jnp.float32) / half)
    ang = pos[:, None] * inv[None, :]
    cos = jnp.cos(ang)[None, :, None, :]
    sin = jnp.sin(ang)[None, :, None, :]
    x1, x2 = x[..., :half], x[..., half:]
    return jnp.concatenate([x1 * cos - x2 * sin, x2 * cos + x1 * sin], axis=-1)

def axial_rope(x):
    n_tokens = x.shape[1]
    rows = n_tokens // GRID_W
    row_pos = jnp.repeat(jnp.arange(rows, dtype=jnp.float32), GRID_W)
    col_pos = jnp.tile(jnp.arange(GRID_W, dtype=jnp.float32), rows)
    xf = x.astype(jnp.float32)
    ax = HEAD_DIM // 2
    out = jnp.concatenate([rope_1d(xf[..., :ax], row_pos), rope_1d(xf[..., ax:], col_pos)], axis=-1)
    return out.astype(x.dtype)

def block_attention(q, k, v):
    b, sq = q.shape[0], q.shape[1]
    nb = sq // Q_BLOCK
    qb = q.reshape(b, nb, Q_BLOCK, N_KV_HEADS, Q_GROUP, HEAD_DIM).transpose(1, 0, 2, 3, 4, 5)
    scale = HEAD_DIM ** -0.5

    def one_block(q_blk):
        s = jnp.einsum('bqhgd,bkhd->bhgqk', q_blk, k, preferred_element_type=jnp.float32) * scale
        p = jax.nn.softmax(s, axis=-1)
        return jnp.einsum('bhgqk,bkhd->bqhgd', p.astype(v.dtype), v)

    o = lax.map(one_block, qb)
    return o.transpose(1, 0, 2, 3, 4, 5).reshape(b, sq, ATTN_Q_W)

def short_conv(x, w):
    ch = x.shape[-1]
    pad = (DN_CONV - 1) // 2
    y = lax.conv_general_dilated(x, w[:, None, :].astype(x.dtype), window_strides=(1,),
                                 padding=[(pad, pad)], dimension_numbers=('NWC', 'WIO', 'NWC'),
                                 feature_group_count=ch)
    return jax.nn.silu(y)

def chunk_gated_delta(q, k, v, g, beta, s0):
    b, s, h, dk = q.shape
    dv = v.shape[-1]
    n = s // DN_CHUNK
    c = DN_CHUNK

    def chunks(a):
        return a.reshape(b, n, c, *a.shape[2:]).swapaxes(2, 3)

    q = chunks(q) * (dk ** -0.5)
    k = chunks(k)
    v = chunks(v)
    g = jnp.cumsum(chunks(g), axis=-1)
    beta = chunks(beta)
    k_beta = k * beta[..., None]
    v_beta = v * beta[..., None]
    tril_incl = jnp.tril(jnp.ones((c, c), dtype=bool))
    tril_strict = jnp.tril(jnp.ones((c, c), dtype=bool), -1)
    decay = jnp.exp(jnp.where(tril_incl, g[..., :, None] - g[..., None, :], -jnp.inf))
    lmat = jnp.where(tril_strict, jnp.einsum('bnhid,bnhjd->bnhij', k_beta, k) * decay, 0.0)
    eye = jnp.eye(c, dtype=jnp.float32)
    t_inv = lax.linalg.triangular_solve(eye + lmat, jnp.broadcast_to(eye, lmat.shape),
                                        left_side=True, lower=True, unit_diagonal=True)
    u = jnp.einsum('bnhij,bnhjd->bnhid', t_inv, v_beta)
    w = jnp.einsum('bnhij,bnhjd->bnhid', t_inv, k_beta * jnp.exp(g)[..., None])
    a_intra = jnp.where(tril_incl, jnp.einsum('bnhid,bnhjd->bnhij', q, k) * decay, 0.0)

    def step(state, xs):
        q_i, k_i, u_i, w_i, g_i, a_i = xs
        v_new = u_i - jnp.einsum('bhcd,bhde->bhce', w_i, state)
        o_i = (jnp.einsum('bhcd,bhde->bhce', q_i * jnp.exp(g_i)[..., None], state)
               + jnp.einsum('bhij,bhje->bhie', a_i, v_new))
        g_last = g_i[..., -1]
        state = (state * jnp.exp(g_last)[..., None, None]
                 + jnp.einsum('bhcd,bhce->bhde', k_i * jnp.exp(g_last[..., None] - g_i)[..., None], v_new))
        return state, o_i

    xs = tuple(a.swapaxes(0, 1) for a in (q, k, u, w, g, a_intra))
    s_final, o = lax.scan(step, s0.astype(jnp.float32), xs)
    o = o.transpose(1, 0, 3, 2, 4).reshape(b, s, h, dv)
    return o, s_final

def delta_branch(dq, dk_, dv_, dz, dbeta, dalpha, conv_w, a_log, dt_bias, dn_norm_g, s_f, s_b):
    b, s = dq.shape[0], dq.shape[1]
    qkv = short_conv(jnp.concatenate([dq, dk_, dv_], axis=-1), conv_w)
    cq, ck, cv = jnp.split(qkv, [DN_QK_W, 2 * DN_QK_W], axis=-1)
    cq = l2_norm(cq.reshape(b, s, DN_HEADS, DN_DK))
    ck = l2_norm(ck.reshape(b, s, DN_HEADS, DN_DK))
    cv = cv.reshape(b, s, DN_HEADS, DN_DV).astype(jnp.float32)
    beta = jax.nn.sigmoid(dbeta.astype(jnp.float32)).reshape(b, s, 2, DN_HEADS)
    g = -jnp.exp(a_log.astype(jnp.float32)) * jax.nn.softplus(
        dalpha.astype(jnp.float32).reshape(b, s, 2, DN_HEADS) + dt_bias.astype(jnp.float32))
    o_f, sf = chunk_gated_delta(cq, ck, cv, g[:, :, 0], beta[:, :, 0], s_f)
    flip = lambda a: a[:, ::-1]
    o_b, sb = chunk_gated_delta(flip(cq), flip(ck), flip(cv), flip(g[:, :, 1]), flip(beta[:, :, 1]), s_b)
    o = rms_norm(o_f + flip(o_b), dn_norm_g) * jax.nn.silu(dz.astype(jnp.float32).reshape(b, s, DN_HEADS, DN_DV))
    return o.reshape(b, s, DN_V_W).astype(dq.dtype), sf, sb

def mixer_block(h, lw, ctx):
    b, s = h.shape[0], h.shape[1]
    split_idx = np.cumsum(IN_WIDTHS)[:-1].tolist()
    aq, ak, av, dq, dk_, dv_, dz, dbeta, dalpha, ga, gb = jnp.split(h @ lw['w_in'], split_idx, axis=-1)
    q = rms_norm(aq.reshape(b, s, N_Q_HEADS, HEAD_DIM), lw['q_norm_g'])
    k = rms_norm(ak.reshape(b, s, N_KV_HEADS, HEAD_DIM), lw['k_norm_g'])
    v = av.reshape(b, s, N_KV_HEADS, HEAD_DIM)
    if ctx is None:
        o_a = block_attention(q, k, v)
        zero = jnp.zeros((b, DN_HEADS, DN_DK, DN_DV), jnp.float32)
        s_f0, s_b0 = zero, zero
    else:
        ctx_k, ctx_v, s_f0, s_b0 = ctx
        keys = jnp.concatenate([ctx_k.astype(k.dtype), axial_rope(k)], axis=1)
        vals = jnp.concatenate([ctx_v.astype(v.dtype), v], axis=1)
        o_a = block_attention(axial_rope(q), keys, vals)
    o_d, sf, sb = delta_branch(dq, dk_, dv_, dz, dbeta, dalpha, lw['conv_w'], lw['a_log'], lw['dt_bias'],
                               lw['dn_norm_g'], s_f0, s_b0)
    merged = jax.nn.sigmoid(ga) * (o_a @ lw['w_pa']) + jax.nn.sigmoid(gb) * (o_d @ lw['w_pb'])
    return merged @ lw['w_o'], (k, v, sf, sb)

def layer_forward(x, mod, lw, ctx):
    sh1, sc1, g1, sh2, sc2, g2 = jnp.split(mod.astype(x.dtype), 6, axis=-1)
    h = rms_norm(x, lw['norm1_g']) * (1.0 + sc1) + sh1
    mix, ctx_out = mixer_block(h, lw, ctx)
    x = x + g1 * mix
    h2 = rms_norm(x, lw['norm2_g']) * (1.0 + sc2) + sh2
    ffn = (jax.nn.silu(h2 @ lw['w_gate']) * (h2 @ lw['w_up'])) @ lw['w_down']
    return x + g2 * ffn, ctx_out

def setup_inputs(seed: int = 0) -> dict:
    key = jax.random.key(seed)
    ks = jax.random.split(key, 32)
    nrm = lambda k, shape, s: jax.random.normal(k, shape, jnp.float32) * s
    dt = jax.random.uniform(ks[13], (DEPTH, 2, DN_HEADS), jnp.float32, 0.001, 0.1)
    return {
        'x_prompt': nrm(ks[0], (BATCH, SEQ, D_MODEL), 1.0),
        'x_sample': nrm(ks[1], (DEC_BATCH, DEC_SEQ, D_MODEL), 1.0),
        'cache_k': nrm(ks[2], (DEC_BATCH, DEPTH, PAST_LEN, N_KV_HEADS, HEAD_DIM), 1.0),
        'cache_v': nrm(ks[3], (DEC_BATCH, DEPTH, PAST_LEN, N_KV_HEADS, HEAD_DIM), 1.0),
        'state_fwd': nrm(ks[4], (DEC_BATCH, DEPTH, DN_HEADS, DN_DK, DN_DV), 0.1),
        'state_bwd': nrm(ks[5], (DEC_BATCH, DEPTH, DN_HEADS, DN_DK, DN_DV), 0.1),
        'c': nrm(ks[6], (DEC_BATCH, D_MODEL), 1.0),
        'c_ctx': nrm(ks[7], (D_MODEL,), 1.0),
        'w_ada': nrm(ks[8], (DEPTH, D_MODEL, 6 * D_MODEL), 0.5 * D_MODEL ** -0.5),
        'b_ada': nrm(ks[9], (DEPTH, 6 * D_MODEL), 0.02),
        'norm1_g': 1.0 + nrm(ks[10], (DEPTH, D_MODEL), 0.1),
        'w_in': nrm(ks[11], (DEPTH, D_MODEL, IN_W), D_MODEL ** -0.5),
        'q_norm_g': 1.0 + nrm(ks[12], (DEPTH, HEAD_DIM), 0.1),
        'k_norm_g': 1.0 + nrm(ks[14], (DEPTH, HEAD_DIM), 0.1),
        'conv_w': nrm(ks[15], (DEPTH, DN_CONV, 2 * DN_QK_W + DN_V_W), DN_CONV ** -0.5),
        'a_log': jnp.log(jax.random.uniform(ks[16], (DEPTH, 2, DN_HEADS), jnp.float32, 1.0, 16.0)),
        'dt_bias': jnp.log(jnp.expm1(dt)),
        'dn_norm_g': 1.0 + nrm(ks[17], (DEPTH, DN_DV), 0.1),
        'w_pa': nrm(ks[18], (DEPTH, ATTN_Q_W, D_MODEL), ATTN_Q_W ** -0.5),
        'w_pb': nrm(ks[19], (DEPTH, DN_V_W, D_MODEL), DN_V_W ** -0.5),
        'w_o': nrm(ks[20], (DEPTH, D_MODEL, D_MODEL), D_MODEL ** -0.5),
        'norm2_g': 1.0 + nrm(ks[21], (DEPTH, D_MODEL), 0.1),
        'w_gate': nrm(ks[22], (DEPTH, D_MODEL, D_FF), D_MODEL ** -0.5),
        'w_up': nrm(ks[23], (DEPTH, D_MODEL, D_FF), D_MODEL ** -0.5),
        'w_down': nrm(ks[24], (DEPTH, D_FF, D_MODEL), D_FF ** -0.5),
    }

def reference(x_prompt, x_sample, cache_k, cache_v, state_fwd, state_bwd, c, c_ctx,
              w_ada, b_ada, norm1_g, w_in, q_norm_g, k_norm_g, conv_w, a_log, dt_bias, dn_norm_g,
              w_pa, w_pb, w_o, norm2_g, w_gate, w_up, w_down):
    y_prompt = x_prompt
    y_sample = x_sample
    ks_out, vs_out, sf_out, sb_out = [], [], [], []
    for l in range(DEPTH):
        lw = dict(w_in=w_in[l], q_norm_g=q_norm_g[l], k_norm_g=k_norm_g[l], conv_w=conv_w[l],
                  a_log=a_log[l], dt_bias=dt_bias[l], dn_norm_g=dn_norm_g[l], w_pa=w_pa[l], w_pb=w_pb[l],
                  w_o=w_o[l], norm1_g=norm1_g[l], norm2_g=norm2_g[l], w_gate=w_gate[l], w_up=w_up[l],
                  w_down=w_down[l])
        mod_ctx = (jax.nn.silu(c_ctx) @ w_ada[l] + b_ada[l]).reshape(1, 1, 6 * D_MODEL)
        y_prompt, (k_c, v_c, sf_c, sb_c) = layer_forward(y_prompt, mod_ctx, lw, None)
        ks_out.append(k_c)
        vs_out.append(v_c)
        sf_out.append(sf_c)
        sb_out.append(sb_c)
        mod_lat = (jax.nn.silu(c) @ w_ada[l] + b_ada[l])[:, None, :]
        ctx = (cache_k[:, l], cache_v[:, l], state_fwd[:, l], state_bwd[:, l])
        y_sample, _ = layer_forward(y_sample, mod_lat, lw, ctx)
    new_cache_k = jnp.stack(ks_out, axis=1)
    new_cache_v = jnp.stack(vs_out, axis=1)
    new_state_fwd = jnp.stack(sf_out, axis=1)
    new_state_bwd = jnp.stack(sb_out, axis=1)
    return (y_prompt, y_sample, new_cache_k, new_cache_v, new_state_fwd, new_state_bwd)


_drawn_inputs = setup_inputs


def setup_inputs(seed=0):
    import zlib

    import numpy as np

    out = dict(_drawn_inputs(seed))
    spreads = {}
    factors = {'cache_k': 8.0,
     'cache_v': 8.0,
     'state_fwd': 8.0,
     'state_bwd': 28.817,
     'q_norm_g': 8.0,
     'dn_norm_g': 5.401}
    for name, (base, spread) in spreads.items():
        noise = np.random.default_rng([zlib.crc32(name.encode()), seed]).standard_normal(out[name].shape)
        drawn = base * np.exp(spread * noise) if base else spread * noise
        out[name] = jnp.asarray(drawn.astype(out[name].dtype))
    for name, factor in factors.items():
        out[name] = (out[name] * factor).astype(out[name].dtype)
    return out
```

```python
from contextlib import ExitStack

import numpy as np

import concourse.bass as bass
from concourse import mybir

F32 = mybir.dt.float32
F32R = mybir.dt.float32r
I32 = mybir.dt.int32
ACT = mybir.ActivationFunctionType
ALU = mybir.AluOpType
AX_X = mybir.AxisListType.X

P = 128
D = 1024
KT = D // P
CTX, LAT = 256, 1024
T = CTX + LAT
NT = T // P
GN = 320
NG = T // GN
FF = 2816
FT = FF // P
PAST = 512
HD = 64
NH = 8
CONV = 5
EPS = 1e-6
CONV_TILES = 12
REST_TILES = 26
IN_TILES = CONV_TILES + REST_TILES
PADDED = T + 8


def segments(lo, hi):
    out = []
    if lo < CTX:
        out.append((lo, min(hi, CTX), 0))
    if hi > CTX:
        out.append((max(lo, CTX), hi, 1))
    return out


def ada_and_norm(nc, io, keep, h_hi, h_lo):
    with ExitStack() as ctx:
        sb = lambda n, s, d=F32: ctx.enter_context(nc.sbuf_tensor(n, s, d))
        sem = lambda n: ctx.enter_context(nc.semaphore(n))
        x = sb("x_rows", [P, NT, D])
        sq = sb("x_squares", [P, D])
        ss = sb("x_sumsq", [P, 3, NT])
        wa = sb("w_ada_slots", [P, 2, KT, P])
        c_raw = sb("c_raw", [P, KT, 2])
        c_act = sb("c_silu", [P, KT, 2])
        b_ada = sb("b_ada_sb", [P, 48])
        gains = sb("norm_gains", [P, 2, KT])
        hf = sb("h_f32", [P, 2, T])
        mod_ps = ctx.enter_context(nc.psum_tensor("mod_ps", [P, 512], F32))
        x_ps = [ctx.enter_context(nc.psum_tensor(f"x_ps{i}", [P, 512], F32)) for i in range(6)]
        small_in, c_done = sem("small_in"), sem("c_done")
        x_in = [sem(f"x_in{i}") for i in range(NT)]
        ada_in = [sem("ada_in0"), sem("ada_in1")]
        ada_done, mod_ready, scale_ready = sem("ada_done"), sem("mod_ready"), sem("scale_ready")
        sumsq_done, rms_step, x_scaled = sem("sumsq_done"), sem("rms_step"), sem("x_scaled")
        xt_ready, hf_ready, hi_ready, lo_ready = sem("xt_ready"), sem("hf_ready"), sem("hi_ready"), sem("lo_ready")
        mod, mod_s = keep["mod"], keep["mod_scale"]
        block = ctx.enter_context(nc.Block())
        TAPS = (0, 4, 8)

        @block.sync
        def _(sp):
            for dst, src in ((c_raw, "c_t"), (b_ada, "b_ada"), (gains, "gains"), (keep["ident"], "ident")):
                sp.dma_start(dst[:], io[src]).then_inc(small_in, 16)
            sp.dma_start(wa[:, 0], io["w_ada"][0]).then_inc(ada_in[0], 16)
            sp.dma_start(wa[:, 1], io["w_ada"][1]).then_inc(ada_in[1], 16)
            with sp.Fori(1, 24) as i:
                for p in range(2):
                    sp.wait_ge(ada_done, 2 * i + p - 1)
                    sp.dma_start(wa[:, p], io["w_ada"][bass.ds(2 * i + p, 1)].rearrange("o p k n -> p (o k) n")).then_inc(ada_in[p], 16)

        @block.gpsimd
        def _(pool):
            for m in range(KT):
                pool.wait_ge(hi_ready, m + 1)
                nc.gpsimd.tensor_tensor(h_lo[:, m], hf[:, m % 2], h_hi[:, m].bitcast(F32), ALU.subtract).then_inc(lo_ready, 1)

        @block.scalar
        def _(act):
            for j in range(NT):
                act.dma_start(x[:, j], io["x"][j * P:(j + 1) * P, :]).then_inc(x_in[j], 16)
            act.wait_ge(small_in, 64)
            nc.scalar.activation(c_act[:], c_raw[:], ACT.Silu).then_inc(c_done, 1)
            for j in range(NT):
                act.wait_ge(x_in[j], 16)
                if j:
                    act.wait_ge(sumsq_done, j)
                nc.scalar.activation(sq[:], x[:, j], ACT.Square, accum_out=ss[:, 0, j:j + 1]).then_inc(sumsq_done, 1)
            act.wait_ge(rms_step, 1)
            nc.scalar.activation(ss[:, 2], ss[:, 1], ACT.Sqrt).then_inc(rms_step, 1)
            for m in range(KT):
                act.wait_ge(hf_ready, 4 * (m + 1))
                nc.scalar.activation(h_hi[:, m], hf[:, m % 2], ACT.Copy).then_inc(hi_ready, 1)

        @block.tensor
        def _(pe):
            pe.wait_ge(c_done, 1)

            def ada_tile(t, p, i):
                pe.wait_ge(ada_in[p], 16 * i + 16)
                for k in range(KT):
                    last = nc.tensor.matmul(mod_ps[:, bass.ds(2 * t, 2)], wa[:, p, k], c_act[:, k], start=(k == 0), stop=(k == KT - 1))
                last.then_inc(ada_done, 1)

            with pe.Fori(0, 24) as i:
                for p in range(2):
                    ada_tile(2 * i + p, p, i)
            for m in range(KT):
                for b, j0 in enumerate(TAPS):
                    n = m * 3 + b
                    if m == 0:
                        pe.wait_ge(x_scaled, min(j0 + 4, NT))
                    if n >= 6:
                        pe.wait_ge(hf_ready, 4 * (m - 1) if b == 0 else 4 * (m - 2) + 2 + b)
                    for j in range(j0, min(j0 + 4, NT)):
                        last = nc.tensor.transpose(x_ps[n % 6][:, (j - j0) * P:(j - j0 + 1) * P], x[:, j, m * P:(m + 1) * P], keep["ident"][:])
                    last.then_inc(xt_ready, 1)

        @block.vector
        def _(dve):
            dve.wait_ge(sumsq_done, NT)
            nc.vector.tensor_scalar(ss[:, 1], ss[:, 0], 1.0 / D, EPS, ALU.mult, ALU.add).then_inc(rms_step, 1)
            dve.wait_ge(rms_step, 2)
            nc.vector.reciprocal(ss[:, 0], ss[:, 2]).then_inc(rms_step, 1)
            dve.wait_ge(rms_step, 3)
            for j in range(NT):
                nc.vector.tensor_scalar(x[:, j], x[:, j], ss[:, 0, j:j + 1], None, ALU.mult).then_inc(x_scaled, 1)
            dve.wait_ge(ada_done, 48)
            nc.vector.tensor_tensor(mod[:], mod_ps[:, 0:96].rearrange("p (t c) -> p t c", c=2), b_ada[:].unsqueeze(2).to_broadcast([P, 48, 2]), ALU.add).then_inc(mod_ready, 1)
            dve.wait_ge(mod_ready, 1)
            for n in range(2):
                nc.vector.scalar_tensor_tensor(mod_s[:, n], mod[:, 24 * n + 8:24 * n + 16], 1.0, gains[:, n].unsqueeze(2).to_broadcast([P, KT, 2]), ALU.add, ALU.mult).then_inc(scale_ready, 1)
            dve.wait_ge(scale_ready, 2)
            for m in range(KT):
                if m >= 2:
                    dve.wait_ge(lo_ready, m - 1)
                for b, j0 in enumerate(TAPS):
                    dve.wait_ge(xt_ready, m * 3 + b + 1)
                    t0, t1 = j0 * P, min(j0 + 4, NT) * P
                    for lo, hi, seg in segments(t0, t1):
                        nc.vector.tensor_scalar(hf[:, m % 2, lo:hi], x_ps[(m * 3 + b) % 6][:, lo - t0:hi - t0], mod_s[:, 0, m, seg:seg + 1], mod[:, m, seg:seg + 1], ALU.mult, ALU.add).then_inc(hf_ready, 1)


def split_product(nc, out, w_hi, w_lo, a_hi, a_lo, ks, first=True, last=True):
    for n, k in enumerate(ks):
        for q, (w, a) in enumerate(((w_hi, a_hi), (w_hi, a_lo), (w_lo, a_hi))):
            ins = nc.tensor.matmul(out, w(k), a(k), start=(first and n == 0 and q == 0), stop=(last and n == len(ks) - 1 and q == 2))
    return ins


def in_projection(nc, io, keep, h_hi, h_lo):
    with ExitStack() as ctx:
        sb = lambda n, s, d=F32: ctx.enter_context(nc.sbuf_tensor(n, s, d))
        sem = lambda n: ctx.enter_context(nc.semaphore(n))
        raw = sb("w_raw", [P, 2, KT, P])
        whi = sb("w_hi", [P, 2, KT, P], F32R)
        wlo = sb("w_lo", [P, 2, KT, P], F32R)
        bg_raw = sb("bg_raw", [P, KT, 32])
        bg_hi = sb("bg_hi", [P, KT, 32], F32R)
        bg_lo = sb("bg_lo", [P, KT, 32], F32R)
        padded = sb("conv_in", [P, 2, PADDED])
        acc = sb("conv_acc", [P, 2, PADDED - 4])
        stage = sb("proj_stage", [P, 2, PADDED - 4])
        conv_w = sb("conv_w_sb", [P, CONV_TILES, CONV])
        conv_now = sb("conv_w_now", [P, 2, CONV])
        ps = [ctx.enter_context(nc.psum_tensor(f"proj_ps{i}", [P, 512], F32)) for i in range(8)]
        w_in = [sem("w_in0"), sem("w_in1")]
        stored = [sem("stored0"), sem("stored1")]
        conv_w_in, bg_split, bg_done, bg_read, pads_zero = sem("conv_w_in"), sem("bg_split"), sem("bg_done"), sem("bg_read"), sem("pads_zero")
        hi_ready, lo_ready, group_done = sem("w_hi_ready"), sem("w_lo_ready"), sem("group_done")
        act_evac, dve_evac = sem("act_evac"), sem("dve_evac")
        conv_tap, silu_done, conv_sc = sem("conv_tap"), sem("silu_done"), sem("conv_sc")
        block = ctx.enter_context(nc.Block())
        bank = lambda p, g: ps[4 * p + g]

        def each_pair(eng, body):
            body(0, True, True, False)
            with eng.Fori(1, CONV_TILES // 2) as i:
                body(i, True, False, False)
            with eng.Fori(CONV_TILES // 2, IN_TILES // 2 - 1) as i:
                body(i, False, False, False)
            body(IN_TILES // 2 - 1, False, False, True)

        def padded_column(lo):
            return lo + (2 if lo < CTX else 6)

        @block.sync
        def _(sp):
            sp.dma_start(bg_raw[:], io["w_bg"]).then_inc(conv_w_in, 16)
            sp.dma_start(conv_w[:], io["conv_w"]).then_inc(conv_w_in, 16)
            for p in range(2):
                sp.dma_start(raw[:, p], io["w_in"][p]).then_inc(w_in[p], 16)

            def body(i, conv, first, last):
                for p in range(2):
                    t = 2 * i + p
                    if not last:
                        sp.wait_ge(lo_ready, t + 1)
                        sp.dma_start(raw[:, p], io["w_in"][bass.ds(t + 2, 1)].rearrange("o p k n -> p (o k) n")).then_inc(w_in[p], 16)
                    if conv:
                        sp.wait_ge(silu_done, t + 1)
                        dst = io["conv_t"][bass.ds(t, 1)].rearrange("o p n -> p (o n)")
                        sp.dma_start(dst[:, 0:CTX], stage[:, p, 0:CTX]).then_inc(stored[p], 16)
                        sp.dma_start(dst[:, CTX:T], stage[:, p, CTX + 4:T + 4]).then_inc(stored[p], 16)
                    else:
                        sp.wait_ge(act_evac, 2 * t + 2)
                        sp.wait_ge(dve_evac, 2 * t + 2)
                        dst = io["proj_t"][bass.ds(t - CONV_TILES, 1)].rearrange("o p n -> p (o n)")
                        sp.dma_start(dst[:, 0:CTX], stage[:, p, 0:CTX]).then_inc(stored[p], 16)
                        sp.dma_start(dst[:, CTX:T], stage[:, p, CTX:T]).then_inc(stored[p], 16)

            each_pair(sp, body)
            sp.wait_ge(stored[0], 32 * (IN_TILES // 2))
            sp.wait_ge(stored[1], 32 * (IN_TILES // 2))

        def evacuate(copy, mine, p, conv, done):
            for g in mine:
                pieces = segments(g * GN, (g + 1) * GN) if conv else [(g * GN, (g + 1) * GN, 0)]
                for lo, hi, _ in pieces:
                    at = padded_column(lo) if conv else lo
                    dst = padded if conv else stage
                    ins = copy(dst[:, p, at:at + hi - lo], bank(p, g)[:, lo - g * GN:hi - g * GN])
                ins.then_inc(done, 1)

        @block.gpsimd
        def _(pool):
            for p in range(2):
                nc.gpsimd.memset(padded[:, p, 0:2], 0.0).then_inc(pads_zero, 1)
                nc.gpsimd.memset(padded[:, p, CTX + 2:CTX + 6], 0.0).then_inc(pads_zero, 1)
                nc.gpsimd.memset(padded[:, p, T + 6:T + 8], 0.0).then_inc(pads_zero, 1)

        @block.scalar
        def _(act):
            act.wait_ge(conv_w_in, 32)
            nc.scalar.activation(bg_hi[:], bg_raw[:], ACT.Copy).then_inc(bg_split, 1)

            def split_hi(t, p, i, wait=True):
                act.wait_ge(w_in[p], 16 * i + 16)
                if wait:
                    act.wait_ge(group_done, 4 * t - 4)
                nc.scalar.activation(whi[:, p], raw[:, p], ACT.Copy).then_inc(hi_ready, 1)

            split_hi(0, 0, 0, False)

            def body(i, conv, first, last):
                for p in range(2):
                    t = 2 * i + p
                    if not (last and p):
                        split_hi(t + 1, 1 - p, i + p, not (first and p == 0))
                    for g in (0, 2):
                        act.wait_ge(group_done, 4 * t + g + 1)
                        if conv and not first:
                            act.wait_ge(conv_tap, CONV * (t - 1))
                        if not conv:
                            act.wait_ge(stored[p], 32 * i)
                        evacuate(lambda o, s: nc.scalar.activation(o, s, ACT.Copy), (g,), p, conv, act_evac)
                    if conv:
                        act.wait_ge(conv_tap, CONV * (t + 1))
                        if not first:
                            act.wait_ge(stored[p], 32 * i)
                        nc.scalar.activation(stage[:, p], acc[:, p], ACT.Silu).then_inc(silu_done, 1)

            each_pair(act, body)

        @block.vector
        def _(dve):
            dve.wait_ge(bg_split, 1)
            nc.vector.tensor_tensor(bg_lo[:], bg_raw[:], bg_hi[:].bitcast(F32), ALU.subtract).then_inc(bg_split, 1)

            def split_lo(t, p, wait=True):
                dve.wait_ge(hi_ready, t + 1)
                if wait:
                    dve.wait_ge(group_done, 4 * t - 4)
                nc.vector.tensor_tensor(wlo[:, p], raw[:, p], whi[:, p].bitcast(F32), ALU.subtract).then_inc(lo_ready, 1)

            split_lo(0, 0, False)
            dve.wait_ge(bg_done, 1)
            nc.vector.tensor_copy(keep["bg"][:], ps[7][:, 0:NT * 32].rearrange("p (j n) -> p j n", n=32)).then_inc(bg_read, 1)
            dve.wait_ge(pads_zero, 6)

            def body(i, conv, first, last):
                for p in range(2):
                    t = 2 * i + p
                    if not (last and p):
                        split_lo(t + 1, 1 - p, not (first and p == 0))
                    for g in (1, 3):
                        dve.wait_ge(group_done, 4 * t + g + 1)
                        if conv and not first:
                            dve.wait_ge(conv_tap, CONV * (t - 1))
                        if not conv:
                            dve.wait_ge(stored[p], 32 * i)
                        evacuate(nc.vector.tensor_copy, (g,), p, conv, dve_evac)
                    if conv:
                        dve.wait_ge(act_evac, 2 * t + 2)
                        dve.wait_ge(dve_evac, 2 * t + 2)
                        if not first:
                            dve.wait_ge(silu_done, t - 1)
                        for c in range(CONV):
                            src = padded[:, p, c:c + PADDED - 4]
                            w = conv_now[:, p, c:c + 1]
                            if c == 0:
                                nc.vector.tensor_copy(conv_now[:, p], conv_w[:, bass.ds(t, 1)].rearrange("p o c -> p (o c)")).then_inc(conv_sc, 1)
                                dve.wait_ge(conv_sc, t + 1)
                                nc.vector.tensor_scalar(acc[:, p], src, w, None, ALU.mult).then_inc(conv_tap, 1)
                            else:
                                dve.wait_ge(conv_tap, CONV * t + c)
                                nc.vector.scalar_tensor_tensor(acc[:, p], src, w, acc[:, p], ALU.mult, ALU.add).then_inc(conv_tap, 1)

            each_pair(dve, body)

        @block.tensor
        def _(pe):
            pe.wait_ge(bg_split, 2)
            for j in range(NT):
                a = lambda part: lambda k: part[:, k, j * P:(j + 1) * P]
                w = lambda part: lambda k: part[:, k]
                last = split_product(nc, ps[7][:, j * 32:(j + 1) * 32], a(h_hi), a(h_lo), w(bg_hi), w(bg_lo), range(KT))
            last.then_inc(bg_done, 1)

            def body(i, conv, first, last):
                for p in range(2):
                    t = 2 * i + p
                    pe.wait_ge(lo_ready, t + 1)
                    for g in range(NG):
                        if not first:
                            pe.wait_ge((act_evac, dve_evac)[g % 2], 2 * t - 3 + g // 2)
                        elif p == 1 and g == 3:
                            pe.wait_ge(bg_read, 1)
                        split_product(nc, bank(p, g)[:, 0:GN], lambda k: whi[:, p, k], lambda k: wlo[:, p, k],
                                      lambda k: h_hi[:, k, g * GN:(g + 1) * GN], lambda k: h_lo[:, k, g * GN:(g + 1) * GN],
                                      range(KT)).then_inc(group_done, 1)

            each_pair(pe, body)


LEVELS = 7
TW = 2048
SCW = 52
G_AT, NEGB_AT, BETA_AT, EG_AT, EGLG_AT, GATE_AT, EGL_AT = 0, 8, 16, 24, 32, 40, 48


def delta_rows(nc, io, keep):
    with ExitStack() as ctx:
        sb = lambda n, s, d=F32: ctx.enter_context(nc.sbuf_tensor(n, s, d))
        sem = lambda n: ctx.enter_context(nc.semaphore(n))
        cin = sb("conv_tile", [P, 2, CONV_TILES, P])
        sq = sb("qk_squares", [P, 2, 1024])
        ss = sb("qk_sumsq", [P, 2, 3, 16])
        qn = sb("q_rows", [P, 2, 512])
        tile = sb("delta_tile", [P, 2, TW])
        row_ps = [[ctx.enter_context(nc.psum_tensor(f"row_ps{p}{n}", [P, 512], F32)) for n in range(3)] for p in range(2)]
        col_ps = [ctx.enter_context(nc.psum_tensor(f"col_ps{n}", [P, 512], F32)) for n in range(2)]
        tile_in = [sem("tile_in0"), sem("tile_in1")]
        stored = [sem("tile_stored0"), sem("tile_stored1")]
        rows_done, squared, summed, rooted, inverse, rows_scaled, v_rows, cols_done, cols_out = (
            sem(n) for n in ("rows_done", "squared", "summed", "rooted", "inverse", "rows_scaled", "v_rows", "cols_done", "cols_out"))
        block = ctx.enter_context(nc.Block())

        def each_pair(eng, body):
            body(0, True)
            with eng.Fori(1, NT // 2) as i:
                body(i, False)

        @block.sync
        def _(sp):
            def body(i, first):
                for p in range(2):
                    j = 2 * i + p
                    if not first:
                        sp.wait_ge(rows_done, j - 1)
                    sp.dma_start(cin[:, p], io["conv_t"][:, :, bass.ds(j * P, P)].rearrange("m p n -> p m n")).then_inc(tile_in[p], 16)
            each_pair(sp, body)

        @block.tensor
        def _(pe):
            def rows(i, p, first):
                pe.wait_ge(tile_in[p], 16 * i + 16)
                if not first:
                    pe.wait_ge(rows_scaled, 2 * (2 * i + p) - 2)
                    pe.wait_ge(v_rows, 2 * i + p - 1)
                for m in range(CONV_TILES):
                    last = nc.tensor.transpose(row_ps[p][m // 4][:, (m % 4) * P:(m % 4 + 1) * P], cin[:, p, m], keep["ident"][:])
                last.then_inc(rows_done, 1)

            def cols(i, p, first):
                j = 2 * i + p
                for n in range(2):
                    pe.wait_ge(rows_scaled, 2 * j + n + 1)
                    if not (first and p == 0):
                        pe.wait_ge(cols_out, 2 * j + n - 1)
                    for m in range(4):
                        src = qn[:, p, m * P:(m + 1) * P] if n == 0 else tile[:, p, m * P:(m + 1) * P]
                        last = nc.tensor.transpose(col_ps[n][:, m * P:(m + 1) * P], src, keep["ident"][:])
                    last.then_inc(cols_done, 1)

            def body(i, first):
                rows(i, 0, first)
                rows(i, 1, first)
                cols(i, 0, first)
                cols(i, 1, first)
            each_pair(pe, body)

        @block.scalar
        def _(act):
            def body(i, first):
                for p in range(2):
                    j = 2 * i + p
                    act.wait_ge(rows_done, j + 1)
                    if not first:
                        act.wait_ge(summed, 3 * j - 3)
                        act.wait_ge(stored[p], 16 * i)
                    for n in range(2):
                        nc.scalar.activation(sq[:, p, n * 512:(n + 1) * 512], row_ps[p][n][:], ACT.Square).then_inc(squared, 1)
                    nc.scalar.activation(tile[:, p, 512:1024], row_ps[p][2][:], ACT.Copy).then_inc(v_rows, 1)
                    act.wait_ge(summed, 3 * j + 3)
                    nc.scalar.activation(ss[:, p, 1], ss[:, p, 0], ACT.Sqrt).then_inc(rooted, 1)
                for p in range(2):
                    for n in range(2):
                        act.wait_ge(cols_done, 2 * (2 * i + p) + n + 1)
                        nc.scalar.activation(tile[:, p, 1024 + 512 * n:1536 + 512 * n], col_ps[n][:], ACT.Copy).then_inc(cols_out, 1)
                    act.wait_ge(cols_out, 2 * (2 * i + p) + 2)
                    act.wait_ge(rows_scaled, 2 * (2 * i + p) + 2)
                    act.dma_start(io["delta_t"][bass.ds(2 * i + p, 1)].rearrange("o p n -> p (o n)"), tile[:, p]).then_inc(stored[p], 16)
            each_pair(act, body)
            for p in range(2):
                act.wait_ge(stored[p], 16 * (NT // 2))

        @block.vector
        def _(dve):
            def body(i, first):
                for p in range(2):
                    j = 2 * i + p
                    dve.wait_ge(squared, 2 * j + 2)
                    nc.vector.tensor_reduce(ss[:, p, 2], sq[:, p].rearrange("p (h d) -> p h d", d=HD), AX_X, ALU.add).then_inc(summed, 1)
                    dve.wait_ge(summed, 3 * j + 1)
                    nc.vector.tensor_scalar(ss[:, p, 0, 0:8], ss[:, p, 2, 0:8], EPS, float(HD), ALU.add, ALU.mult).then_inc(summed, 1)
                    nc.vector.tensor_scalar(ss[:, p, 0, 8:16], ss[:, p, 2, 8:16], EPS, None, ALU.add).then_inc(summed, 1)
                for p in range(2):
                    j = 2 * i + p
                    dve.wait_ge(rooted, j + 1)
                    nc.vector.reciprocal(ss[:, p, 2], ss[:, p, 1]).then_inc(inverse, 1)
                    dve.wait_ge(inverse, j + 1)
                    if not first:
                        dve.wait_ge(cols_done, 2 * j - 2)
                    for n, dst in enumerate((qn[:, p], tile[:, p, 0:512])):
                        nc.vector.tensor_tensor(dst.rearrange("p (h d) -> p h d", d=HD), row_ps[p][n][:].rearrange("p (h d) -> p h d", d=HD),
                                                ss[:, p, 2, 8 * n:8 * n + 8].unsqueeze(2).to_broadcast([P, 8, HD]), ALU.mult).then_inc(rows_scaled, 1)
            each_pair(dve, body)


def delta_scalars(nc, io, keep, tab):
    with ExitStack() as ctx:
        sb = lambda n, s, d=F32: ctx.enter_context(nc.sbuf_tensor(n, s, d))
        sem = lambda n: ctx.enter_context(nc.semaphore(n))
        z, az, sp_, g, b = (sb(n, [P, NT, 16]) for n in ("alpha_z", "alpha_abs", "softplus", "log_decay", "beta_cols"))
        par = sb("decay_params", [P, 2, 16])
        gl = sb("tile_decay", [P, 2, NT, 8])
        cum_ps = [ctx.enter_context(nc.psum_tensor(f"cum_ps{n}", [P, 512], F32)) for n in range(2)]
        par_in, a_step, v_step, cum_done = sem("par_in"), sem("scalar_step"), sem("vector_step"), sem("cum_done")
        block = ctx.enter_context(nc.Block())
        bg = keep["bg"]
        per_tile = lambda a, w: a.unsqueeze(1).to_broadcast([P, NT, w])
        col = lambda d, at, n=8: tab[:, d, :, at:at + n]

        @block.sync
        def _(sp):
            sp.dma_start(par[:], io["decay_params"]).then_inc(par_in, 16)
            for name in ("tri", "ones", "offdiag", "maskneg", "levels"):
                sp.dma_start(keep[name][:], io[name]).then_inc(par_in, 16)
            sp.wait_ge(par_in, 96)

        @block.scalar
        def _(act):
            act.wait_ge(par_in, 96)
            nc.scalar.activation(b[:], bg[:, :, 0:16], ACT.Exp, scale=-1.0).then_inc(a_step, 1)
            act.wait_ge(v_step, 1)
            nc.scalar.activation(az[:], z[:], ACT.Abs).then_inc(a_step, 1)
            act.wait_ge(a_step, 2)
            nc.scalar.activation(sp_[:], az[:], ACT.Exp, scale=-1.0).then_inc(a_step, 1)
            nc.scalar.activation(par[:, 0], par[:, 0], ACT.Exp).then_inc(a_step, 1)
            act.wait_ge(v_step, 3)
            nc.scalar.activation(az[:], sp_[:], ACT.Ln).then_inc(a_step, 1)
            act.wait_ge(v_step, 15)
            for d in range(2):
                nc.scalar.activation(col(d, EG_AT), col(d, G_AT), ACT.Exp).then_inc(a_step, 1)
                nc.scalar.activation(col(d, EGLG_AT), col(d, EGLG_AT), ACT.Exp).then_inc(a_step, 1)
                nc.scalar.activation(col(d, EGL_AT, 4), col(d, EGL_AT, 4), ACT.Exp).then_inc(a_step, 1)

        @block.vector
        def _(dve):
            n = [0]

            def step(ins, wait=True):
                n[0] += 1
                ins.then_inc(v_step, 1)
                if wait:
                    dve.wait_ge(v_step, n[0])

            dve.wait_ge(par_in, 96)
            step(nc.vector.tensor_tensor(z[:], bg[:, :, 16:32], per_tile(par[:, 1], 16), ALU.add))
            dve.wait_ge(a_step, 3)
            step(nc.vector.tensor_scalar(z[:], z[:], 0.0, None, ALU.max))
            step(nc.vector.tensor_scalar(sp_[:], sp_[:], 1.0, None, ALU.add))
            dve.wait_ge(a_step, 5)
            step(nc.vector.tensor_tensor(z[:], z[:], az[:], ALU.add))
            step(nc.vector.scalar_tensor_tensor(g[:], z[:], -1.0, per_tile(par[:, 0], 16), ALU.mult, ALU.mult))
            step(nc.vector.tensor_scalar(b[:], b[:], 1.0, None, ALU.add))
            step(nc.vector.reciprocal(b[:], b[:]))
            for d in range(2):
                dve.wait_ge(cum_done, d + 1)
                ps = cum_ps[d][:, 0:160].rearrange("p (a j h) -> p a j h", a=2, h=8)
                step(nc.vector.tensor_copy(col(d, G_AT), ps[:, 0]))
                step(nc.vector.tensor_copy(gl[:, d], ps[:, 1]))
                step(nc.vector.tensor_tensor(col(d, EGLG_AT), gl[:, d], col(d, G_AT), ALU.subtract), False)
                pairs = gl[:, d].rearrange("p j (m e) -> p j m e", e=2)
                for e in range(2):
                    half = slice(64 * e, 64 * e + 64)
                    ins = nc.vector.tensor_copy(tab[half, d, :, EGL_AT:EGL_AT + 4], pairs[half, :, :, e])
                nc.vector.tensor_copy(col(d, BETA_AT), b[:, :, 8 * d:8 * d + 8])
                nc.vector.tensor_scalar(col(d, NEGB_AT), b[:, :, 8 * d:8 * d + 8], -1.0, None, ALU.mult)
                step(nc.vector.tensor_copy(col(d, GATE_AT), g[:, :, 8 * d:8 * d + 8]), False)
            assert n[0] == 15

        @block.tensor
        def _(pe):
            pe.wait_ge(v_step, 5)
            for d in range(2):
                ps = cum_ps[d][:, 0:160].rearrange("p (a j h) -> p a j h", a=2, h=8)
                nc.tensor.matmul(ps[:, 0], keep["tri"][:, d], g[:, :, 8 * d:8 * d + 8], start=True, stop=True)
                nc.tensor.matmul(ps[:, 1], keep["ones"][:], g[:, :, 8 * d:8 * d + 8], start=True, stop=True).then_inc(cum_done, 1)


def delta_scan(nc, io, keep, tab, o_rows):
    with ExitStack() as ctx:
        sb = lambda n, s, d=F32: ctx.enter_context(nc.sbuf_tensor(n, s, d))
        sem = lambda n: ctx.enter_context(nc.semaphore(n))
        H4 = 4
        tin = sb("delta_in", [P, 2, 2, TW])
        sc = sb("step_scalars", [P, 2, 2, SCW])
        DT = sb("decay_t", [P, 4, H4, P])
        tri_g = DO = NTf = sb("n_t", [P, 4, H4, P])
        NTr = sb("n_t_r", [P, 4, H4, P], F32R)
        Nh = sb("n_hi", [P, 4, H4, P], F32R)
        Nl = sb("n_lo", [P, 4, H4, P], F32R)
        NM = sb("n_t_level", [P, 2, 4, H4, P], F32R)
        XX = sb("x_inv", [P, 4, 2, H4, P], F32R)
        X, XT = XX[:, :, 0], XX[:, :, 1]
        Y = sb("y_res", [P, 4, H4, P], F32R)
        AT = sb("attn_t", [P, 4, H4, P])
        WT = sb("w_t", [P, 4, H4, P])
        eyes = sb("eyes", [P, 2, P], F32R)
        spare = sb("spare", [P, 4])
        S = sb("state", [P, 2, 4, HD])
        Sd = sb("state_decayed", [P, 2, 4, HD])
        r, vn, kd, t1 = (sb(n, [P, 2, NH, HD]) for n in ("v_minus", "v_new", "k_decayed", "scan_tmp"))
        bk = {n: [ctx.enter_context(nc.psum_tensor(f"bank_{n}{e}", [P, 512], F32)) for e in range(2)] for n in "AS"}
        BC = [ctx.enter_context(nc.psum_tensor(f"banks_bc{e}", [P, 2, 512], F32)) for e in range(2)]
        bk["B"], bk["C"] = [b[:, 0] for b in BC], [b[:, 1] for b in BC]
        names = ("scalars tri_ready row_ps arg_ready decay_ready off_ready kk_ps qk_ps n_ready at_ready nr_ready n_ps nh_ready "
                 "nl_ready nm_ready y_ps y_ready z_ps x_ready r_ps r_ready xr_ps w_ready "
                 "ks_ps v_minus_ready kd_ready sd_ready wr_ps vn_ready qs_ps qs_ready av_ps o_ready st_ps s_ready eyes_ready "
                 "zeroed kept_out state_in").split()
        e = {n: sem("d_" + n) for n in names}
        tile_in = [[sem(f"d_in{p}{d}") for d in range(2)] for p in range(2)]
        block = ctx.enter_context(nc.Block())
        bank = lambda n, q: bk[n][q % 2][:].rearrange("p (h i) -> p h i", h=4)
        hb = lambda n, d: bk[n][d][:].rearrange("p (h i) -> p h i", h=NH)
        both = lambda n, par: bk[n][par][:].rearrange("p (d m i) -> p d m i", d=2, m=4)
        idn = lambda a: a.unsqueeze(1).to_broadcast([P, H4, P])
        mask_t = lambda lv, d: keep["levels"][:, lv, 1 - d]
        half = lambda h: slice(64 * (h % 2), 64 * (h % 2) + 64)
        heads = lambda q: range(q % 2, NH, 2)

        def steps(eng, body, between=None):
            for p in range(2):
                body(p, p, p, 1 - p, True)
            if between:
                between()
            with eng.Fori(1, NT // 2) as i:
                for p in range(2):
                    body(2 * i + p, p, 2 * i + p, NT + 1 - (2 * i + p), False)

        @block.sync
        def _(sp):
            def load(p, d, tile):
                sp.dma_start(tin[:, p, d], io["delta_t"][bass.ds(tile, 1)].rearrange("o p n -> p (o n)")).then_inc(tile_in[p][d], 16)

            for p in range(2):
                load(p, 0, p)
                load(p, 1, 1 - p)
            sp.wait_ge(e["s_ready"], 2)
            for d in range(2):
                load(0, d, (2, NT - 1)[d])
            sp.wait_ge(e["s_ready"], 4)
            for d in range(2):
                sp.dma_start(io["state_out"][d], S[:, d]).then_inc(e["kept_out"], 16)
            sp.wait_ge(e["kept_out"], 32)
            for d in range(2):
                sp.dma_start(S[:, d], io["state_in"][d]).then_inc(e["state_in"], 16)
            for d in range(2):
                load(1, d, (3, NT - 2)[d])
            with sp.Fori(1, NT // 2 - 1) as i:
                for p in range(2):
                    sp.wait_ge(e["s_ready"], 2 * (2 * i + p) + 2)
                    load(p, 0, 2 * i + p + 2)
                    load(p, 1, NT - 1 - (2 * i + p))

        @block.gpsimd
        def _(pool):
            for d in range(2):
                nc.gpsimd.memset(S[:, d], 0.0).then_inc(e["zeroed"], 1)
            nc.gpsimd.tensor_copy(eyes[:, 0], keep["ident"][:]).then_inc(e["eyes_ready"], 1)
            nc.gpsimd.tensor_scalar(eyes[:, 1], keep["ident"][:], -1.0, None, ALU.mult).then_inc(e["eyes_ready"], 1)
            pool.wait_ge(e["zeroed"], 2)

            def body(n, p, tf, tb, ctxt):
                pool.wait_ge(e["scalars"], n + 1)
                for q in range(4):
                    d, par = q // 2, q % 2
                    nc.gpsimd.tensor_tensor(tri_g[:, q], idn(keep["tri"][:, d]),
                                            sc[:, p, d, GATE_AT + par:GATE_AT + 8:2].unsqueeze(2).to_broadcast([P, H4, P]), ALU.mult).then_inc(e["tri_ready"], 1)
                for q in range(4):
                    pool.wait_ge(e["decay_ready"], 4 * n + q + 1)
                    nc.gpsimd.tensor_tensor(DO[:, q], DT[:, q], idn(keep["offdiag"][:]), ALU.mult).then_inc(e["off_ready"], 1)
                for lv in range(LEVELS):
                    for q in range(4):
                        if lv == 0:
                            pool.wait_ge(e["nr_ready"], 4 * n + q + 1)
                        elif lv == 2:
                            pool.wait_ge(e["z_ps"], LEVELS * n * 4 + q + 1)
                        elif lv > 2:
                            pool.wait_ge(e["y_ps"], ((LEVELS - 1) * n + lv - 3) * 4 + q + 1)
                        nc.gpsimd.tensor_tensor(NM[:, lv % 2, q], NTr[:, q].bitcast(F32), idn(mask_t(lv, q // 2)), ALU.mult).then_inc(e["nm_ready"], 1)
                for d in range(2):
                    pool.wait_ge(tile_in[p][d], 16 * ((n - p) // 2) + 16 if ctxt else 8 * (n - p) + 16)
                    nc.gpsimd.tensor_tensor(kd[:, d], tin[:, p, d, 0:512].rearrange("p (h i) -> p h i", h=NH),
                                            sc[:, p, d, EGLG_AT:EGLG_AT + 8].unsqueeze(2).to_broadcast([P, NH, HD]), ALU.mult).then_inc(e["kd_ready"], 1)
                    if not (ctxt and p == 0):
                        pool.wait_ge(e["s_ready"], 2 * n + d - 1)
                    nc.gpsimd.tensor_tensor(Sd[:, d], S[:, d], sc[:, p, d, EGL_AT:EGL_AT + 4].unsqueeze(2).to_broadcast([P, 4, HD]), ALU.mult).then_inc(e["sd_ready"], 1)
            steps(pool, body, lambda: pool.wait_ge(e["state_in"], 32))

        @block.scalar
        def _(act):
            cp = lambda o, s: nc.scalar.activation(o, s, ACT.Copy)

            def body(n, p, tf, tb, ctxt):
                if not ctxt:
                    act.wait_ge(e["s_ready"], 2 * n - 2)
                cp(sc[:, p, 0], tab[:, 0, bass.ds(tf, 1)].rearrange("p o n -> p (o n)"))
                cp(sc[:, p, 1], tab[:, 1, bass.ds(tb, 1)].rearrange("p o n -> p (o n)")).then_inc(e["scalars"], 1)
                for q in range(4):
                    act.wait_ge(e["arg_ready"], 4 * n + q + 1)
                    nc.scalar.activation(DT[:, q], DT[:, q], ACT.Exp).then_inc(e["decay_ready"], 1)
                for q in range(4):
                    act.wait_ge(e["n_ready"], 4 * n + q + 1)
                    if not (ctxt and p == 0):
                        act.wait_ge(e["nm_ready"], LEVELS * n * 4)
                    cp(NTr[:, q], NTf[:, q]).then_inc(e["nr_ready"], 1)
                    act.wait_ge(e["n_ps"], 4 * n + q + 1)
                    cp(Nh[:, q], bank("A", q)).then_inc(e["nh_ready"], 1)
                for lv in range(1, LEVELS):
                    for q in range(4):
                        act.wait_ge(e["y_ps"], ((LEVELS - 1) * n + lv - 1) * 4 + q + 1)
                        cp(Y[:, q], bank("A", q)).then_inc(e["y_ready"], 1)
                for q in range(4):
                    act.wait_ge(e["r_ps"], 4 * n + q + 1)
                    cp(Y[:, q], bank("A", q)).then_inc(e["r_ready"], 1)
            steps(act, body)

        @block.vector
        def _(dve):
            dve.wait_ge(e["zeroed"], 2)

            def body(n, p, tf, tb, ctxt):
                first = ctxt and p == 0
                rows = lambda d, at: tin[:, p, d, at:at + 512].rearrange("p (h i) -> p h i", h=NH)
                eg = lambda par: sc[:, p, :, EG_AT + par:EG_AT + 8:2].unsqueeze(3).to_broadcast([P, 2, 4, HD])
                wide = lambda d, at: sc[:, p, d, at:at + 8].unsqueeze(2).to_broadcast([P, NH, HD])
                for q in range(4):
                    d = q // 2
                    dve.wait_ge(e["row_ps"], 4 * n + q + 1)
                    for m, h in enumerate(heads(q)):
                        last = nc.vector.scalar_tensor_tensor(DT[:, q, m], bank("A", q)[:, m], sc[:, p, d, G_AT + h:G_AT + h + 1], keep["maskneg"][:, d], ALU.subtract, ALU.add)
                    last.then_inc(e["arg_ready"], 1)
                for q in range(4):
                    d = q // 2
                    dve.wait_ge(e["qk_ps"], 4 * n + q + 1)
                    dve.wait_ge(e["off_ready"], 4 * n + q + 1)
                    for m, h in enumerate(heads(q)):
                        last = nc.vector.scalar_tensor_tensor(NTf[:, q, m], bank("B", q)[:, m], sc[:, p, d, NEGB_AT + h:NEGB_AT + h + 1], DO[:, q, m], ALU.mult, ALU.mult)
                    last.then_inc(e["n_ready"], 1)
                    nc.vector.tensor_tensor(AT[:, q], bank("C", q), DT[:, q], ALU.mult).then_inc(e["at_ready"], 1)
                for q in range(4):
                    d = q // 2
                    dve.wait_ge(e["nh_ready"], 4 * n + q + 1)
                    nc.vector.tensor_tensor(Nl[:, q], bank("A", q), Nh[:, q].bitcast(F32), ALU.subtract).then_inc(e["nl_ready"], 1)
                for lv in range(LEVELS):
                    for q in range(4):
                        dve.wait_ge(e["z_ps"], (LEVELS * n + lv) * 4 + q + 1)
                        nc.vector.tensor_copy(XX[:, q].rearrange("p t h i -> p t (h i)"), BC[q % 2][:]).then_inc(e["x_ready"], 1)
                for q in range(4):
                    dve.wait_ge(e["xr_ps"], 4 * n + q + 1)
                    nc.vector.tensor_tensor(WT[:, q], bank("B", q), XT[:, q].bitcast(F32), ALU.add).then_inc(e["w_ready"], 1)
                for par in range(2):
                    dve.wait_ge(e["ks_ps"], 2 * n + par + 1)
                    nc.vector.tensor_tensor(t1[:, :, par::2], both("A", par), eg(par), ALU.mult).then_inc(e["v_minus_ready"], 1)
                dve.wait_ge(e["v_minus_ready"], 4 * n + 2)
                for d in range(2):
                    nc.vector.tensor_tensor(r[:, d], rows(d, 512), t1[:, d], ALU.subtract).then_inc(e["v_minus_ready"], 1)
                for d in range(2):
                    dve.wait_ge(e["wr_ps"], 2 * n + d + 1)
                    nc.vector.tensor_tensor(vn[:, d], hb("B", d), wide(d, BETA_AT), ALU.mult).then_inc(e["vn_ready"], 1)
                for par in range(2):
                    dve.wait_ge(e["qs_ps"], 2 * n + par + 1)
                    dve.wait_ge(e["v_minus_ready"], 4 * n + 4)
                    nc.vector.tensor_tensor(t1[:, :, par::2], both("C", par), eg(par), ALU.mult).then_inc(e["qs_ready"], 1)
                for d in range(2):
                    tile = (tf, tb)[d]
                    dve.wait_ge(e["st_ps"], 2 * n + d + 1)
                    dve.wait_ge(e["sd_ready"], 2 * n + d + 1)
                    nc.vector.tensor_tensor(S[:, d], bk["A"][d][:, 0:256].rearrange("p (m i) -> p m i", m=4), Sd[:, d], ALU.add).then_inc(e["s_ready"], 1)
                    dve.wait_ge(e["av_ps"], 2 * n + d + 1)
                    dve.wait_ge(e["qs_ready"], 2 * n + 2)
                    nc.vector.memset(spare[0:1, 2 * p + d:2 * p + d + 1], 0.0)
                    nc.vector.tensor_tensor(o_rows[:, d, bass.ds(tile, 1)].rearrange("p o (h i) -> p (o h) i", h=NH), hb("S", d), t1[:, d], ALU.add).then_inc(e["o_ready"], 1)
            steps(dve, body)

        @block.tensor
        def _(pe):
            pe.wait_ge(e["eyes_ready"], 2)
            pe.wait_ge(e["zeroed"], 2)
            mm = lambda o, a, b, st=True, sp_=True: nc.tensor.matmul(o, a, b, start=st, stop=sp_)

            def body(n, p, tf, tb, ctxt):
                first = ctxt and p == 0
                kT = lambda d, h: tin[half(h), p, d, 1536 + (h // 2) * P:1536 + (h // 2 + 1) * P]
                qT = lambda d, h: tin[half(h), p, d, 1024 + (h // 2) * P:1024 + (h // 2 + 1) * P]
                L, LY = LEVELS * n * 4, (LEVELS - 1) * n * 4
                for q in range(4):
                    d = q // 2
                    pe.wait_ge(e["tri_ready"], 4 * n + q + 1)
                    if q >= 2:
                        pe.wait_ge(e["arg_ready"], 4 * n + q - 1)
                    elif not first:
                        pe.wait_ge(e["s_ready"], 2 * n)
                    mm(bk["A"][q % 2][:], keep["ones"][:], tri_g[:, q].rearrange("p h i -> p (h i)")).then_inc(e["row_ps"], 1)
                for q in range(4):
                    d = q // 2
                    if q % 2 == 0:
                        pe.wait_ge(tile_in[p][d], 16 * ((n - p) // 2) + 16 if ctxt else 8 * (n - p) + 16)
                    if q >= 2:
                        pe.wait_ge(e["at_ready"], 4 * n + q - 1)
                    elif not first:
                        pe.wait_ge(e["qs_ready"], 2 * n)
                    for m, h in enumerate(heads(q)):
                        mm(bank("B", q)[:, m], kT(d, h), kT(d, h))
                        last = mm(bank("C", q)[:, m], kT(d, h), qT(d, h))
                    last.then_inc(e["qk_ps"], 1)
                for q in range(4):
                    pe.wait_ge(e["n_ready"], 4 * n + q + 1)
                    if q >= 2:
                        pe.wait_ge(e["nl_ready"], 4 * n + q - 1)
                    else:
                        pe.wait_ge(e["arg_ready"], 4 * n + q + 3)
                    for m in range(4):
                        last = nc.tensor.transpose(bank("A", q)[:, m], NTf[:, q, m], keep["ident"][:])
                    last.then_inc(e["n_ps"], 1)
                for lv in range(LEVELS):
                    for q in range(4):
                        if lv == 0:
                            pe.wait_ge(e["nm_ready"], L + q + 1)
                            continue
                        pe.wait_ge(e["x_ready"], L + (lv - 1) * 4 + q + 1)
                        pe.wait_ge(e["nm_ready"], L + lv * 4 + q + 1)
                        if lv == 1 and q < 2:
                            pe.wait_ge(e["nl_ready"], 4 * n + q + 3)
                        else:
                            pe.wait_ge(e["y_ready"], LY + (lv - 1) * 4 + q - 1)
                        for m in range(4):
                            last = mm(bank("A", q)[:, m], NM[:, lv % 2, q, m], X[:, q, m])
                        last.then_inc(e["y_ps"], 1)
                    for q in range(4):
                        if lv:
                            pe.wait_ge(e["y_ready"], LY + (lv - 1) * 4 + q + 1)
                        if lv or q >= 2:
                            pe.wait_ge(e["x_ready"], L + lv * 4 + q - 1)
                        else:
                            pe.wait_ge(e["at_ready"], 4 * n + q + 3)
                        flat = lambda a: a.rearrange("p h i -> p (h i)")
                        if lv:
                            mm(bk["B"][q % 2], eyes[:, 0], flat(X[:, q]), True, False)
                            mm(bk["C"][q % 2], eyes[:, 0], flat(XT[:, q]), True, False)
                        else:
                            mm(bk["C"][q % 2], eyes[:, 0], flat(NM[:, 0, q]), True, False)
                        for m in range(4):
                            if lv:
                                mm(bank("B", q)[:, m], XT[:, q, m], Y[:, q, m], False, m == 3)
                                last = mm(bank("C", q)[:, m], Y[:, q, m], XT[:, q, m], False, m == 3)
                            else:
                                mm(bank("B", q)[:, m], NM[:, 0, q, m], eyes[:, 0], True, False)
                                mm(bank("B", q)[:, m], eyes[:, 0], eyes[:, 0], False, True)
                                last = mm(bank("C", q)[:, m], eyes[:, 0], eyes[:, 0], False, m == 3)
                        last.then_inc(e["z_ps"], 1)
                for q in range(4):
                    pe.wait_ge(e["x_ready"], L + (LEVELS - 1) * 4 + q + 1)
                    pe.wait_ge(e["y_ready"], LY + (LEVELS - 1) * 4)
                    pe.wait_ge(e["nl_ready"], 4 * n + q + 1)
                    if q >= 2:
                        pe.wait_ge(e["r_ready"], 4 * n + q - 1)
                    for m in range(4):
                        o = bank("A", q)[:, m]
                        mm(o, eyes[:, 0], eyes[:, 0], True, False)
                        mm(o, eyes[:, 1], XT[:, q, m], False, False)
                        mm(o, Nh[:, q, m], XT[:, q, m], False, False)
                        last = mm(o, Nl[:, q, m], XT[:, q, m], False, True)
                    last.then_inc(e["r_ps"], 1)
                for q in range(4):
                    pe.wait_ge(e["r_ready"], 4 * n + q + 1)
                    if q >= 2:
                        pe.wait_ge(e["w_ready"], 4 * n + q - 1)
                    else:
                        pe.wait_ge(e["x_ready"], L + LEVELS * 4 - 2 + q + 1)
                    for m in range(4):
                        last = mm(bank("B", q)[:, m], X[:, q, m], Y[:, q, m])
                    last.then_inc(e["xr_ps"], 1)
                for name, operand, done in (("A", kT, "ks_ps"), ("C", qT, "qs_ps")):
                    pe.wait_ge(e["r_ready"], 4 * n + 4)
                    for par in range(2):
                        for d in range(2):
                            for m in range(4):
                                last = mm(both(name, par)[:, d, m], operand(d, 2 * m + par), S[half(par), d, m])
                        last.then_inc(e[done], 1)
                for d in range(2):
                    pe.wait_ge(e["v_minus_ready"], 4 * n + 3 + d)
                    pe.wait_ge(e["w_ready"], 4 * n + 4)
                    for h in range(NH):
                        last = mm(hb("B", d)[:, h], WT[:, 2 * d + h % 2, h // 2], r[:, d, h])
                    last.then_inc(e["wr_ps"], 1)
                for d in range(2):
                    pe.wait_ge(e["vn_ready"], 2 * n + d + 1)
                    pe.wait_ge(e["kd_ready"], 2 * n + d + 1)
                    for h in range(NH):
                        last = mm(bk["A"][d][half(h), (h // 2) * HD:(h // 2 + 1) * HD], kd[:, d, h], vn[:, d, h])
                    last.then_inc(e["st_ps"], 1)
                    if not first:
                        pe.wait_ge(e["o_ready"], 2 * n - 1 + d)
                    for h in range(NH):
                        last = mm(hb("S", d)[:, h], AT[:, 2 * d + h % 2, h // 2], vn[:, d, h])
                    last.then_inc(e["av_ps"], 1)
            steps(pe, body, lambda: pe.wait_ge(e["state_in"], 32))


def delta_gate(nc, io, keep, o_rows):
    with ExitStack() as ctx:
        sb = lambda n, s, d=F32: ctx.enter_context(nc.sbuf_tensor(n, s, d))
        sem = lambda n: ctx.enter_context(nc.semaphore(n))
        zt = sb("z_t", [P, 4, T])
        sq = sb("o_squares", [P, 2, 512])
        ss = sb("o_sumsq", [P, 3, NT, NH])
        out = sb("o_gated", [P, 2, 4, P])
        gn = sb("dn_gain", [P, 1])
        ps = [ctx.enter_context(nc.psum_tensor(f"o_ps{n}", [P, 512], F32)) for n in range(4)]
        z_in, z_act, added, squared, summed, small, scaled, turned, gated, stored = (
            sem(n) for n in ("z_in", "z_act", "o_added", "o_squared", "o_summed", "o_small", "o_scaled", "o_turned", "o_gated_s", "o_stored"))
        block = ctx.enter_context(nc.Block())
        of = o_rows[:, 0]

        @block.sync
        def _(sp):
            sp.dma_start(zt[:], io["proj_t"][6:10].rearrange("m p n -> p m n")).then_inc(z_in, 16)
            sp.dma_start(gn[:], io["dn_g"]).then_inc(z_in, 16)
            for j in range(NT):
                sp.wait_ge(gated, j + 1)
                sp.dma_start(io["od_t"][:, :, j * P:(j + 1) * P].rearrange("m p n -> p m n"), out[:, j % 2]).then_inc(stored, 16)
                sp.wait_ge(stored, 16 * (j + 1))

        @block.scalar
        def _(act):
            for j in range(NT):
                act.wait_ge(added, j + 1)
                if j >= 2:
                    act.wait_ge(summed, j - 1)
                nc.scalar.activation(sq[:, j % 2], of[:, j], ACT.Square).then_inc(squared, 1)
            act.wait_ge(small, 1)
            nc.scalar.activation(ss[:, 2], ss[:, 1], ACT.Sqrt).then_inc(small, 1)
            act.wait_ge(z_in, 32)
            for m in range(4):
                nc.scalar.activation(zt[:, m], zt[:, m], ACT.Silu).then_inc(z_act, 1)

        @block.vector
        def _(dve):
            for j in range(NT):
                nc.vector.tensor_tensor(of[:, j], of[:, j], o_rows[:, 1, j], ALU.add).then_inc(added, 1)
            for j in range(NT):
                dve.wait_ge(squared, j + 1)
                nc.vector.tensor_reduce(ss[:, 0, j], sq[:, j % 2].rearrange("p (h d) -> p h d", d=HD), AX_X, ALU.add).then_inc(summed, 1)
            dve.wait_ge(summed, NT)
            nc.vector.tensor_scalar(ss[:, 1], ss[:, 0], 1.0 / HD, EPS, ALU.mult, ALU.add).then_inc(small, 1)
            dve.wait_ge(small, 2)
            nc.vector.reciprocal(ss[:, 0], ss[:, 2]).then_inc(small, 1)
            dve.wait_ge(small, 3)

            def gate(j):
                dve.wait_ge(turned, j + 1)
                if j >= 2:
                    dve.wait_ge(stored, 16 * (j - 1))
                nc.vector.scalar_tensor_tensor(out[:, j % 2], ps[j % 4][:].rearrange("p (m n) -> p m n", m=4), gn[:, 0:1], zt[:, :, j * P:(j + 1) * P], ALU.mult, ALU.mult).then_inc(gated, 1)

            for j in range(NT):
                o = of[:, j].rearrange("p (h d) -> p h d", d=HD)
                nc.vector.tensor_tensor(o, o, ss[:, 0, j].unsqueeze(2).to_broadcast([P, NH, HD]), ALU.mult).then_inc(scaled, 1)
            dve.wait_ge(z_act, 4)
            for j in range(NT):
                gate(j)

        @block.tensor
        def _(pe):
            for j in range(NT):
                pe.wait_ge(scaled, j + 1)
                if j >= 4:
                    pe.wait_ge(gated, j - 3)
                for m in range(4):
                    last = nc.tensor.transpose(ps[j % 4][:, m * P:(m + 1) * P], of[:, j, m * P:(m + 1) * P], keep["ident"][:])
                last.then_inc(turned, 1)


KEYS = CTX + PAST + LAT
KTILES = KEYS // P


def attention_keys(nc, io, keep, K2, Vs):
    with ExitStack() as ctx:
        sb = lambda n, s, d=F32: ctx.enter_context(nc.sbuf_tensor(n, s, d))
        sem = lambda n: ctx.enter_context(nc.semaphore(n))
        kvt = sb("kv_t", [P, 2, T])
        k = sb("k_all", [P, KTILES, P])
        v = sb("v_all", [P, KTILES, P])
        kn = sb("k_normed", [P, NT, P])
        k2 = sb("k_twice", [P, 2, KTILES, P])
        doubled = sem("k_doubled")
        sq = sb("k_squares", [P, NT, P])
        ss = sb("k_sumsq", [P, 3, NT, 2])
        kg = sb("k_gain", [P, HD])
        tab = sb("rope_all", [P, 2, 8, HD])
        k_ps = ctx.enter_context(nc.psum_tensor("k_ps", [P, 1536], F32))
        v_ps = ctx.enter_context(nc.psum_tensor("v_ps", [P, 1536], F32))
        t_ps = [ctx.enter_context(nc.psum_tensor(f"kt_ps{n}", [P, 512], F32)) for n in range(2)]
        loaded, turned, a_step, v_step, kt_done, k_hi, k_lo, cache_out = (
            sem(n) for n in ("kv_in", "kv_turned", "ka_step", "kv_step", "kt_done", "k_hi", "k_lo", "cache_out"))
        block = ctx.enter_context(nc.Block())
        by_head = lambda a: a.rearrange("p j (g d) -> p j g d", g=2)

        @block.gpsimd
        def _(pool):
            nc.gpsimd.sem_clear(range(keep["first_sem"].num + 1, doubled.num))

        @block.sync
        def _(sp):
            sp.dma_start(kvt[:], io["proj_t"][4:6].rearrange("m p n -> p m n")).then_inc(loaded, 16)
            sp.dma_start(k[:, 2:6], io["cache_k"].rearrange("(j p) n -> p j n", p=P)).then_inc(loaded, 16)
            sp.dma_start(v[:, 2:6], io["cache_v"].rearrange("(j p) n -> p j n", p=P)).then_inc(loaded, 16)
            sp.dma_start(kg[:], io["k_gain"]).then_inc(loaded, 16)
            sp.dma_start(tab[:], io["rope_rows"]).then_inc(loaded, 16)
            sp.wait_ge(v_step, 5)
            sp.dma_start(io["new_k"].rearrange("(j p) n -> p j n", p=P), k[:, 0:2]).then_inc(cache_out, 16)
            sp.wait_ge(a_step, 4)
            sp.dma_start(io["new_v"].rearrange("(j p) n -> p j n", p=P), v[:, 0:2]).then_inc(cache_out, 16)
            sp.wait_ge(cache_out, 32)

        @block.tensor
        def _(pe):
            pe.wait_ge(loaded, 80)
            for j in range(NT):
                nc.tensor.transpose(k_ps[:, j * P:(j + 1) * P], kvt[:, 0, j * P:(j + 1) * P], keep["ident"][:])
            for j in range(NT):
                last = nc.tensor.transpose(v_ps[:, j * P:(j + 1) * P], kvt[:, 1, j * P:(j + 1) * P], keep["ident"][:])
            last.then_inc(turned, 1)
            pe.wait_ge(doubled, 2)
            n = 0
            for g in range(2):
                for j0 in range(0, KTILES, 4):
                    if n >= 2:
                        pe.wait_ge(k_lo, n - 1)
                    for j in range(j0, min(j0 + 4, KTILES)):
                        last = nc.tensor.transpose(t_ps[n % 2][:, (j - j0) * P:(j - j0 + 1) * P], k2[:, g, j], keep["ident"][:])
                    last.then_inc(kt_done, 1)
                    n += 1

        @block.scalar
        def _(act):
            cp = lambda o, s: nc.scalar.activation(o, s, ACT.Copy)
            act.wait_ge(turned, 1)
            nc.scalar.activation(sq[:].rearrange("p j n -> p (j n)"), k_ps[:, 0:T], ACT.Square).then_inc(a_step, 1)
            act.wait_ge(v_step, 2)
            nc.scalar.activation(ss[:, 2], ss[:, 1], ACT.Sqrt).then_inc(a_step, 1)
            cp(v[:, 0:2], v_ps[:, 0:CTX].rearrange("p (j n) -> p j n", n=P)).then_inc(a_step, 1)
            cp(v[:, 6:14], v_ps[:, CTX:T].rearrange("p (j n) -> p j n", n=P)).then_inc(a_step, 1)
            act.wait_ge(a_step, 4)
            cp(Vs[:, :, :, 0:HD], by_head(v[:])).then_inc(a_step, 1)
            act.wait_ge(v_step, 12)
            for g in range(2):
                head = k[:, :, g * HD:(g + 1) * HD].unsqueeze(2).to_broadcast([P, KTILES, 2, HD])
                cp(k2[:, g].rearrange("p j (r d) -> p j r d", r=2), head).then_inc(doubled, 1)
            n = 0
            for g in range(2):
                for j0 in range(0, KTILES, 4):
                    w = min(4, KTILES - j0) * P
                    act.wait_ge(kt_done, n + 1)
                    cp(K2[:, g, j0 * P:j0 * P + w], t_ps[n % 2][:, 0:w]).then_inc(k_hi, 1)
                    n += 1

        @block.vector
        def _(dve):
            n = [0]

            def step(ins):
                n[0] += 1
                ins.then_inc(v_step, 1)
                dve.wait_ge(v_step, n[0])

            dve.wait_ge(a_step, 1)
            step(nc.vector.tensor_reduce(ss[:, 0], by_head(sq[:]), AX_X, ALU.add))
            step(nc.vector.tensor_scalar(ss[:, 1], ss[:, 0], 1.0 / HD, EPS, ALU.mult, ALU.add))
            dve.wait_ge(a_step, 2)
            step(nc.vector.reciprocal(ss[:, 0], ss[:, 2]))
            step(nc.vector.tensor_tensor(by_head(kn[:]), k_ps[:, 0:T].rearrange("p (j g d) -> p j g d", g=2, d=HD),
                                         ss[:, 0].unsqueeze(3).to_broadcast([P, NT, 2, HD]), ALU.mult))
            gain = kg[:].unsqueeze(1).unsqueeze(1)
            step(nc.vector.tensor_tensor(by_head(k[:, 0:2]), by_head(kn[:, 0:2]), gain.to_broadcast([P, 2, 2, HD]), ALU.mult))
            step(nc.vector.tensor_tensor(by_head(kn[:, 2:NT]), by_head(kn[:, 2:NT]), gain.to_broadcast([P, 8, 2, HD]), ALU.mult))
            cos = tab[:, 0].unsqueeze(2).to_broadcast([P, 8, 2, HD])
            step(nc.vector.tensor_tensor(by_head(k[:, 6:14]), by_head(kn[:, 2:NT]), cos, ALU.mult))
            for g in range(2):
                for part in range(2):
                    pick = lambda a, at: a.rearrange("p j (x i) -> p j x i", x=2)[:, :, :, at:at + 16]
                    own = lambda a: a[:, :, g * HD:(g + 1) * HD]
                    ins = nc.vector.tensor_tensor(pick(own(sq[:, 2:NT]), 16 * part), pick(own(kn[:, 2:NT]), 16 - 16 * part), pick(tab[:, 1], 16 * part), ALU.mult)
                    step(ins)
            step(nc.vector.tensor_tensor(k[:, 6:14], k[:, 6:14], sq[:, 2:NT], ALU.add))
            dve.wait_ge(a_step, 5)
            step(nc.vector.tensor_tensor(Vs[:, :, :, HD:P], by_head(v[:]), Vs[:, :, :, 0:HD].bitcast(F32), ALU.subtract))
            n = 0
            for g in range(2):
                for j0 in range(0, KTILES, 4):
                    w = min(4, KTILES - j0) * P
                    dve.wait_ge(k_hi, n + 1)
                    low = K2[64:128, g, j0 * P:j0 * P + w]
                    nc.vector.tensor_tensor(low, t_ps[n % 2][64:128, 0:w], low.bitcast(F32), ALU.subtract).then_inc(k_lo, 1)
                    n += 1


def attend(nc, io, keep, K2, Vs, tag, tile0, tiles, nb, w, key0, rotary):
    with ExitStack() as ctx:
        sb = lambda n, s, d=F32: ctx.enter_context(nc.sbuf_tensor(tag + n, s, d))
        sem = lambda n: ctx.enter_context(nc.semaphore(tag + n))
        wt = w // P
        qin = sb("q_t", [P, 4, P])
        rt = sb("rope_tile", [P, 2, HD])
        q1, q2, qt = (sb(n, [P, NH, HD]) for n in ("q1", "q2", "q_tmp"))
        qd = sb("q_twice", [P, NH, P])
        st = sb("q_stats", [P, 4, NH])
        qg = sb("q_gain", [P, HD])
        Qh = sb("q_hi2", [P, NH, P], F32R)
        Ql = sb("q_lo2", [P, NH, P], F32R)
        pr = sb("probs", [P, 2, nb * w])
        pmax = sb("block_max", [P, NH, 3])
        negm = sb("neg_max", [P, NH])
        sums = sb("block_sums", [P, NH, nb])
        rinv = sb("inv_sums", [P, 2, NH])
        PTh = sb("probs_t_hi", [P, 2, nb * wt, 4, P], F32R)
        PTl = sb("probs_t_lo", [P, 2, nb * wt, 4, P], F32R)
        tmp = sb("o_low", [64, 4, P])
        bc = sb("inv_bcast", [64, 4, P])
        u = sb("o_sum", [64, 4, P])
        oT = sb("o_t", [P, 4, P])
        s_ps = [ctx.enter_context(nc.psum_tensor(f"{tag}s_ps{n}", [P, 512], F32)) for n in range(4)]
        t_ps = [ctx.enter_context(nc.psum_tensor(f"{tag}t_ps{n}", [P, 512], F32)) for n in range(2)]
        o_ps = ctx.enter_context(nc.psum_tensor(tag + "o_ps", [P, 512], F32))
        m_ps = ctx.enter_context(nc.psum_tensor(tag + "m_ps", [P, 512], F32))
        names = ("gain_in q_in stored q_rows q_squared q_mean q_root q_step dup_done q_hi q_lo scores_done block_maxed max_ready "
                 "exp_done turned hi_ready lo_ready sums_ready inv_ready pv_done tmp_ready inv_ps inv_copied u_ready out_ready").split()
        e = {n: sem(n) for n in names}
        block = ctx.enter_context(nc.Block())
        QS = 6 if rotary else 2

        def each_tile(eng, body):
            body(0, True)
            with eng.Fori(1, tiles) as n:
                body(n, False)

        def rows_of(n):
            return bass.ds(n * P + tile0 * P, P)

        @block.sync
        def _(sp):
            sp.dma_start(qg[:], io["q_gain"]).then_inc(e["gain_in"], 16)

            def body(n, first):
                if not first:
                    sp.wait_ge(e["q_rows"], n)
                sp.dma_start(qin[:], io["proj_t"][0:4, :, rows_of(n)].rearrange("m p n -> p m n")).then_inc(e["q_in"], 16)
                if rotary:
                    if not first:
                        sp.wait_ge(e["q_step"], QS * n)
                    sp.dma_start(rt[:], io["rope_tiles"][bass.ds(n, 1)].rearrange("o p a d -> p (o a) d")).then_inc(e["q_in"], 16)
                sp.wait_ge(e["out_ready"], 2 * n + 2)
                sp.dma_start(io["oa_t"][:, :, rows_of(n)].rearrange("m p n -> p m n"), oT[:]).then_inc(e["stored"], 16)
            each_tile(sp, body)
            sp.wait_ge(e["stored"], 16 * tiles)

        @block.tensor
        def _(pe):
            def scores(n, h):
                for kb in range(nb):
                    G = nb * h + kb
                    if not (isinstance(n, int) and n == 0 and G < 4):
                        pe.wait_ge(e["exp_done"], nb * NH * n + G - 3)
                    keys = K2[:, h // 4, key0 + kb * w:key0 + (kb + 1) * w]
                    o = s_ps[G % 4][:, 0:w]
                    nc.tensor.matmul(o, Qh[:, h], keys, start=True, stop=False)
                    nc.tensor.matmul(o, Ql[:, h], keys, start=False, stop=True).then_inc(e["scores_done"], 1)

            def turn(n, h, first):
                for c in range(nb):
                    G = nb * h + c
                    pe.wait_ge(e["exp_done"], nb * NH * n + G + 1)
                    if G >= 2:
                        pe.wait_ge(e["lo_ready"], nb * NH * n + G - 1)
                    else:
                        pe.wait_ge(e["q_lo"], 2 * n + G + 1)
                    for b in range(wt):
                        last = nc.tensor.transpose(t_ps[G % 2][:, b * P:(b + 1) * P], pr[:, h % 2, c * w + b * P:c * w + (b + 1) * P], keep["ident"][:])
                    last.then_inc(e["turned"], 1)

            def values(n, g, first):
                pe.wait_ge(e["lo_ready"], nb * NH * n + nb * (4 * g + 4))
                if not (first and g == 0):
                    pe.wait_ge(e["u_ready"], 2 * n + g)
                for kt in range(nb * wt):
                    lhs = Vs[:, key0 // P + kt, g]
                    nc.tensor.matmul(o_ps[:], lhs, PTh[:, g, kt].rearrange("p h q -> p (h q)"), start=(kt == 0), stop=False)
                    last = nc.tensor.matmul(o_ps[:], lhs, PTl[:, g, kt].rearrange("p h q -> p (h q)"), start=False, stop=(kt == nb * wt - 1))
                last.then_inc(e["pv_done"], 1)
                pe.wait_ge(e["inv_ready"], 2 * n + g + 1)
                if not (first and g == 0):
                    pe.wait_ge(e["inv_copied"], 2 * n + g)
                for m in range(4):
                    last = nc.tensor.matmul(m_ps[0:64, m * P:(m + 1) * P], rinv[:, 1, 4 * g + m:4 * g + m + 1].to_broadcast([P, 64]), keep["ident"][:], start=True, stop=True)
                last.then_inc(e["inv_ps"], 1)

            def body(n, first):
                pe.wait_ge(e["q_in"], (32 if rotary else 16) * n + (32 if rotary else 16))
                if not first:
                    pe.wait_ge(e["inv_copied"], 2 * n)
                for m in range(4):
                    last = nc.tensor.transpose(m_ps[:, m * P:(m + 1) * P], qin[:, m], keep["ident"][:])
                last.then_inc(e["q_rows"], 1)
                for c in range(2):
                    pe.wait_ge(e["q_step"], QS * n + QS)
                    if not first:
                        pe.wait_ge(e["lo_ready"], nb * NH * n)
                    for m in range(4):
                        last = nc.tensor.transpose(t_ps[c][:, m * P:(m + 1) * P], qd[:, 4 * c + m], keep["ident"][:])
                    last.then_inc(e["dup_done"], 1)
                pe.wait_ge(e["q_lo"], 2 * n + 2)
                for h in range(NH + 1):
                    if h < NH:
                        scores(n, h)
                    if h:
                        turn(n, h - 1, first)
                    if h == 5:
                        values(n, 0, first)
                values(n, 1, first)
            each_tile(pe, body)

        @block.scalar
        def _(act):
            cp = lambda o, s: nc.scalar.activation(o, s, ACT.Copy)

            def body(n, first):
                act.wait_ge(e["q_rows"], n + 1)
                nc.scalar.activation(qt[:].rearrange("p h d -> p (h d)"), m_ps[:], ACT.Square).then_inc(e["q_squared"], 1)
                act.wait_ge(e["q_mean"], 2 * n + 2)
                nc.scalar.activation(st[:, 2], st[:, 1], ACT.Ln).then_inc(e["q_root"], 1)
                act.wait_ge(e["q_root"], 2 * n + 1)
                nc.scalar.activation(st[:, 3], st[:, 2], ACT.Exp, scale=-0.5).then_inc(e["q_root"], 1)
                for c in range(2):
                    act.wait_ge(e["dup_done"], 2 * n + c + 1)
                    cp(Qh[:, 4 * c:4 * c + 4].rearrange("p h n -> p (h n)"), t_ps[c][:]).then_inc(e["q_hi"], 1)

                def finish(g):
                    act.wait_ge(e["pv_done"], 2 * n + g + 1)
                    if not (first and g == 0):
                        act.wait_ge(e["u_ready"], 2 * n + g)
                    cp(tmp[:].rearrange("p h q -> p (h q)"), o_ps[64:128, :]).then_inc(e["tmp_ready"], 1)
                    act.wait_ge(e["inv_ps"], 2 * n + g + 1)
                    if not (first and g == 0):
                        act.wait_ge(e["out_ready"], 2 * n + g)
                    cp(bc[:].rearrange("p h q -> p (h q)"), m_ps[0:64, :]).then_inc(e["inv_copied"], 1)

                for h in range(NH + 1):
                    if h < NH:
                        act.wait_ge(e["max_ready"], NH * n + h + 1)
                        if not (first and h < 2):
                            act.wait_ge(e["turned"], nb * (NH * n + h - 1))
                        for kb in range(nb):
                            G = nb * h + kb
                            nc.scalar.activation(pr[:, h % 2, kb * w:(kb + 1) * w], s_ps[G % 4][:, 0:w], ACT.Exp, bias=negm[:, h:h + 1],
                                                 accum_out=sums[:, h, kb:kb + 1]).then_inc(e["exp_done"], 1)
                    if h:
                        g, hh = (h - 1) // 4, (h - 1) % 4
                        if not first:
                            act.wait_ge(e["pv_done"], 2 * n - 1 + g)
                        for c in range(nb):
                            G = nb * (h - 1) + c
                            act.wait_ge(e["turned"], nb * NH * n + G + 1)
                            cp(PTh[:, g, c * wt:(c + 1) * wt, hh], t_ps[G % 2][:, 0:w].rearrange("p (b q) -> p b q", b=wt)).then_inc(e["hi_ready"], 1)
                    if h == 6:
                        finish(0)
                finish(1)
            each_tile(act, body)

        @block.vector
        def _(dve):
            dve.wait_ge(e["gain_in"], 16)
            over_heads = lambda a: a.unsqueeze(1).to_broadcast([P, NH, HD])

            def body(n, first):
                qs = [0]

                def step(ins, wait=True):
                    qs[0] += 1
                    ins.then_inc(e["q_step"], 1)
                    if wait:
                        dve.wait_ge(e["q_step"], QS * n + qs[0])

                dve.wait_ge(e["q_squared"], n + 1)
                nc.vector.tensor_reduce(st[:, 0], qt[:], AX_X, ALU.add).then_inc(e["q_mean"], 1)
                dve.wait_ge(e["q_mean"], 2 * n + 1)
                nc.vector.tensor_scalar(st[:, 1], st[:, 0], HD * EPS, None, ALU.add).then_inc(e["q_mean"], 1)
                dve.wait_ge(e["q_root"], 2 * n + 2)
                step(nc.vector.tensor_tensor(q1[:], m_ps[:].rearrange("p (h d) -> p h d", d=HD), st[:, 3].unsqueeze(2).to_broadcast([P, NH, HD]), ALU.mult))
                twice = lambda a: a.unsqueeze(2).to_broadcast([P, NH, 2, HD])
                both = qd[:].rearrange("p h (r d) -> p h r d", r=2)
                gained = nc.vector.tensor_tensor(q1[:], q1[:], over_heads(qg[:]), ALU.mult) if rotary else \
                    nc.vector.tensor_tensor(both, twice(q1[:]), qg[:].unsqueeze(1).unsqueeze(1).to_broadcast([P, NH, 2, HD]), ALU.mult)
                step(gained)
                if rotary:
                    dve.wait_ge(e["q_in"], 32 * n + 32)
                    step(nc.vector.tensor_tensor(q2[:], q1[:], over_heads(rt[:, 0]), ALU.mult), False)
                    pick = lambda a, at: a.rearrange("p h (x i) -> p h x i", x=2)[:, :, :, at:at + 16]
                    for part in range(2):
                        sin = rt[:, 1].rearrange("p (x i) -> p x i", x=2)[:, :, 16 * part:16 * part + 16].unsqueeze(1).to_broadcast([P, NH, 2, 16])
                        step(nc.vector.tensor_tensor(pick(qt[:], 16 * part), pick(q1[:], 16 - 16 * part), sin, ALU.mult), part == 1)
                    step(nc.vector.tensor_tensor(both, twice(q2[:]), twice(qt[:]), ALU.add))
                for c in range(2):
                    dve.wait_ge(e["q_hi"], 2 * n + c + 1)
                    nc.vector.tensor_tensor(Ql[:, 4 * c:4 * c + 4].rearrange("p h n -> p (h n)"), t_ps[c][:], Qh[:, 4 * c:4 * c + 4].rearrange("p h n -> p (h n)").bitcast(F32), ALU.subtract).then_inc(e["q_lo"], 1)

                def inverse(g):
                    dve.wait_ge(e["exp_done"], nb * (NH * n + 4 * g + 4))
                    nc.vector.tensor_reduce(rinv[:, 0, 4 * g:4 * g + 4], sums[:, 4 * g:4 * g + 4], AX_X, ALU.add).then_inc(e["sums_ready"], 1)
                    dve.wait_ge(e["sums_ready"], 2 * n + g + 1)
                    nc.vector.reciprocal(rinv[:, 1, 4 * g:4 * g + 4], rinv[:, 0, 4 * g:4 * g + 4]).then_inc(e["inv_ready"], 1)

                def finish(g):
                    dve.wait_ge(e["tmp_ready"], 2 * n + g + 1)
                    nc.vector.tensor_tensor(u[:].rearrange("p h q -> p (h q)"), o_ps[0:64, :], tmp[:].rearrange("p h q -> p (h q)"), ALU.add).then_inc(e["u_ready"], 1)
                    dve.wait_ge(e["u_ready"], 2 * n + g + 1)
                    dve.wait_ge(e["inv_copied"], 2 * n + g + 1)
                    if not first:
                        dve.wait_ge(e["stored"], 16 * n)
                    for par in range(2):
                        last = nc.vector.tensor_tensor(oT[64 * par:64 * par + 64, 2 * g:2 * g + 2], u[:, par::2], bc[:, par::2], ALU.mult)
                    last.then_inc(e["out_ready"], 1)

                for h in range(NH + 1):
                    if h < NH:
                        for kb in range(nb):
                            G = nb * h + kb
                            dve.wait_ge(e["scores_done"], nb * NH * n + G + 1)
                            nc.vector.tensor_reduce(pmax[:, h, kb:kb + 1], s_ps[G % 4][:, 0:w], AX_X, ALU.max).then_inc(e["block_maxed"], 1)
                        dve.wait_ge(e["block_maxed"], nb * (NH * n + h + 1))
                        nc.vector.tensor_reduce(negm[:, h:h + 1], pmax[:, h, 0:nb], AX_X, ALU.max, negate=True).then_inc(e["max_ready"], 1)
                    if h:
                        g, hh = (h - 1) // 4, (h - 1) % 4
                        for c in range(nb):
                            G = nb * (h - 1) + c
                            dve.wait_ge(e["hi_ready"], nb * NH * n + G + 1)
                            dst = slice(c * wt, (c + 1) * wt)
                            nc.vector.tensor_tensor(PTl[:, g, dst, hh], t_ps[G % 2][:, 0:w].rearrange("p (b q) -> p b q", b=wt), PTh[:, g, dst, hh].bitcast(F32), ALU.subtract).then_inc(e["lo_ready"], 1)
                    if h == 4:
                        inverse(0)
                    if h == 6:
                        finish(0)
                inverse(1)
                finish(1)
            each_tile(dve, body)


def attention(nc, io, keep):
    with ExitStack() as ctx:
        K2 = ctx.enter_context(nc.sbuf_tensor("keys_hi_lo", [P, 2, KEYS], F32R))
        Vs = ctx.enter_context(nc.sbuf_tensor("values_hi_lo", [P, KTILES, 2, P], F32R))
        attention_keys(nc, io, keep, K2, Vs)
        attend(nc, io, keep, K2, Vs, "c_", 0, 2, 1, CTX, 0, False)
        attend(nc, io, keep, K2, Vs, "l_", 2, 8, 3, 512, CTX, True)


HT = T // 2
HJ = HT // P


def half_segments(half, lo, hi):
    return [(a - half * HT, b - half * HT, s) for a, b, s in segments(half * HT + lo, half * HT + hi)]


def mix_out(nc, io, keep, half, x1, h_hi, h_lo):
    with ExitStack() as ctx:
        tag = f"m{half}_"
        sb = lambda n, s, d=F32: ctx.enter_context(nc.sbuf_tensor(tag + n, s, d))
        sem = lambda n: ctx.enter_context(nc.semaphore(tag + n))
        raw = sb("w_raw", [P, 2, KT, P])
        whi = sb("w_hi", [P, 2, KT, P], F32R)
        wlo = sb("w_lo", [P, 2, KT, P], F32R)
        o_raw = sb("o_raw", [P, KT, HT])
        o_hi = sb("o_hi", [P, KT, HT], F32R)
        o_lo = sb("o_lo", [P, KT, HT], F32R)
        gate = sb("gates", [P, 2, 2, HT])
        rows = sb("x_rows2", [P, HJ, D])
        rstd = sb("rstd", [P, 2, HT])
        ps = [ctx.enter_context(nc.psum_tensor(f"{tag}ps{p}", [P, 4, 512], F32)) for p in range(2)]
        w_in = [sem(f"w_in{p}") for p in range(2)]
        g_in = [sem(f"g_in{p}") for p in range(2)]
        names = ("o_in x_in hi lo o_split o_split_lo done sig weighted summed m_hi m_lo xt_ps xt x1_ready x1_sq total norm scaled h_hi").split()
        e = {n: sem(n) for n in names}
        block = ctx.enter_context(nc.Block())
        N = 2 * KT
        tok = slice(half * HT, (half + 1) * HT)
        mod, mod_s = keep["mod"], keep["mod_scale"]
        cp = lambda o, s: nc.scalar.activation(o, s, ACT.Copy)
        groups = lambda p, a: ps[p][:, a:a + 2, 0:GN]
        two = lambda a: a.rearrange("p (g n) -> p g n", g=2)

        @block.sync
        def _(sp):
            for m in range(4):
                sp.dma_start(o_raw[:, m], io["oa_t"][m, :, tok]).then_inc(e["o_in"], 16)
                sp.dma_start(o_raw[:, 4 + m], io["od_t"][m, :, tok]).then_inc(e["o_in"], 16)
            for t in range(N):
                if t >= 2:
                    sp.wait_ge(e["lo"], t - 1)
                sp.dma_start(raw[:, t % 2], io["w_mix"][t]).then_inc(w_in[t % 2], 16)
                if t < KT:
                    if t >= 2:
                        sp.wait_ge(e["m_lo"], t - 1)
                    sp.dma_start(gate[:, t % 2, 0], io["proj_t"][10 + t, :, tok]).then_inc(g_in[t % 2], 16)
                    sp.dma_start(gate[:, t % 2, 1], io["proj_t"][18 + t, :, tok]).then_inc(g_in[t % 2], 16)

        @block.gpsimd
        def _(pool):
            for t in range(KT):
                pool.wait_ge(e["weighted"], 2 * t + 2)
                nc.gpsimd.tensor_tensor(gate[:, t % 2, 0], gate[:, t % 2, 0], gate[:, t % 2, 1], ALU.add).then_inc(e["summed"], 1)
                pool.wait_ge(e["m_hi"], t + 1)
                nc.gpsimd.tensor_tensor(h_lo[:, t], gate[:, t % 2, 0], h_hi[:, t].bitcast(F32), ALU.subtract).then_inc(e["m_lo"], 1)

        @block.scalar
        def _(act):
            act.dma_start(rows[:], io["x"][tok, :].rearrange("(j p) n -> p j n", p=P)).then_inc(e["x_in"], 16)

            def split_hi(t):
                act.wait_ge(w_in[t % 2], 16 * (t // 2 + 1))
                if t >= 2:
                    act.wait_ge(e["done"], t - 1)
                cp(whi[:, t % 2], raw[:, t % 2]).then_inc(e["hi"], 1)

            split_hi(0)
            act.wait_ge(e["o_in"], 128)
            for k in range(KT):
                cp(o_hi[:, k], o_raw[:, k]).then_inc(e["o_split"], 1)
            for t in range(N):
                if t + 1 < N:
                    split_hi(t + 1)
                if t < KT:
                    act.wait_ge(g_in[t % 2], 32 * (t // 2 + 1))
                    nc.scalar.activation(gate[:, t % 2], gate[:, t % 2], ACT.Sigmoid).then_inc(e["sig"], 1)
                    act.wait_ge(e["summed"], t + 1)
                    cp(h_hi[:, t], gate[:, t % 2, 0]).then_inc(e["m_hi"], 1)
                else:
                    m = t - KT
                    act.wait_ge(e["xt_ps"], m + 1)
                    cp(x1[:, m, 0:512], ps[t % 2][:, 2])
                    cp(x1[:, m, 512:HT], ps[t % 2][:, 3, 0:P]).then_inc(e["xt"], 1)
            for m in range(KT):
                act.wait_ge(e["x1_ready"], m + 1)
                nc.scalar.activation(o_raw[:, m], x1[:, m], ACT.Square).then_inc(e["x1_sq"], 1)
            act.wait_ge(e["norm"], 1)
            nc.scalar.activation(rstd[:, 1], rstd[:, 0], ACT.Sqrt).then_inc(e["norm"], 1)
            for m in range(KT):
                act.wait_ge(e["scaled"], m + 1)
                for lo, hi, seg in half_segments(half, 0, HT):
                    last = nc.scalar.activation(h_hi[:, m, lo:hi], o_raw[:, m, lo:hi], ACT.Identity, bias=mod[:, 24 + m, seg:seg + 1])
                last.then_inc(e["h_hi"], 1)

        @block.vector
        def _(dve):
            def split_lo(t):
                dve.wait_ge(e["hi"], t + 1)
                if t >= 2:
                    dve.wait_ge(e["done"], t - 1)
                nc.vector.tensor_tensor(wlo[:, t % 2], raw[:, t % 2], whi[:, t % 2].bitcast(F32), ALU.subtract).then_inc(e["lo"], 1)

            split_lo(0)
            for k in range(KT):
                dve.wait_ge(e["o_split"], k + 1)
                nc.vector.tensor_tensor(o_lo[:, k], o_raw[:, k], o_hi[:, k].bitcast(F32), ALU.subtract).then_inc(e["o_split_lo"], 1)
            for t in range(N):
                if t + 1 < N:
                    split_lo(t + 1)
                dve.wait_ge(e["done"], t + 1)
                if t < KT:
                    dve.wait_ge(e["sig"], t + 1)
                    for s in range(2):
                        nc.vector.tensor_tensor(two(gate[:, t % 2, s]), groups(t % 2, 2 * s), two(gate[:, t % 2, s]), ALU.mult).then_inc(e["weighted"], 1)
                else:
                    m = t - KT
                    dve.wait_ge(e["xt"], m + 1)
                    for g in range(2):
                        for lo, hi, seg in half_segments(half, g * GN, (g + 1) * GN):
                            last = nc.vector.scalar_tensor_tensor(x1[:, m, lo:hi], ps[t % 2][:, g, lo - g * GN:hi - g * GN], mod[:, 16 + m, seg:seg + 1], x1[:, m, lo:hi], ALU.mult, ALU.add)
                    last.then_inc(e["x1_ready"], 1)
            dve.wait_ge(e["total"], 1)
            nc.vector.tensor_scalar(two(rstd[:, 0]), groups(0, 0), 1.0 / D, EPS, ALU.mult, ALU.add).then_inc(e["norm"], 1)
            dve.wait_ge(e["norm"], 2)
            nc.vector.reciprocal(rstd[:, 0], rstd[:, 1]).then_inc(e["norm"], 1)
            dve.wait_ge(e["norm"], 3)
            for m in range(KT):
                for lo, hi, seg in half_segments(half, 0, HT):
                    last = nc.vector.scalar_tensor_tensor(o_raw[:, m, lo:hi], x1[:, m, lo:hi], mod_s[:, 1, m, seg:seg + 1], rstd[:, 0, lo:hi], ALU.mult, ALU.mult)
                last.then_inc(e["scaled"], 1)
            for m in range(KT):
                dve.wait_ge(e["h_hi"], m + 1)
                for lo, hi, seg in half_segments(half, 0, HT):
                    nc.vector.scalar_tensor_tensor(h_lo[:, m, lo:hi], o_raw[:, m, lo:hi], mod[:, 24 + m, seg:seg + 1], h_hi[:, m, lo:hi].bitcast(F32), ALU.add, ALU.subtract)

        @block.tensor
        def _(pe):
            part = lambda a, g: lambda k: a[:, k, g * GN:(g + 1) * GN]
            w = lambda a, p: lambda k: a[:, p, k]
            pe.wait_ge(e["o_split_lo"], KT)
            for t in range(N):
                p = t % 2
                pe.wait_ge(e["lo"], t + 1)
                if t < KT:
                    if t >= 2:
                        pe.wait_ge(e["weighted"], 2 * t - 2)
                    for s in range(2):
                        for g in range(2):
                            last = split_product(nc, ps[p][:, 2 * s + g, 0:GN], w(whi, p), w(wlo, p), part(o_hi, g), part(o_lo, g), range(4 * s, 4 * s + 4))
                else:
                    m = t - KT
                    if m < 2:
                        pe.wait_ge(e["weighted"], 2 * (t - 2) + 2)
                    else:
                        pe.wait_ge(e["x1_ready"], m - 1)
                    if m == 0:
                        pe.wait_ge(e["x_in"], 16)
                    for j in range(HJ):
                        last = nc.tensor.transpose(ps[p][:, 2 + j // 4, (j % 4) * P:(j % 4 + 1) * P], rows[:, j, m * P:(m + 1) * P], keep["ident"][:])
                    last.then_inc(e["xt_ps"], 1)
                    pe.wait_ge(e["m_lo"], KT)
                    for g in range(2):
                        last = split_product(nc, ps[p][:, g, 0:GN], w(whi, p), w(wlo, p), part(h_hi, g), part(h_lo, g), range(KT))
                last.then_inc(e["done"], 1)
            pe.wait_ge(e["x1_ready"], KT)
            pe.wait_ge(e["x1_sq"], KT)
            for g in range(2):
                for m in range(KT):
                    last = nc.tensor.matmul(ps[0][:, g, 0:GN], keep["ones"][:], o_raw[:, m, g * GN:(g + 1) * GN], start=(m == 0), stop=(m == KT - 1))
            last.then_inc(e["total"], 1)


def feed_forward(nc, io, keep, half, x1, h_hi, h_lo):
    with ExitStack() as ctx:
        tag = f"f{half}_"
        sb = lambda n, s, d=F32: ctx.enter_context(nc.sbuf_tensor(tag + n, s, d))
        sem = lambda n: ctx.enter_context(nc.semaphore(tag + n))
        raw = sb("w_raw", [P, 2, KT, P])
        whi = sb("w_hi", [P, 2, KT, P], F32R)
        wlo = sb("w_lo", [P, 2, KT, P], F32R)
        f_hi = sb("ff_hi", [P, FT, HT], F32R)
        f_lo = sb("ff_lo", [P, FT, HT], F32R)
        sg = sb("silu_gate", [P, 2, HT])
        hf = sb("ff_f32", [P, 2, HT])
        ps = [ctx.enter_context(nc.psum_tensor(f"{tag}ps{p}", [P, 4, 512], F32)) for p in range(2)]
        w_in = [sem(f"w_in{p}") for p in range(2)]
        names = "hi lo done sig prod f_hi f_lo y_t yt_ps y_rows".split()
        e = {n: sem(n) for n in names}
        stored = [sem(f"stored{p}") for p in range(2)]
        block = ctx.enter_context(nc.Block())
        mod = keep["mod"]
        NU = 2 * FT
        PARTS = ((0, 8), (8, 15), (15, 22))
        tok0 = half * HT
        cp = lambda o, s: nc.scalar.activation(o, s, ACT.Copy)
        two = lambda a: a.rearrange("p (g n) -> p g n", g=2)

        def phases(eng, up, down):
            up(0, True, False)
            with eng.Fori(1, FT // 2 - 1) as i:
                up(i, False, False)
            up(FT // 2 - 1, False, True)
            down(0, True, False)
            with eng.Fori(1, KT // 2 - 1) as i:
                down(i, False, False)
            down(KT // 2 - 1, False, True)

        @block.sync
        def _(sp):
            for t in range(2):
                sp.dma_start(raw[:, t], io["w_up"][t]).then_inc(w_in[t], 16)

            def up(i, first, last):
                for r in range(4):
                    t = 4 * i + r + 2
                    sp.wait_ge(e["lo"], t - 1)
                    if last and r >= 2:
                        load_part(0, r - 2, r - 2, r % 2)
                    else:
                        sp.dma_start(raw[:, r % 2], io["w_up"][bass.ds(t, 1)].rearrange("o p k n -> p (o k) n")).then_inc(w_in[r % 2], 16)

            def load_part(m, c, seq, slot):
                a, b = PARTS[c]
                src = io["w_down"][bass.ds(m, 1)].rearrange("o p k n -> p (o k) n")
                sp.dma_start(raw[:, slot, 0:b - a], src[:, a:b]).then_inc(w_in[slot], 16)

            def down(i, first, last):
                for q in range(2):
                    for c in range(3):
                        s = 3 * q + c + 2
                        if not (last and s >= 6):
                            sp.wait_ge(e["lo"], NU + 6 * i + s - 1)
                            load_part(2 * i + s // 3, s % 3, s, s % 2)
                    if not (first and q == 0):
                        store_rows(2 * i + q - 1, 1 - q)

            def store_rows(m, q):
                sp.wait_ge(e["y_rows"], m + 1)
                sp.dma_start(io["y"][tok0:tok0 + HT, bass.ds(m * P, P)].rearrange("(j p) n -> p j n", p=P), sg[:, q].rearrange("p (j n) -> p j n", n=P)).then_inc(stored[q], 16)

            phases(sp, up, down)
            store_rows(KT - 1, 1)
            for p in range(2):
                sp.wait_ge(stored[p], 16 * (KT // 2))

        @block.gpsimd
        def _(pool):
            def up(i, first, last):
                for q in range(2):
                    f = 2 * i + q
                    pool.wait_ge(e["f_hi"], f + 1)
                    nc.gpsimd.tensor_tensor(f_lo[:, bass.ds(f, 1)].rearrange("p o n -> p (o n)"), hf[:, q], f_hi[:, bass.ds(f, 1)].rearrange("p o n -> p (o n)").bitcast(F32), ALU.subtract).then_inc(e["f_lo"], 1)

            up(0, True, False)
            with pool.Fori(1, FT // 2) as i:
                up(i, False, False)

        @block.scalar
        def _(act):
            def split_hi(t, slot, arrivals, nk=KT, wait=True):
                act.wait_ge(w_in[slot], 16 * arrivals)
                if wait:
                    act.wait_ge(e["done"], t - 1)
                cp(whi[:, slot, 0:nk], raw[:, slot, 0:nk]).then_inc(e["hi"], 1)

            split_hi(0, 0, 1, wait=False)

            def up(i, first, last):
                for q in range(2):
                    f = 2 * i + q
                    split_hi(2 * f + 1, 1, f + 1, wait=not (first and q == 0))
                    act.wait_ge(e["done"], 2 * f + 1)
                    if not first:
                        act.wait_ge(e["prod"], f - 1)
                    nc.scalar.activation(two(sg[:, q]), ps[q][:, 0:2, 0:GN], ACT.Silu).then_inc(e["sig"], 1)
                    split_hi(2 * f + 2, 0, f + 2)
                    act.wait_ge(e["prod"], f + 1)
                    cp(f_hi[:, bass.ds(f, 1)].rearrange("p o n -> p (o n)"), hf[:, q]).then_inc(e["f_hi"], 1)

            def down(i, first, last):
                for q in range(2):
                    m = 2 * i + q
                    for c in range(3):
                        s = 3 * q + c + 1
                        if not (last and s == 6):
                            a, b = PARTS[s % 3]
                            split_hi(NU + 6 * i + s, s % 2, FT + 3 * i + s // 2 + 1, b - a)
                    if not (first and q == 0):
                        copy_rows(m - 1, 1 - q, None if first else 16 * (i - 1 + q))

            def copy_rows(m, q, stores):
                act.wait_ge(e["yt_ps"], m + 1)
                if stores is not None:
                    act.wait_ge(stored[q], stores)
                cp(sg[:, q, 0:512], ps[q][:, 2])
                cp(sg[:, q, 512:HT], ps[q][:, 3, 0:P]).then_inc(e["y_rows"], 1)

            phases(act, up, down)
            copy_rows(KT - 1, 1, 16 * (KT // 2 - 1))

        @block.vector
        def _(dve):
            def split_lo(t, slot, nk=KT, wait=True):
                dve.wait_ge(e["hi"], t + 1)
                if wait:
                    dve.wait_ge(e["done"], t - 1)
                nc.vector.tensor_tensor(wlo[:, slot, 0:nk], raw[:, slot, 0:nk], whi[:, slot, 0:nk].bitcast(F32), ALU.subtract).then_inc(e["lo"], 1)

            split_lo(0, 0, wait=False)

            def up(i, first, last):
                for q in range(2):
                    f = 2 * i + q
                    split_lo(2 * f + 1, 1, wait=not (first and q == 0))
                    split_lo(2 * f + 2, 0)
                    dve.wait_ge(e["sig"], f + 1)
                    dve.wait_ge(e["done"], 2 * f + 2)
                    if not first:
                        dve.wait_ge(e["f_lo"], f - 1)
                    nc.vector.tensor_tensor(two(hf[:, q]), ps[q][:, 2:4, 0:GN], two(sg[:, q]), ALU.mult).then_inc(e["prod"], 1)

            def down(i, first, last):
                for q in range(2):
                    m = 2 * i + q
                    for c in range(3):
                        s = 3 * q + c + 1
                        if not (last and s == 6):
                            a, b = PARTS[s % 3]
                            split_lo(NU + 6 * i + s, s % 2, b - a)
                    dve.wait_ge(e["done"], NU + 3 * m + 3)
                    if first:
                        dve.wait_ge(e["f_lo"], FT)
                    else:
                        dve.wait_ge(e["yt_ps"], m - 1)
                    for g in range(2):
                        for lo, hi, seg in half_segments(half, g * GN, (g + 1) * GN):
                            x1m = x1[:, bass.ds(m, 1), lo:hi].rearrange("p o n -> p (o n)")
                            gain = gate2[:, bass.ds(m, 1), seg].rearrange("p o -> p o")
                            last_ = nc.vector.scalar_tensor_tensor(hf[:, q, lo:hi], ps[q][:, g, lo - g * GN:hi - g * GN], gain, x1m, ALU.mult, ALU.add)
                    last_.then_inc(e["y_t"], 1)

            gate2 = mod[:, 40:48]
            phases(dve, up, down)

        @block.tensor
        def _(pe):
            part = lambda a, g: lambda k: a[:, k, g * GN:(g + 1) * GN]
            w = lambda a, p, k0=0: lambda k: a[:, p, k - k0]

            def up(i, first, last):
                for q in range(2):
                    f = 2 * i + q
                    for u in range(2):
                        pe.wait_ge(e["lo"], 2 * f + u + 1)
                        if not first:
                            pe.wait_ge(e["sig"] if u == 0 else e["prod"], f - 1)
                        for g in range(2):
                            ins = split_product(nc, ps[q][:, 2 * u + g, 0:GN], w(whi, u), w(wlo, u), part(h_hi, g), part(h_lo, g), range(KT))
                        ins.then_inc(e["done"], 1)

            def turn_y(m, q, first):
                pe.wait_ge(e["y_t"], m + 1)
                if not first:
                    pe.wait_ge(e["y_rows"], m - 1)
                for j in range(HJ):
                    ins = nc.tensor.transpose(ps[q][:, 2 + j // 4, (j % 4) * P:(j % 4 + 1) * P], hf[:, q, j * P:(j + 1) * P], keep["ident"][:])
                ins.then_inc(e["yt_ps"], 1)

            def down(i, first, last):
                for q in range(2):
                    m = 2 * i + q
                    if first and q == 0:
                        pe.wait_ge(e["f_lo"], FT)
                    for c, (a, b) in enumerate(PARTS):
                        s = 3 * q + c
                        pe.wait_ge(e["lo"], NU + 6 * i + s + 1)
                        if c == 0:
                            if first:
                                pe.wait_ge(e["prod"], FT - 1 + q)
                            else:
                                pe.wait_ge(e["y_t"], m - 1)
                        for g in range(2):
                            ins = split_product(nc, ps[q][:, g, 0:GN], w(whi, s % 2, a), w(wlo, s % 2, a), part(f_hi, g), part(f_lo, g), range(a, b), first=(c == 0), last=(c == 2))
                        ins.then_inc(e["done"], 1)
                    if not (first and q == 0):
                        turn_y(m - 1, 1 - q, first)

            phases(pe, up, down)
            turn_y(KT - 1, 1, False)


def merge_and_ffn(nc, io, keep):
    for half in range(2):
        with ExitStack() as ctx:
            x1 = ctx.enter_context(nc.sbuf_tensor(f"x1_{half}", [P, KT, HT], F32))
            h_hi = ctx.enter_context(nc.sbuf_tensor(f"h2_hi{half}", [P, KT, HT], F32R))
            h_lo = ctx.enter_context(nc.sbuf_tensor(f"h2_lo{half}", [P, KT, HT], F32R))
            mix_out(nc, io, keep, half, x1, h_hi, h_lo)
            feed_forward(nc, io, keep, half, x1, h_hi, h_lo)


def build(nc, io):
    with ExitStack() as ctx:
        sb = lambda n, s, d=F32: ctx.enter_context(nc.sbuf_tensor(n, s, d))
        keep = {
            "ident": sb("ident_sb", [P, P]),
            "mod": sb("mod", [P, 48, 2]),
            "mod_scale": sb("mod_scale", [P, 2, KT, 2]),
            "bg": sb("beta_gate_cols", [P, NT, 32]),
            "ones": sb("ones_sb", [P, P]),
        }
        keep["first_sem"] = ctx.enter_context(nc.semaphore("first_sem"))
        with ExitStack() as c1:
            h_hi = c1.enter_context(nc.sbuf_tensor("h_hi", [P, KT, T], F32R))
            h_lo = c1.enter_context(nc.sbuf_tensor("h_lo", [P, KT, T], F32R))
            ada_and_norm(nc, io, keep, h_hi, h_lo)
            in_projection(nc, io, keep, h_hi, h_lo)
        with ExitStack() as c2:
            sb2 = lambda n, s, d=F32: c2.enter_context(nc.sbuf_tensor(n, s, d))
            keep["tri"] = sb2("tri_sb", [P, 2, P])
            keep["offdiag"] = sb2("offdiag_sb", [P, P])
            keep["maskneg"] = sb2("maskneg_sb", [P, 2, P])
            keep["levels"] = sb2("levels_sb", [P, LEVELS, 2, P])
            tab = sb2("scalar_table", [P, 2, NT, SCW])
            o_rows = sb2("o_rows", [P, 2, NT, 512])
            delta_rows(nc, io, keep)
            delta_scalars(nc, io, keep, tab)
            delta_scan(nc, io, keep, tab, o_rows)
            delta_gate(nc, io, keep, o_rows)
        attention(nc, io, keep)
        merge_and_ffn(nc, io, keep)


def tiles_of(w):
    k, n = w.shape
    return np.ascontiguousarray(w.reshape(k // P, P, n // P, P).transpose(2, 1, 0, 3))


def constants():
    i = np.arange(P)
    tri = (i[:, None] <= i[None, :]).astype(np.float32)
    tri = np.stack([tri, tri.T], 1)
    levels = np.zeros((P, LEVELS, 2, P), np.float32)
    for lv in range(LEVELS):
        s = 2 ** lv
        b = i // s
        low = (b[:, None] // 2 == b[None, :] // 2) & (b[:, None] % 2 == 1) & (b[None, :] % 2 == 0)
        levels[:, lv, 0], levels[:, lv, 1] = low, low.T
    t = np.arange(LAT)
    inv = (np.float32(10000.0) ** (-np.arange(16, dtype=np.float32) / 16)).astype(np.float32)
    ang = np.stack([t // 64, t % 64], 1).astype(np.float32)[:, :, None] * inv
    cos = np.concatenate([np.cos(ang), np.cos(ang)], 2).reshape(LAT, HD)
    sin = np.concatenate([-np.sin(ang), np.sin(ang)], 2).reshape(LAT, HD)
    rope = np.stack([cos, sin], 1).astype(np.float32).reshape(8, P, 2, HD)
    return {
        "ident": np.eye(P, dtype=np.float32),
        "ones": np.ones((P, P), np.float32),
        "tri": tri,
        "offdiag": 1 - np.eye(P, dtype=np.float32),
        "maskneg": (1 - tri) * np.float32(-1e30),
        "levels": levels,
        "rope_tiles": rope,
        "rope_rows": rope.transpose(1, 2, 0, 3),
    }


def laid_out(inp):
    a = {k: np.asarray(v) for k, v in inp.items()}
    w = a["w_in"][0]
    cols = np.concatenate([np.arange(768, 2304), np.arange(0, 768), np.arange(2304, 2816), np.arange(2848, 4896)])
    paired = lambda s: s.reshape(4, 2, HD, HD).transpose(1, 2, 0, 3).reshape(P, 4, HD)
    out = constants() | {
        "x": np.concatenate([a["x_prompt"][0], a["x_sample"][0]], 0),
        "c_t": np.stack([a["c_ctx"].reshape(KT, P).T, a["c"][0].reshape(KT, P).T], -1),
        "w_ada": tiles_of(a["w_ada"][0]),
        "b_ada": a["b_ada"][0].reshape(48, P).T,
        "gains": np.stack([a["norm1_g"][0].reshape(KT, P).T, a["norm2_g"][0].reshape(KT, P).T], 1),
        "w_in": tiles_of(w[:, cols]),
        "w_bg": w[:, 2816:2848].reshape(KT, P, 32).transpose(1, 0, 2),
        "conv_w": a["conv_w"][0].T.reshape(CONV_TILES, P, CONV).transpose(1, 0, 2),
        "decay_params": np.broadcast_to(np.stack([a["a_log"][0].reshape(16), a["dt_bias"][0].reshape(16)]), (P, 2, 16)),
        "dn_g": np.tile(a["dn_norm_g"][0], 2).reshape(P, 1),
        "cache_k": a["cache_k"][0, 0].reshape(PAST, P),
        "cache_v": a["cache_v"][0, 0].reshape(PAST, P),
        "k_gain": np.broadcast_to(a["k_norm_g"][0], (P, HD)),
        "q_gain": np.broadcast_to(a["q_norm_g"][0], (P, HD)),
        "w_mix": np.concatenate([tiles_of(np.concatenate([a["w_pa"][0], a["w_pb"][0]], 0)), tiles_of(a["w_o"][0])], 0),
        "w_up": np.stack([tiles_of(a["w_gate"][0]), tiles_of(a["w_up"][0])], 1).reshape(2 * FT, P, KT, P),
        "w_down": tiles_of(a["w_down"][0]),
        "state_in": np.stack([paired(a["state_fwd"][0, 0]), paired(a["state_bwd"][0, 0])]),
    }
    return {k: np.ascontiguousarray(v) for k, v in out.items()}


SCRATCH = {"conv_t": (CONV_TILES, P, T), "proj_t": (REST_TILES, P, T), "delta_t": (NT, P, TW), "od_t": (4, P, T), "oa_t": (4, P, T)}
RESULTS = {"state_out": (2, P, 4, HD), "new_k": (CTX, P), "new_v": (CTX, P), "y": (T, D)}


def kernel(**inputs):
    import concourse.bacc as bacc
    from concourse.bass_utils import run_bass_kernel_spmd

    nc = bacc.Bacc("TRN2", target_bir_lowering=False, num_devices=1)
    data = laid_out(inputs)
    io = {n: nc.dram_tensor(f"{n}_dram", a.shape, mybir.dt.from_np(a.dtype), kind="ExternalInput").ap() for n, a in data.items()}
    for n, shape in SCRATCH.items():
        io[n] = nc.dram_tensor(n, shape, F32, kind="Internal").ap()
    for n, shape in RESULTS.items():
        io[n] = nc.dram_tensor(f"{n}_out", shape, F32, kind="ExternalOutput").ap()
    build(nc, io)
    res = run_bass_kernel_spmd(nc, [{f"{n}_dram": a for n, a in data.items()}], core_ids=[0]).results[0]
    y = res["y_out"]
    kv = lambda a: a.reshape(1, CTX, 1, 2, HD).transpose(0, 2, 1, 3, 4)
    state = res["state_out_out"].reshape(2, 2, HD, 4, HD).transpose(0, 3, 1, 2, 4).reshape(2, 1, 1, NH, HD, HD)
    return y[None, :CTX], y[None, CTX:], kv(res["new_k_out"]), kv(res["new_v_out"]), state[0], state[1]
```

```python
from contextlib import ExitStack

import numpy as np

import concourse.bass as bass
from concourse import mybir

F32 = mybir.dt.float32
F32R = mybir.dt.float32r
I32 = mybir.dt.int32
ACT = mybir.ActivationFunctionType
ALU = mybir.AluOpType
AX_X = mybir.AxisListType.X

P = 128
D = 1024
KT = D // P
CTX, LAT = 256, 1024
T = CTX + LAT
NT = T // P
GN = 320
NG = T // GN
FF = 2816
FT = FF // P
PAST = 512
HD = 64
NH = 8
CONV = 5
EPS = 1e-6
CONV_TILES = 12
REST_TILES = 26
IN_TILES = CONV_TILES + REST_TILES
ADA1 = 2 * KT
ADA2 = 4 * KT
PADDED = T + 8


def segments(lo, hi):
    out = []
    if lo < CTX:
        out.append((lo, min(hi, CTX), 0))
    if hi > CTX:
        out.append((max(lo, CTX), hi, 1))
    return out


def ada_and_norm(nc, io, keep, h_hi, h_lo):
    with ExitStack() as ctx:
        sb = lambda n, s, d=F32: ctx.enter_context(nc.sbuf_tensor(n, s, d))
        sem = lambda n: ctx.enter_context(nc.semaphore(n))
        x = sb("x_rows", [P, NT, D])
        sq = sb("x_squares", [P, D])
        ss = sb("x_sumsq", [P, 3, NT])
        wa = sb("w_ada_slots", [P, 4, KT, P])
        c_raw = sb("c_raw", [P, KT, 2])
        c_act, b_ada, gains = keep["c_act"], keep["b_ada"], keep["gains"]
        hf = sb("h_f32", [P, 2, T])
        mod_ps = ctx.enter_context(nc.psum_tensor("mod_ps", [P, 512], F32))
        x_ps = [ctx.enter_context(nc.psum_tensor(f"x_ps{i}", [P, 512], F32)) for i in range(6)]
        small_in, c_done = sem("small_in"), sem("c_done")
        x_in = [sem(f"x_in{i}") for i in range(NT)]
        ada_in = [sem(f"ada_in{p}") for p in range(4)]
        ada_done, mod_ready, scale_ready = sem("ada_done"), sem("mod_ready"), sem("scale_ready")
        sumsq_done, rms_step, x_scaled = sem("sumsq_done"), sem("rms_step"), sem("x_scaled")
        xt_ready, hf_ready, hi_ready, lo_ready = sem("xt_ready"), sem("hf_ready"), sem("hi_ready"), sem("lo_ready")
        mod, mod_s = keep["mod"], keep["mod_scale"]
        block = ctx.enter_context(nc.Block())
        TAPS = (0, 4, 8)

        @block.sync
        def _(sp):
            for dst, src in ((c_raw, "c_t"), (b_ada, "b_ada"), (gains, "gains"), (keep["ident"], "ident")):
                sp.dma_start(dst[:], io[src]).then_inc(small_in, 16)
            for t in range(ADA1):
                if t >= 4:
                    sp.wait_ge(ada_done, t - 3)
                sp.dma_start(wa[:, t % 4], io["w_ada"][t]).then_inc(ada_in[t % 4], 16)

        @block.gpsimd
        def _(pool):
            for m in range(KT):
                pool.wait_ge(hi_ready, m + 1)
                nc.gpsimd.tensor_tensor(h_lo[:, m], hf[:, m % 2], h_hi[:, m].bitcast(F32), ALU.subtract).then_inc(lo_ready, 1)

        @block.scalar
        def _(act):
            for j in range(NT):
                act.dma_start(x[:, j], io["x"][j * P:(j + 1) * P, :]).then_inc(x_in[j], 16)
            act.wait_ge(small_in, 64)
            nc.scalar.activation(c_act[:], c_raw[:], ACT.Silu).then_inc(c_done, 1)
            for j in range(NT):
                act.wait_ge(x_in[j], 16)
                if j:
                    act.wait_ge(sumsq_done, j)
                nc.scalar.activation(sq[:], x[:, j], ACT.Square, accum_out=ss[:, 0, j:j + 1]).then_inc(sumsq_done, 1)
            act.wait_ge(rms_step, 1)
            nc.scalar.activation(ss[:, 2], ss[:, 1], ACT.Sqrt).then_inc(rms_step, 1)
            for m in range(KT):
                act.wait_ge(hf_ready, 4 * (m + 1))
                nc.scalar.activation(h_hi[:, m], hf[:, m % 2], ACT.Copy).then_inc(hi_ready, 1)

        @block.tensor
        def _(pe):
            pe.wait_ge(c_done, 1)

            for t in range(ADA1):
                pe.wait_ge(ada_in[t % 4], 16 * (t // 4) + 16)
                for k in range(KT):
                    last = nc.tensor.matmul(mod_ps[:, 2 * t:2 * t + 2], wa[:, t % 4, k], c_act[:, k], start=(k == 0), stop=(k == KT - 1))
                last.then_inc(ada_done, 1)
            for m in range(KT):
                for b, j0 in enumerate(TAPS):
                    n = m * 3 + b
                    if m == 0:
                        pe.wait_ge(x_scaled, min(j0 + 4, NT))
                    if n >= 6:
                        pe.wait_ge(hf_ready, 4 * (m - 1) if b == 0 else 4 * (m - 2) + 2 + b)
                    for j in range(j0, min(j0 + 4, NT)):
                        last = nc.tensor.transpose(x_ps[n % 6][:, (j - j0) * P:(j - j0 + 1) * P], x[:, j, m * P:(m + 1) * P], keep["ident"][:])
                    last.then_inc(xt_ready, 1)

        @block.vector
        def _(dve):
            dve.wait_ge(sumsq_done, NT)
            nc.vector.tensor_scalar(ss[:, 1], ss[:, 0], 1.0 / D, EPS, ALU.mult, ALU.add).then_inc(rms_step, 1)
            dve.wait_ge(rms_step, 2)
            nc.vector.reciprocal(ss[:, 0], ss[:, 2]).then_inc(rms_step, 1)
            dve.wait_ge(rms_step, 3)
            for j in range(NT):
                nc.vector.tensor_scalar(x[:, j], x[:, j], ss[:, 0, j:j + 1], None, ALU.mult).then_inc(x_scaled, 1)
            dve.wait_ge(ada_done, ADA1)
            nc.vector.tensor_tensor(mod[:, 0:ADA1], mod_ps[:, 0:2 * ADA1].rearrange("p (t c) -> p t c", c=2), b_ada[:, 0:ADA1].unsqueeze(2).to_broadcast([P, ADA1, 2]), ALU.add).then_inc(mod_ready, 1)
            dve.wait_ge(mod_ready, 1)
            nc.vector.scalar_tensor_tensor(mod_s[:, 0], mod[:, 8:16], 1.0, gains[:, 0].unsqueeze(2).to_broadcast([P, KT, 2]), ALU.add, ALU.mult).then_inc(scale_ready, 1)
            dve.wait_ge(scale_ready, 1)
            for m in range(KT):
                if m >= 2:
                    dve.wait_ge(lo_ready, m - 1)
                for b, j0 in enumerate(TAPS):
                    dve.wait_ge(xt_ready, m * 3 + b + 1)
                    t0, t1 = j0 * P, min(j0 + 4, NT) * P
                    for lo, hi, seg in segments(t0, t1):
                        nc.vector.tensor_scalar(hf[:, m % 2, lo:hi], x_ps[(m * 3 + b) % 6][:, lo - t0:hi - t0], mod_s[:, 0, m, seg:seg + 1], mod[:, m, seg:seg + 1], ALU.mult, ALU.add).then_inc(hf_ready, 1)


def split_product(nc, out, w_hi, w_lo, a_hi, a_lo, ks, first=True, last=True):
    for n, k in enumerate(ks):
        for q, (w, a) in enumerate(((w_hi, a_hi), (w_hi, a_lo), (w_lo, a_hi))):
            ins = nc.tensor.matmul(out, w(k), a(k), start=(first and n == 0 and q == 0), stop=(last and n == len(ks) - 1 and q == 2))
    return ins


def in_projection(nc, io, keep, h_hi, h_lo):
    with ExitStack() as ctx:
        sb = lambda n, s, d=F32: ctx.enter_context(nc.sbuf_tensor(n, s, d))
        sem = lambda n: ctx.enter_context(nc.semaphore(n))
        raw = sb("w_raw", [P, 2, KT, P])
        whi = sb("w_hi", [P, 2, KT, P], F32R)
        wlo = sb("w_lo", [P, 2, KT, P], F32R)
        bg_raw = sb("bg_raw", [P, KT, 32])
        bg_hi = sb("bg_hi", [P, KT, 32], F32R)
        bg_lo = sb("bg_lo", [P, KT, 32], F32R)
        padded = sb("conv_in", [P, 2, PADDED])
        acc = sb("conv_acc", [P, 2, PADDED - 4])
        stage = sb("proj_stage", [P, 2, PADDED - 4])
        conv_w = sb("conv_w_sb", [P, CONV_TILES, CONV])
        conv_now = sb("conv_w_now", [P, 2, CONV])
        wa = sb("w_ada_pairs", [P, 2, 2, KT, P])
        wc = sb("w_ada_by_c", [P, 2, 2, KT, P])
        ws = sb("w_ada_sums", [P, 2, 2, P])
        ps = [ctx.enter_context(nc.psum_tensor(f"proj_ps{i}", [P, 512], F32)) for i in range(8)]
        mod_ps = [ps[4 * p + 3][:, 512 - ADA2:512] for p in range(2)]
        ada_in = [sem("ada2_in0"), sem("ada2_in1")]
        ada_scaled, ada_summed, ada_done = sem("ada2_scaled"), sem("ada2_summed"), sem("ada2_done")
        mod_ready = sem("mod2_ready")
        w_in = [sem("w_in0"), sem("w_in1")]
        stored = [sem("stored0"), sem("stored1")]
        conv_w_in, bg_split, bg_done, bg_read, pads_zero = sem("conv_w_in"), sem("bg_split"), sem("bg_done"), sem("bg_read"), sem("pads_zero")
        hi_ready, lo_ready, group_done = sem("w_hi_ready"), sem("w_lo_ready"), sem("group_done")
        act_evac, dve_evac = sem("act_evac"), sem("dve_evac")
        conv_tap, silu_done, conv_sc = sem("conv_tap"), sem("silu_done"), sem("conv_sc")
        block = ctx.enter_context(nc.Block())
        bank = lambda p, g: ps[4 * p + g]

        def each_pair(eng, body):
            body(0, True, True, False, None)
            with eng.Fori(1, CONV_TILES // 2) as i:
                body(i, True, False, False, None)
            ada_end = CONV_TILES // 2 + ADA2 // 4
            with eng.Fori(CONV_TILES // 2, ada_end - 1) as i:
                body(i, False, False, False, "more")
            body(ada_end - 1, False, False, False, "last")
            with eng.Fori(CONV_TILES // 2 + ADA2 // 4, IN_TILES // 2 - 1) as i:
                body(i, False, False, False, None)
            body(IN_TILES // 2 - 1, False, False, True, None)

        pair = lambda a: io["w_ada"][bass.ds(ADA1 + 2 * a, 2)].rearrange("u p k n -> p u k n")

        def padded_column(lo):
            return lo + (2 if lo < CTX else 6)

        @block.sync
        def _(sp):
            sp.dma_start(bg_raw[:], io["w_bg"]).then_inc(conv_w_in, 16)
            sp.dma_start(conv_w[:], io["conv_w"]).then_inc(conv_w_in, 16)
            sp.dma_start(keep["ones"][:], io["ones"]).then_inc(conv_w_in, 16)
            for p in range(2):
                sp.dma_start(raw[:, p], io["w_in"][p]).then_inc(w_in[p], 16)

            for a in range(2):
                sp.dma_start(wa[:, a], pair(a)).then_inc(ada_in[a], 16)

            def body(i, conv, first, last, ada):
                for p in range(2):
                    t = 2 * i + p
                    a = t - CONV_TILES
                    if ada == "more":
                        sp.wait_ge(ada_scaled, 4 * a + 4)
                        sp.dma_start(wa[:, p], pair(a + 2)).then_inc(ada_in[p], 16)
                    if not last:
                        sp.wait_ge(lo_ready, t + 1)
                        sp.dma_start(raw[:, p], io["w_in"][bass.ds(t + 2, 1)].rearrange("o p k n -> p (o k) n")).then_inc(w_in[p], 16)
                    if conv:
                        sp.wait_ge(silu_done, t + 1)
                        dst = io["conv_t"][bass.ds(t, 1)].rearrange("o p n -> p (o n)")
                        sp.dma_start(dst[:, 0:CTX], stage[:, p, 0:CTX]).then_inc(stored[p], 16)
                        sp.dma_start(dst[:, CTX:T], stage[:, p, CTX + 4:T + 4]).then_inc(stored[p], 16)
                    else:
                        sp.wait_ge(act_evac, 2 * t + 2)
                        sp.wait_ge(dve_evac, 2 * t + 2)
                        dst = io["proj_t"][bass.ds(t - CONV_TILES, 1)].rearrange("o p n -> p (o n)")
                        sp.dma_start(dst[:, 0:CTX], stage[:, p, 0:CTX]).then_inc(stored[p], 16)
                        sp.dma_start(dst[:, CTX:T], stage[:, p, CTX:T]).then_inc(stored[p], 16)

            each_pair(sp, body)
            sp.wait_ge(stored[0], 32 * (IN_TILES // 2))
            sp.wait_ge(stored[1], 32 * (IN_TILES // 2))

        def evacuate(copy, mine, p, conv, done):
            for g in mine:
                pieces = segments(g * GN, (g + 1) * GN) if conv else [(g * GN, (g + 1) * GN, 0)]
                for lo, hi, _ in pieces:
                    at = padded_column(lo) if conv else lo
                    dst = padded if conv else stage
                    ins = copy(dst[:, p, at:at + hi - lo], bank(p, g)[:, lo - g * GN:hi - g * GN])
                ins.then_inc(done, 1)

        @block.gpsimd
        def _(pool):
            for p in range(2):
                nc.gpsimd.memset(padded[:, p, 0:2], 0.0).then_inc(pads_zero, 1)
                nc.gpsimd.memset(padded[:, p, CTX + 2:CTX + 6], 0.0).then_inc(pads_zero, 1)
                nc.gpsimd.memset(padded[:, p, T + 6:T + 8], 0.0).then_inc(pads_zero, 1)

            def scale(i, first):
                for p in range(2):
                    a = 2 * i + p
                    pool.wait_ge(ada_in[p], 16 * i + 16)
                    if not (first and p == 0):
                        pool.wait_ge(ada_summed, a)
                    for u in range(2):
                        for c in range(2):
                            nc.gpsimd.tensor_tensor(wc[:, u, c], wa[:, p, u], keep["c_act"][:, :, c].unsqueeze(2).to_broadcast([P, KT, P]), ALU.mult).then_inc(ada_scaled, 1)

            scale(0, True)
            with pool.Fori(1, ADA2 // 4) as i:
                scale(i, False)

        @block.scalar
        def _(act):
            act.wait_ge(conv_w_in, 48)
            nc.scalar.activation(bg_hi[:], bg_raw[:], ACT.Copy).then_inc(bg_split, 1)

            def split_hi(t, p, i, wait=True):
                act.wait_ge(w_in[p], 16 * i + 16)
                if wait:
                    act.wait_ge(group_done, 4 * t - 4)
                nc.scalar.activation(whi[:, p], raw[:, p], ACT.Copy).then_inc(hi_ready, 1)

            split_hi(0, 0, 0, False)

            def body(i, conv, first, last, ada):
                for p in range(2):
                    t = 2 * i + p
                    if not (last and p):
                        split_hi(t + 1, 1 - p, i + p, not (first and p == 0))
                    for g in (0, 2):
                        act.wait_ge(group_done, 4 * t + g + 1)
                        if conv and not first:
                            act.wait_ge(conv_tap, CONV * (t - 1))
                        if not conv:
                            act.wait_ge(stored[p], 32 * i)
                        evacuate(lambda o, s: nc.scalar.activation(o, s, ACT.Copy), (g,), p, conv, act_evac)
                    if conv:
                        act.wait_ge(conv_tap, CONV * (t + 1))
                        if not first:
                            act.wait_ge(stored[p], 32 * i)
                        nc.scalar.activation(stage[:, p], acc[:, p], ACT.Silu).then_inc(silu_done, 1)

            each_pair(act, body)

        @block.vector
        def _(dve):
            dve.wait_ge(bg_split, 1)
            nc.vector.tensor_tensor(bg_lo[:], bg_raw[:], bg_hi[:].bitcast(F32), ALU.subtract).then_inc(bg_split, 1)

            def split_lo(t, p, wait=True):
                dve.wait_ge(hi_ready, t + 1)
                if wait:
                    dve.wait_ge(group_done, 4 * t - 4)
                nc.vector.tensor_tensor(wlo[:, p], raw[:, p], whi[:, p].bitcast(F32), ALU.subtract).then_inc(lo_ready, 1)

            split_lo(0, 0, False)
            dve.wait_ge(bg_done, 1)
            nc.vector.tensor_copy(keep["bg"][:], ps[7][:, 0:NT * 32].rearrange("p (j n) -> p j n", n=32)).then_inc(bg_read, 1)
            dve.wait_ge(pads_zero, 6)

            def body(i, conv, first, last, ada):
                for p in range(2):
                    t = 2 * i + p
                    if not (last and p):
                        split_lo(t + 1, 1 - p, not (first and p == 0))
                    if ada:
                        a = t - CONV_TILES
                        dve.wait_ge(ada_scaled, 4 * a + 4)
                        for u in range(2):
                            ins = nc.vector.tensor_reduce(ws[:, u], wc[:, u].rearrange("p c k n -> p c n k"), AX_X, ALU.add)
                        ins.then_inc(ada_summed, 1)
                    for g in (1, 3):
                        dve.wait_ge(group_done, 4 * t + g + 1)
                        if conv and not first:
                            dve.wait_ge(conv_tap, CONV * (t - 1))
                        if not conv:
                            dve.wait_ge(stored[p], 32 * i)
                        evacuate(nc.vector.tensor_copy, (g,), p, conv, dve_evac)
                    if conv:
                        dve.wait_ge(act_evac, 2 * t + 2)
                        dve.wait_ge(dve_evac, 2 * t + 2)
                        if not first:
                            dve.wait_ge(silu_done, t - 1)
                        for c in range(CONV):
                            src = padded[:, p, c:c + PADDED - 4]
                            w = conv_now[:, p, c:c + 1]
                            if c == 0:
                                nc.vector.tensor_copy(conv_now[:, p], conv_w[:, bass.ds(t, 1)].rearrange("p o c -> p (o c)")).then_inc(conv_sc, 1)
                                dve.wait_ge(conv_sc, t + 1)
                                nc.vector.tensor_scalar(acc[:, p], src, w, None, ALU.mult).then_inc(conv_tap, 1)
                            else:
                                dve.wait_ge(conv_tap, CONV * t + c)
                                nc.vector.scalar_tensor_tensor(acc[:, p], src, w, acc[:, p], ALU.mult, ALU.add).then_inc(conv_tap, 1)

            each_pair(dve, body)
            dve.wait_ge(ada_done, ADA2 // 2)
            mod = keep["mod"]
            for p in range(2):
                of_slot = lambda a: a.rearrange("p (i s u) -> p i s u", s=2, u=2)[:, :, p]
                dst = mod[:, ADA1:].rearrange("p (i s u) c -> p i s u c", s=2, u=2)[:, :, p]
                nc.vector.tensor_tensor(dst, mod_ps[p].rearrange("p (i u c) -> p i u c", u=2, c=2), of_slot(keep["b_ada"][:, ADA1:]).unsqueeze(3).to_broadcast([P, ADA2 // 4, 2, 2]), ALU.add).then_inc(mod_ready, 1)
            dve.wait_ge(mod_ready, 2)
            nc.vector.scalar_tensor_tensor(keep["mod_scale"][:, 1], mod[:, 32:40], 1.0, keep["gains"][:, 1].unsqueeze(2).to_broadcast([P, KT, 2]), ALU.add, ALU.mult)

        @block.tensor
        def _(pe):
            pe.wait_ge(bg_split, 2)
            for j in range(NT):
                a = lambda part: lambda k: part[:, k, j * P:(j + 1) * P]
                w = lambda part: lambda k: part[:, k]
                last = split_product(nc, ps[7][:, j * 32:(j + 1) * 32], a(h_hi), a(h_lo), w(bg_hi), w(bg_lo), range(KT))
            last.then_inc(bg_done, 1)

            def body(i, conv, first, last, ada):
                for p in range(2):
                    t = 2 * i + p
                    pe.wait_ge(lo_ready, t + 1)
                    for g in range(NG):
                        if not first:
                            pe.wait_ge((act_evac, dve_evac)[g % 2], 2 * t - 3 + g // 2)
                        elif p == 1 and g == 3:
                            pe.wait_ge(bg_read, 1)
                        if ada and g == 3:
                            pe.wait_ge(ada_summed, t - CONV_TILES + 1)
                            for u in range(2):
                                for c in range(2):
                                    ins = nc.tensor.matmul(mod_ps[p][:, bass.ds(4 * (i - CONV_TILES // 2) + 2 * u + c, 1)], ws[:, u, c], keep["ones"][:, 0:1], start=True, stop=True)
                            ins.then_inc(ada_done, 1)
                        split_product(nc, bank(p, g)[:, 0:GN], lambda k: whi[:, p, k], lambda k: wlo[:, p, k],
                                      lambda k: h_hi[:, k, g * GN:(g + 1) * GN], lambda k: h_lo[:, k, g * GN:(g + 1) * GN],
                                      range(KT)).then_inc(group_done, 1)

            each_pair(pe, body)


LEVELS = 7
TW = 2048
SCW = 52
G_AT, NEGB_AT, BETA_AT, EG_AT, EGLG_AT, GATE_AT, EGL_AT = 0, 8, 16, 24, 32, 40, 48


def delta_rows(nc, io, keep):
    with ExitStack() as ctx:
        sb = lambda n, s, d=F32: ctx.enter_context(nc.sbuf_tensor(n, s, d))
        sem = lambda n: ctx.enter_context(nc.semaphore(n))
        cin = sb("conv_tile", [P, 2, CONV_TILES, P])
        sq = sb("qk_squares", [P, 2, 1024])
        ss = sb("qk_sumsq", [P, 2, 3, 16])
        qn = sb("q_rows", [P, 2, 512])
        tile = sb("delta_tile", [P, 2, TW])
        row_ps = [[ctx.enter_context(nc.psum_tensor(f"row_ps{p}{n}", [P, 512], F32)) for n in range(3)] for p in range(2)]
        col_ps = [ctx.enter_context(nc.psum_tensor(f"col_ps{n}", [P, 512], F32)) for n in range(2)]
        tile_in = [sem("tile_in0"), sem("tile_in1")]
        stored = [sem("tile_stored0"), sem("tile_stored1")]
        rows_done, squared, summed, rooted, inverse, rows_scaled, v_rows, cols_done, cols_out = (
            sem(n) for n in ("rows_done", "squared", "summed", "rooted", "inverse", "rows_scaled", "v_rows", "cols_done", "cols_out"))
        block = ctx.enter_context(nc.Block())

        def each_pair(eng, body):
            body(0, True)
            with eng.Fori(1, NT // 2) as i:
                body(i, False)

        @block.sync
        def _(sp):
            def body(i, first):
                for p in range(2):
                    j = 2 * i + p
                    if not first:
                        sp.wait_ge(rows_done, j - 1)
                    sp.dma_start(cin[:, p], io["conv_t"][:, :, bass.ds(j * P, P)].rearrange("m p n -> p m n")).then_inc(tile_in[p], 16)
            each_pair(sp, body)

        @block.tensor
        def _(pe):
            def rows(i, p, first):
                pe.wait_ge(tile_in[p], 16 * i + 16)
                if not first:
                    pe.wait_ge(rows_scaled, 2 * (2 * i + p) - 2)
                    pe.wait_ge(v_rows, 2 * i + p - 1)
                for m in range(CONV_TILES):
                    last = nc.tensor.transpose(row_ps[p][m // 4][:, (m % 4) * P:(m % 4 + 1) * P], cin[:, p, m], keep["ident"][:])
                last.then_inc(rows_done, 1)

            def cols(i, p, first):
                j = 2 * i + p
                for n in range(2):
                    pe.wait_ge(rows_scaled, 2 * j + n + 1)
                    if not (first and p == 0):
                        pe.wait_ge(cols_out, 2 * j + n - 1)
                    for m in range(4):
                        src = qn[:, p, m * P:(m + 1) * P] if n == 0 else tile[:, p, m * P:(m + 1) * P]
                        last = nc.tensor.transpose(col_ps[n][:, m * P:(m + 1) * P], src, keep["ident"][:])
                    last.then_inc(cols_done, 1)

            def body(i, first):
                rows(i, 0, first)
                rows(i, 1, first)
                cols(i, 0, first)
                cols(i, 1, first)
            each_pair(pe, body)

        @block.scalar
        def _(act):
            def body(i, first):
                for p in range(2):
                    j = 2 * i + p
                    act.wait_ge(rows_done, j + 1)
                    if not first:
                        act.wait_ge(summed, 3 * j - 3)
                        act.wait_ge(stored[p], 16 * i)
                    for n in range(2):
                        nc.scalar.activation(sq[:, p, n * 512:(n + 1) * 512], row_ps[p][n][:], ACT.Square).then_inc(squared, 1)
                    nc.scalar.activation(tile[:, p, 512:1024], row_ps[p][2][:], ACT.Copy).then_inc(v_rows, 1)
                    act.wait_ge(summed, 3 * j + 3)
                    nc.scalar.activation(ss[:, p, 1], ss[:, p, 0], ACT.Sqrt).then_inc(rooted, 1)
                for p in range(2):
                    for n in range(2):
                        act.wait_ge(cols_done, 2 * (2 * i + p) + n + 1)
                        nc.scalar.activation(tile[:, p, 1024 + 512 * n:1536 + 512 * n], col_ps[n][:], ACT.Copy).then_inc(cols_out, 1)
                    act.wait_ge(cols_out, 2 * (2 * i + p) + 2)
                    act.wait_ge(rows_scaled, 2 * (2 * i + p) + 2)
                    act.dma_start(io["delta_t"][bass.ds(2 * i + p, 1)].rearrange("o p n -> p (o n)"), tile[:, p]).then_inc(stored[p], 16)
            each_pair(act, body)
            for p in range(2):
                act.wait_ge(stored[p], 16 * (NT // 2))

        @block.vector
        def _(dve):
            def body(i, first):
                for p in range(2):
                    j = 2 * i + p
                    dve.wait_ge(squared, 2 * j + 2)
                    nc.vector.tensor_reduce(ss[:, p, 2], sq[:, p].rearrange("p (h d) -> p h d", d=HD), AX_X, ALU.add).then_inc(summed, 1)
                    dve.wait_ge(summed, 3 * j + 1)
                    nc.vector.tensor_scalar(ss[:, p, 0, 0:8], ss[:, p, 2, 0:8], EPS, float(HD), ALU.add, ALU.mult).then_inc(summed, 1)
                    nc.vector.tensor_scalar(ss[:, p, 0, 8:16], ss[:, p, 2, 8:16], EPS, None, ALU.add).then_inc(summed, 1)
                for p in range(2):
                    j = 2 * i + p
                    dve.wait_ge(rooted, j + 1)
                    nc.vector.reciprocal(ss[:, p, 2], ss[:, p, 1]).then_inc(inverse, 1)
                    dve.wait_ge(inverse, j + 1)
                    if not first:
                        dve.wait_ge(cols_done, 2 * j - 2)
                    for n, dst in enumerate((qn[:, p], tile[:, p, 0:512])):
                        nc.vector.tensor_tensor(dst.rearrange("p (h d) -> p h d", d=HD), row_ps[p][n][:].rearrange("p (h d) -> p h d", d=HD),
                                                ss[:, p, 2, 8 * n:8 * n + 8].unsqueeze(2).to_broadcast([P, 8, HD]), ALU.mult).then_inc(rows_scaled, 1)
            each_pair(dve, body)


def delta_scalars(nc, io, keep, tab):
    with ExitStack() as ctx:
        sb = lambda n, s, d=F32: ctx.enter_context(nc.sbuf_tensor(n, s, d))
        sem = lambda n: ctx.enter_context(nc.semaphore(n))
        z, az, sp_, g, b = (sb(n, [P, NT, 16]) for n in ("alpha_z", "alpha_abs", "softplus", "log_decay", "beta_cols"))
        par = sb("decay_params", [P, 2, 16])
        gl = sb("tile_decay", [P, 2, NT, 8])
        cum_ps = [ctx.enter_context(nc.psum_tensor(f"cum_ps{n}", [P, 512], F32)) for n in range(2)]
        par_in, a_step, v_step, cum_done = sem("par_in"), sem("scalar_step"), sem("vector_step"), sem("cum_done")
        block = ctx.enter_context(nc.Block())
        bg = keep["bg"]
        per_tile = lambda a, w: a.unsqueeze(1).to_broadcast([P, NT, w])
        col = lambda d, at, n=8: tab[:, d, :, at:at + n]

        @block.sync
        def _(sp):
            sp.dma_start(par[:], io["decay_params"]).then_inc(par_in, 16)
            for name in ("tri", "offdiag", "maskneg", "levels"):
                sp.dma_start(keep[name][:], io[name]).then_inc(par_in, 16)
            sp.wait_ge(par_in, 80)

        @block.scalar
        def _(act):
            act.wait_ge(par_in, 80)
            nc.scalar.activation(b[:], bg[:, :, 0:16], ACT.Exp, scale=-1.0).then_inc(a_step, 1)
            act.wait_ge(v_step, 1)
            nc.scalar.activation(az[:], z[:], ACT.Abs).then_inc(a_step, 1)
            act.wait_ge(a_step, 2)
            nc.scalar.activation(sp_[:], az[:], ACT.Exp, scale=-1.0).then_inc(a_step, 1)
            nc.scalar.activation(par[:, 0], par[:, 0], ACT.Exp).then_inc(a_step, 1)
            act.wait_ge(v_step, 3)
            nc.scalar.activation(az[:], sp_[:], ACT.Ln).then_inc(a_step, 1)
            act.wait_ge(v_step, 15)
            for d in range(2):
                nc.scalar.activation(col(d, EG_AT), col(d, G_AT), ACT.Exp).then_inc(a_step, 1)
                nc.scalar.activation(col(d, EGLG_AT), col(d, EGLG_AT), ACT.Exp).then_inc(a_step, 1)
                nc.scalar.activation(col(d, EGL_AT, 4), col(d, EGL_AT, 4), ACT.Exp).then_inc(a_step, 1)

        @block.vector
        def _(dve):
            n = [0]

            def step(ins, wait=True):
                n[0] += 1
                ins.then_inc(v_step, 1)
                if wait:
                    dve.wait_ge(v_step, n[0])

            dve.wait_ge(par_in, 80)
            step(nc.vector.tensor_tensor(z[:], bg[:, :, 16:32], per_tile(par[:, 1], 16), ALU.add))
            dve.wait_ge(a_step, 3)
            step(nc.vector.tensor_scalar(z[:], z[:], 0.0, None, ALU.max))
            step(nc.vector.tensor_scalar(sp_[:], sp_[:], 1.0, None, ALU.add))
            dve.wait_ge(a_step, 5)
            step(nc.vector.tensor_tensor(z[:], z[:], az[:], ALU.add))
            step(nc.vector.scalar_tensor_tensor(g[:], z[:], -1.0, per_tile(par[:, 0], 16), ALU.mult, ALU.mult))
            step(nc.vector.tensor_scalar(b[:], b[:], 1.0, None, ALU.add))
            step(nc.vector.reciprocal(b[:], b[:]))
            for d in range(2):
                dve.wait_ge(cum_done, d + 1)
                ps = cum_ps[d][:, 0:160].rearrange("p (a j h) -> p a j h", a=2, h=8)
                step(nc.vector.tensor_copy(col(d, G_AT), ps[:, 0]))
                step(nc.vector.tensor_copy(gl[:, d], ps[:, 1]))
                step(nc.vector.tensor_tensor(col(d, EGLG_AT), gl[:, d], col(d, G_AT), ALU.subtract), False)
                pairs = gl[:, d].rearrange("p j (m e) -> p j m e", e=2)
                for e in range(2):
                    half = slice(64 * e, 64 * e + 64)
                    ins = nc.vector.tensor_copy(tab[half, d, :, EGL_AT:EGL_AT + 4], pairs[half, :, :, e])
                nc.vector.tensor_copy(col(d, BETA_AT), b[:, :, 8 * d:8 * d + 8])
                nc.vector.tensor_scalar(col(d, NEGB_AT), b[:, :, 8 * d:8 * d + 8], -1.0, None, ALU.mult)
                step(nc.vector.tensor_copy(col(d, GATE_AT), g[:, :, 8 * d:8 * d + 8]), False)
            assert n[0] == 15

        @block.tensor
        def _(pe):
            pe.wait_ge(v_step, 5)
            for d in range(2):
                ps = cum_ps[d][:, 0:160].rearrange("p (a j h) -> p a j h", a=2, h=8)
                nc.tensor.matmul(ps[:, 0], keep["tri"][:, d], g[:, :, 8 * d:8 * d + 8], start=True, stop=True)
                nc.tensor.matmul(ps[:, 1], keep["ones"][:], g[:, :, 8 * d:8 * d + 8], start=True, stop=True).then_inc(cum_done, 1)


def delta_scan(nc, io, keep, tab, o_rows):
    with ExitStack() as ctx:
        sb = lambda n, s, d=F32: ctx.enter_context(nc.sbuf_tensor(n, s, d))
        sem = lambda n: ctx.enter_context(nc.semaphore(n))
        H4 = 4
        tin = sb("delta_in", [P, 2, 2, TW])
        sc = sb("step_scalars", [P, 2, 2, SCW])
        DT = sb("decay_t", [P, 4, H4, P])
        tri_g = DO = NTf = sb("n_t", [P, 4, H4, P])
        NTr = sb("n_t_r", [P, 4, H4, P], F32R)
        NTl = sb("n_t_lo", [P, 4, H4, P], F32R)
        NM = sb("n_t_level", [P, 4, H4, P], F32R)
        XX = sb("x_inv", [P, 4, 2, H4, P], F32R)
        X, XT = XX[:, :, 0], XX[:, :, 1]
        Y = sb("y_res", [P, 4, H4, P], F32R)
        AT = sb("attn_t", [P, 2, 4, H4, P])
        WT = sb("w_t", [P, 2, 4, H4, P])
        eyes = sb("eyes", [P, 2, P], F32R)
        spare = sb("spare", [P, 4])
        S = sb("state", [P, 2, 4, 2, HD])
        Sd = sb("state_decayed", [P, 2, 4, 2, HD])
        blocks = lambda a, d: [(half(h), a[half(h), d, :, h]) for h in range(2)]
        vn, kd, t1 = (sb(n, [P, 2, NH, HD]) for n in ("v_new", "k_decayed", "scan_tmp"))
        r = t1
        bk = {n: [ctx.enter_context(nc.psum_tensor(f"bank_{n}{e}", [P, 512], F32)) for e in range(2)] for n in "AS"}
        BC = [ctx.enter_context(nc.psum_tensor(f"banks_bc{e}", [P, 2, 512], F32)) for e in range(2)]
        bk["B"], bk["C"] = [b[:, 0] for b in BC], [b[:, 1] for b in BC]
        names = ("scalars tri_ready row_ps arg_ready decay_ready off_ready qk_ps n_ready at_ready nr_ready nl_ready "
                 "nm_ready x_first y_ps y_ready z_ps x_ready r_ps r_ready xr_ps w_ready "
                 "ks_ps v_minus_ready kd_ready sd_ready wr_ps vn_ready qs_ps qs_ready av_ps o_ready st_ps s_ready eyes_ready "
                 "zeroed kept_out state_in").split()
        e = {n: sem("d_" + n) for n in names}
        tile_in = [[sem(f"d_in{p}{d}") for d in range(2)] for p in range(2)]
        block = ctx.enter_context(nc.Block())
        pairs = lambda d: bk["S"][d][:].rearrange("p (m i) -> p m i", m=4)
        kq = lambda q: [BC[q % 2][:, m // 2, (m % 2) * 256:(m % 2) * 256 + 256].rearrange("p (t i) -> p t i", t=2) for m in range(4)]
        bank = lambda n, q: bk[n][q % 2][:].rearrange("p (h i) -> p h i", h=4)
        hb = lambda n, d: bk[n][d][:].rearrange("p (h i) -> p h i", h=NH)
        idn = lambda a: a.unsqueeze(1).to_broadcast([P, H4, P])
        mask_t = lambda lv, d: keep["levels"][:, lv, 1 - d]
        half = lambda h: slice(64 * (h % 2), 64 * (h % 2) + 64)
        heads = lambda q: range(q % 2, NH, 2)
        PIECES = 5

        def steps(eng, body, recur=None):
            for p in range(2):
                body(p, p, p, 1 - p, True)
            with eng.Fori(1, NT // 2) as i:
                for p in range(2):
                    body(2 * i + p, p, 2 * i + p, NT + 1 - (2 * i + p), False)
            if recur:
                for c in range(PIECES):
                    recur(NT - 1, 1, c)

        @block.sync
        def _(sp):
            def load(p, d, tile):
                sp.dma_start(tin[:, p, d], io["delta_t"][bass.ds(tile, 1)].rearrange("o p n -> p (o n)")).then_inc(tile_in[p][d], 16)

            for p in range(2):
                load(p, 0, p)
                load(p, 1, 1 - p)
            sp.wait_ge(e["s_ready"], 2)
            for d in range(2):
                load(0, d, (2, NT - 1)[d])
            sp.wait_ge(e["s_ready"], 4)
            for d in range(2):
                for rows, s in blocks(S, d):
                    sp.dma_start(io["state_out"][d, rows], s).then_inc(e["kept_out"], 16)
            for d in range(2):
                load(1, d, (3, NT - 2)[d])
            sp.wait_ge(e["kept_out"], 64)
            for d in range(2):
                for rows, s in blocks(S, d):
                    sp.dma_start(s, io["state_in"][d, rows]).then_inc(e["state_in"], 16)
            with sp.Fori(1, NT // 2 - 1) as i:
                for p in range(2):
                    sp.wait_ge(e["s_ready"], 2 * (2 * i + p) + 2)
                    load(p, 0, 2 * i + p + 2)
                    load(p, 1, NT - 1 - (2 * i + p))

        @block.gpsimd
        def _(pool):
            for d in range(2):
                nc.gpsimd.memset(S[:, d], 0.0).then_inc(e["zeroed"], 1)
            nc.gpsimd.tensor_copy(eyes[:, 0], keep["ident"][:]).then_inc(e["eyes_ready"], 1)
            nc.gpsimd.tensor_scalar(eyes[:, 1], keep["ident"][:], -1.0, None, ALU.mult).then_inc(e["eyes_ready"], 1)
            pool.wait_ge(e["zeroed"], 2)

            def decayed(k, p, ctxt):
                for d in range(2):
                    pool.wait_ge(tile_in[p][d], 16 * ((k - p) // 2) + 16 if ctxt else 8 * (k - p) + 16)
                    if not (isinstance(k, int) and k == 0):
                        pool.wait_ge(e["s_ready"], 2 * k)
                    nc.gpsimd.tensor_tensor(kd[:, d], tin[:, p, d, 0:512].rearrange("p (h i) -> p h i", h=NH),
                                            sc[:, p, d, EGLG_AT:EGLG_AT + 8].unsqueeze(2).to_broadcast([P, NH, HD]), ALU.mult).then_inc(e["kd_ready"], 1)
                    if not ctxt and p == 0:
                        pool.wait_ge(e["state_in"], 64)
                    flat = lambda a: a[:, d].rearrange("p m h i -> p m (h i)")
                    nc.gpsimd.tensor_tensor(flat(Sd), flat(S), sc[:, p, d, EGL_AT:EGL_AT + 4].unsqueeze(2).to_broadcast([P, 4, 2 * HD]), ALU.mult).then_inc(e["sd_ready"], 1)

            def body(n, p, tf, tb, ctxt):
                L, LY = LEVELS * n * 4, (LEVELS - 1) * n * 4
                pool.wait_ge(e["scalars"], n + 1)
                for q in range(4):
                    d, par = q // 2, q % 2
                    nc.gpsimd.tensor_tensor(tri_g[:, q], idn(keep["tri"][:, d]),
                                            sc[:, p, d, GATE_AT + par:GATE_AT + 8:2].unsqueeze(2).to_broadcast([P, H4, P]), ALU.mult).then_inc(e["tri_ready"], 1)
                for q in range(4):
                    pool.wait_ge(e["decay_ready"], 4 * n + q + 1)
                    nc.gpsimd.tensor_tensor(DO[:, q], DT[:, q], idn(keep["offdiag"][:]), ALU.mult).then_inc(e["off_ready"], 1)
                if not (ctxt and p == 0):
                    decayed(n - 1, 1 - p, ctxt)
                for lv in range(LEVELS):
                    for q in range(4):
                        if lv == 0:
                            pool.wait_ge(e["nr_ready"], 4 * n + q + 1)
                        elif lv == 1:
                            pool.wait_ge(e["x_first"], 4 * n + q + 1)
                        else:
                            pool.wait_ge(e["y_ps"], LY + (lv - 2) * 4 + q + 1)
                        nc.gpsimd.tensor_tensor(NM[:, q], NTr[:, q].bitcast(F32), idn(mask_t(lv, q // 2)), ALU.mult).then_inc(e["nm_ready"], 1)
            steps(pool, body)
            decayed(NT - 1, 1, False)

        @block.scalar
        def _(act):
            cp = lambda o, s: nc.scalar.activation(o, s, ACT.Copy)

            def body(n, p, tf, tb, ctxt):
                L = LEVELS * n * 4
                if not ctxt:
                    act.wait_ge(e["s_ready"], 2 * n - 2)
                cp(sc[:, p, 0], tab[:, 0, bass.ds(tf, 1)].rearrange("p o n -> p (o n)"))
                cp(sc[:, p, 1], tab[:, 1, bass.ds(tb, 1)].rearrange("p o n -> p (o n)")).then_inc(e["scalars"], 1)
                for q in range(4):
                    act.wait_ge(e["arg_ready"], 4 * n + q + 1)
                    nc.scalar.activation(DT[:, q], DT[:, q], ACT.Exp).then_inc(e["decay_ready"], 1)
                for q in range(4):
                    act.wait_ge(e["n_ready"], 4 * n + q + 1)
                    if not (ctxt and p == 0):
                        act.wait_ge(e["nm_ready"], L)
                    cp(NTr[:, q], NTf[:, q]).then_inc(e["nr_ready"], 1)
                for lv in range(1, LEVELS):
                    for q in range(4):
                        act.wait_ge(e["z_ps"], L + lv * 4 + q + 1)
                        cp(XX[:, q].rearrange("p t h i -> p t (h i)"), BC[q % 2][:]).then_inc(e["x_ready"], 1)
            steps(act, body)

        @block.vector
        def _(dve):
            dve.wait_ge(e["zeroed"], 2)

            def recur(k, p, c):
                rows = lambda d, at: tin[:, p, d, at:at + 512].rearrange("p (h i) -> p h i", h=NH)
                wide = lambda d, at: sc[:, p, d, at:at + 8].unsqueeze(2).to_broadcast([P, NH, HD])
                if c == 0:
                    for d in range(2):
                        dve.wait_ge(e["ks_ps"], 2 * k + d + 1)
                        nc.vector.tensor_tensor(t1[:, d], hb("S", d), wide(d, EG_AT), ALU.mult).then_inc(e["v_minus_ready"], 1)
                    dve.wait_ge(e["v_minus_ready"], 4 * k + 2)
                    for d in range(2):
                        nc.vector.tensor_tensor(r[:, d], rows(d, 512), t1[:, d], ALU.subtract).then_inc(e["v_minus_ready"], 1)
                elif c == 1:
                    for d in range(2):
                        dve.wait_ge(e["wr_ps"], 2 * k + d + 1)
                        nc.vector.tensor_tensor(vn[:, d], hb("S", d), wide(d, BETA_AT), ALU.mult).then_inc(e["vn_ready"], 1)
                elif c == 2:
                    dve.wait_ge(e["v_minus_ready"], 4 * k + 4)
                    for d in range(2):
                        dve.wait_ge(e["qs_ps"], 2 * k + d + 1)
                        nc.vector.tensor_tensor(t1[:, d], hb("S", d), wide(d, EG_AT), ALU.mult).then_inc(e["qs_ready"], 1)
                elif c == 3:
                    for d in range(2):
                        dve.wait_ge(e["av_ps"], 2 * k + d + 1)
                        dve.wait_ge(e["qs_ready"], 2 * k + 2)
                        nc.vector.memset(spare[0:1, 2 * p + d:2 * p + d + 1], 0.0)
                        nc.vector.tensor_tensor(o_rows[:, d, bass.ds(k, 1)].rearrange("p o (h i) -> p (o h) i", h=NH), hb("S", d), t1[:, d], ALU.add).then_inc(e["o_ready"], 1)
                else:
                    for d in range(2):
                        dve.wait_ge(e["st_ps"], 2 * k + d + 1)
                        dve.wait_ge(e["sd_ready"], 2 * k + d + 1)
                        for h, ((rows, s), (_, decayed)) in enumerate(zip(blocks(S, d), blocks(Sd, d))):
                            last = nc.vector.tensor_tensor(s, pairs(d)[rows, :, HD * h:HD * h + HD], decayed, ALU.add)
                        last.then_inc(e["s_ready"], 1)

            def body(n, p, tf, tb, ctxt):
                LY = (LEVELS - 1) * n * 4
                for q in range(4):
                    d = q // 2
                    dve.wait_ge(e["row_ps"], 4 * n + q + 1)
                    for m, h in enumerate(heads(q)):
                        last = nc.vector.scalar_tensor_tensor(DT[:, q, m], bank("A", q)[:, m], sc[:, p, d, G_AT + h:G_AT + h + 1], keep["maskneg"][:, d], ALU.subtract, ALU.add)
                    last.then_inc(e["arg_ready"], 1)
                for q in range(4):
                    d = q // 2
                    dve.wait_ge(e["qk_ps"], 4 * n + q + 1)
                    dve.wait_ge(e["off_ready"], 4 * n + q + 1)
                    for m, h in enumerate(heads(q)):
                        last = nc.vector.scalar_tensor_tensor(NTf[:, q, m], kq(q)[m][:, 1], sc[:, p, d, NEGB_AT + h:NEGB_AT + h + 1], DO[:, q, m], ALU.mult, ALU.mult)
                    last.then_inc(e["n_ready"], 1)
                    qk = BC[q % 2][:].rearrange("p b (m t i) -> p b m t i", m=2, t=2)[:, :, :, 0]
                    grid = lambda a: a.rearrange("p (b m) i -> p b m i", b=2)
                    nc.vector.tensor_tensor(grid(AT[:, p, q]), qk, grid(DT[:, q]), ALU.mult).then_inc(e["at_ready"], 1)
                for q in range(4):
                    dve.wait_ge(e["nr_ready"], 4 * n + q + 1)
                    nc.vector.tensor_tensor(NTl[:, q], NTf[:, q], NTr[:, q].bitcast(F32), ALU.subtract).then_inc(e["nl_ready"], 1)
                for q in range(4):
                    dve.wait_ge(e["nm_ready"], LEVELS * n * 4 + q + 1)
                    nc.vector.tensor_tensor(XT[:, q], NM[:, q].bitcast(F32), idn(keep["ident"][:]), ALU.add)
                    dve.wait_ge(e["z_ps"], LEVELS * n * 4 + q + 1)
                    nc.vector.tensor_tensor(X[:, q], bank("B", q), idn(keep["ident"][:]), ALU.add).then_inc(e["x_first"], 1)
                for lv in range(1, LEVELS):
                    for q in range(4):
                        dve.wait_ge(e["y_ps"], LY + (lv - 1) * 4 + q + 1)
                        nc.vector.tensor_tensor(Y[:, q], bank("A", q), idn(keep["ident"][:]), ALU.add).then_inc(e["y_ready"], 1)
                    if lv <= PIECES and not (ctxt and p == 0):
                        recur(n - 1, 1 - p, lv - 1)
                for q in range(4):
                    dve.wait_ge(e["r_ps"], 4 * n + q + 1)
                    nc.vector.tensor_tensor(Y[:, q], bank("A", q), idn(keep["ident"][:]), ALU.add).then_inc(e["r_ready"], 1)
                for q in range(4):
                    dve.wait_ge(e["xr_ps"], 4 * n + q + 1)
                    nc.vector.tensor_tensor(WT[:, p, q], bank("B", q), XT[:, q].bitcast(F32), ALU.add).then_inc(e["w_ready"], 1)
            steps(dve, body, recur)

        @block.tensor
        def _(pe):
            pe.wait_ge(e["eyes_ready"], 2)
            pe.wait_ge(e["zeroed"], 2)
            mm = lambda o, a, b, st=True, sp_=True: nc.tensor.matmul(o, a, b, start=st, stop=sp_)
            kT = lambda p, d, m: tin[:, p, d, 1536 + m * P:1536 + (m + 1) * P]
            qT = lambda p, d, m: tin[:, p, d, 1024 + m * P:1024 + (m + 1) * P]

            def recur(k, p, c):
                if c in (0, 2):
                    operand, done = ((kT, "ks_ps"), None, (qT, "qs_ps"))[c]
                    if c == 2:
                        pe.wait_ge(e["vn_ready"], 2 * k + 2)
                    elif not (isinstance(k, int) and k == 0):
                        pe.wait_ge(e["s_ready"], 2 * k)
                        if not isinstance(k, int) and p == 0:
                            pe.wait_ge(e["state_in"], 64)
                    for d in range(2):
                        for m in range(4):
                            last = mm(pairs(d)[:, m], operand(p, d, m), S[:, d, m].rearrange("p h i -> p (h i)"))
                        last.then_inc(e[done], 1)
                elif c == 1:
                    for d in range(2):
                        pe.wait_ge(e["v_minus_ready"], 4 * k + 3 + d)
                        pe.wait_ge(e["w_ready"], 4 * k + 4)
                        for h in range(NH):
                            last = mm(hb("S", d)[:, h], WT[:, p, 2 * d + h % 2, h // 2], r[:, d, h])
                        last.then_inc(e["wr_ps"], 1)
                elif c == 3:
                    pe.wait_ge(e["qs_ready"], 2 * k + 2)
                    for d in range(2):
                        for h in range(NH):
                            last = mm(hb("S", d)[:, h], AT[:, p, 2 * d + h % 2, h // 2], vn[:, d, h])
                        last.then_inc(e["av_ps"], 1)
                else:
                    for d in range(2):
                        pe.wait_ge(e["o_ready"], 2 * k + d + 1)
                        pe.wait_ge(e["kd_ready"], 2 * k + d + 1)
                        pair = lambda a, m: a[:, d, 2 * m:2 * m + 2].rearrange("p h i -> p (h i)")
                        for m in range(4):
                            last = mm(pairs(d)[:, m], pair(kd, m), pair(vn, m))
                        last.then_inc(e["st_ps"], 1)

            def body(n, p, tf, tb, ctxt):
                first = ctxt and p == 0
                L, LY = LEVELS * n * 4, (LEVELS - 1) * n * 4
                for q in range(4):
                    pe.wait_ge(e["tri_ready"], 4 * n + q + 1)
                    if q >= 2:
                        pe.wait_ge(e["arg_ready"], 4 * n + q - 1)
                    elif not first:
                        pe.wait_ge(e["r_ready"], 4 * n)
                    mm(bk["A"][q % 2][:], keep["ones"][:], tri_g[:, q].rearrange("p h i -> p (h i)")).then_inc(e["row_ps"], 1)
                for q in range(4):
                    d = q // 2
                    if q % 2 == 0:
                        pe.wait_ge(tile_in[p][d], 16 * ((n - p) // 2) + 16 if ctxt else 8 * (n - p) + 16)
                    if q >= 2:
                        pe.wait_ge(e["at_ready"], 4 * n + q - 1)
                    elif not first:
                        pe.wait_ge(e["w_ready"], 4 * n)
                    for m, h in enumerate(heads(q)):
                        both = tin[half(h), p, d, 1024:2048].rearrange("p (t m i) -> p t m i", t=2, m=4)[:, :, m]
                        last = mm(kq(q)[m], kT(p, d, m)[half(h)], both)
                    last.then_inc(e["qk_ps"], 1)
                for q in range(4):
                    pe.wait_ge(e["nm_ready"], L + q + 1)
                    if q >= 2:
                        pe.wait_ge(e["x_first"], 4 * n + q - 1)
                    else:
                        pe.wait_ge(e["at_ready"], 4 * n + q + 3)
                    for m in range(4):
                        last = mm(bank("B", q)[:, m], NM[:, q, m], eyes[:, 0])
                    last.then_inc(e["z_ps"], 1)
                for lv in range(1, LEVELS):
                    for q in range(4):
                        if lv == 1:
                            pe.wait_ge(e["x_first"], 4 * n + q + 1)
                        else:
                            pe.wait_ge(e["x_ready"], LY + (lv - 2) * 4 + q + 1)
                        pe.wait_ge(e["nm_ready"], L + lv * 4 + q + 1)
                        if lv == 1 and q < 2:
                            pe.wait_ge(e["arg_ready"], 4 * n + q + 3)
                        else:
                            pe.wait_ge(e["y_ready"], LY + (lv - 1) * 4 + q - 1)
                        for m in range(4):
                            last = mm(bank("A", q)[:, m], NM[:, q, m], X[:, q, m])
                        last.then_inc(e["y_ps"], 1)
                    if lv <= PIECES and not first:
                        recur(n - 1, 1 - p, lv - 1)
                    for q in range(4):
                        pe.wait_ge(e["y_ready"], LY + (lv - 1) * 4 + q + 1)
                        if lv == 1 and q < 2:
                            pe.wait_ge(e["x_first"], 4 * n + q + 3)
                        else:
                            pe.wait_ge(e["x_ready"], LY + (lv - 1) * 4 + q - 1)
                        for m in range(4):
                            mm(bank("B", q)[:, m], XT[:, q, m], Y[:, q, m])
                            last = mm(bank("C", q)[:, m], Y[:, q, m], XT[:, q, m])
                        last.then_inc(e["z_ps"], 1)
                for q in range(4):
                    pe.wait_ge(e["x_ready"], LY + (LEVELS - 2) * 4 + q + 1)
                    pe.wait_ge(e["nl_ready"], 4 * n + q + 1)
                    if q >= 2:
                        pe.wait_ge(e["r_ready"], 4 * n + q - 1)
                    else:
                        pe.wait_ge(e["y_ready"], LY + (LEVELS - 1) * 4)
                    mm(bk["A"][q % 2][:], eyes[:, 1], X[:, q].rearrange("p h i -> p (h i)"), True, False)
                    for m in range(4):
                        o = bank("A", q)[:, m]
                        mm(o, NTr[:, q, m], X[:, q, m], False, False)
                        last = mm(o, NTl[:, q, m], X[:, q, m], False, m == 3)
                    last.then_inc(e["r_ps"], 1)
                for q in range(4):
                    pe.wait_ge(e["r_ready"], 4 * n + q + 1)
                    if q >= 2:
                        pe.wait_ge(e["w_ready"], 4 * n + q - 1)
                    else:
                        pe.wait_ge(e["x_ready"], LY + (LEVELS - 1) * 4 - 1 + q)
                    for m in range(4):
                        last = mm(bank("B", q)[:, m], Y[:, q, m], XT[:, q, m])
                    last.then_inc(e["xr_ps"], 1)
            steps(pe, body, recur)


def delta_gate(nc, io, keep, o_rows):
    with ExitStack() as ctx:
        sb = lambda n, s, d=F32: ctx.enter_context(nc.sbuf_tensor(n, s, d))
        sem = lambda n: ctx.enter_context(nc.semaphore(n))
        zt = sb("z_t", [P, 4, T])
        sq = sb("o_squares", [P, 2, 512])
        ss = sb("o_sumsq", [P, 3, NT, NH])
        out = sb("o_gated", [P, 2, 4, P])
        gn = sb("dn_gain", [P, 1])
        ps = [ctx.enter_context(nc.psum_tensor(f"o_ps{n}", [P, 512], F32)) for n in range(4)]
        z_in, z_act, added, squared, summed, small, scaled, turned, gated, stored = (
            sem(n) for n in ("z_in", "z_act", "o_added", "o_squared", "o_summed", "o_small", "o_scaled", "o_turned", "o_gated_s", "o_stored"))
        block = ctx.enter_context(nc.Block())
        of = o_rows[:, 0]

        @block.sync
        def _(sp):
            sp.dma_start(zt[:], io["proj_t"][6:10].rearrange("m p n -> p m n")).then_inc(z_in, 16)
            sp.dma_start(gn[:], io["dn_g"]).then_inc(z_in, 16)
            for j in range(NT):
                sp.wait_ge(gated, j + 1)
                sp.dma_start(io["od_t"][:, :, j * P:(j + 1) * P].rearrange("m p n -> p m n"), out[:, j % 2]).then_inc(stored, 16)
                sp.wait_ge(stored, 16 * (j + 1))

        @block.scalar
        def _(act):
            for j in range(NT):
                act.wait_ge(added, j + 1)
                if j >= 2:
                    act.wait_ge(summed, j - 1)
                nc.scalar.activation(sq[:, j % 2], of[:, j], ACT.Square).then_inc(squared, 1)
            act.wait_ge(small, 1)
            nc.scalar.activation(ss[:, 2], ss[:, 1], ACT.Sqrt).then_inc(small, 1)
            act.wait_ge(z_in, 32)
            for m in range(4):
                nc.scalar.activation(zt[:, m], zt[:, m], ACT.Silu).then_inc(z_act, 1)

        @block.vector
        def _(dve):
            for j in range(NT):
                back = 1 - j if j < 2 else NT + 1 - j
                nc.vector.tensor_tensor(of[:, j], of[:, j], o_rows[:, 1, back], ALU.add).then_inc(added, 1)
            for j in range(NT):
                dve.wait_ge(squared, j + 1)
                nc.vector.tensor_reduce(ss[:, 0, j], sq[:, j % 2].rearrange("p (h d) -> p h d", d=HD), AX_X, ALU.add).then_inc(summed, 1)
            dve.wait_ge(summed, NT)
            nc.vector.tensor_scalar(ss[:, 1], ss[:, 0], 1.0 / HD, EPS, ALU.mult, ALU.add).then_inc(small, 1)
            dve.wait_ge(small, 2)
            nc.vector.reciprocal(ss[:, 0], ss[:, 2]).then_inc(small, 1)
            dve.wait_ge(small, 3)

            def gate(j):
                dve.wait_ge(turned, j + 1)
                if j >= 2:
                    dve.wait_ge(stored, 16 * (j - 1))
                nc.vector.scalar_tensor_tensor(out[:, j % 2], ps[j % 4][:].rearrange("p (m n) -> p m n", m=4), gn[:, 0:1], zt[:, :, j * P:(j + 1) * P], ALU.mult, ALU.mult).then_inc(gated, 1)

            for j in range(NT):
                o = of[:, j].rearrange("p (h d) -> p h d", d=HD)
                nc.vector.tensor_tensor(o, o, ss[:, 0, j].unsqueeze(2).to_broadcast([P, NH, HD]), ALU.mult).then_inc(scaled, 1)
            dve.wait_ge(z_act, 4)
            for j in range(NT):
                gate(j)

        @block.tensor
        def _(pe):
            for j in range(NT):
                pe.wait_ge(scaled, j + 1)
                if j >= 4:
                    pe.wait_ge(gated, j - 3)
                for m in range(4):
                    last = nc.tensor.transpose(ps[j % 4][:, m * P:(m + 1) * P], of[:, j, m * P:(m + 1) * P], keep["ident"][:])
                last.then_inc(turned, 1)


KEYS = CTX + PAST + LAT
KTILES = KEYS // P


def attention_keys(nc, io, keep, K2, Vs):
    with ExitStack() as ctx:
        sb = lambda n, s, d=F32: ctx.enter_context(nc.sbuf_tensor(n, s, d))
        sem = lambda n: ctx.enter_context(nc.semaphore(n))
        kvt = sb("kv_t", [P, 2, T])
        k = sb("k_all", [P, KTILES, P])
        v = sb("v_all", [P, KTILES, P])
        kn = sb("k_normed", [P, NT, P])
        k2 = sb("k_twice", [P, 2, KTILES, P])
        doubled = sem("k_doubled")
        sq = sb("k_squares", [P, NT, P])
        ss = sb("k_sumsq", [P, 3, NT, 2])
        kg = sb("k_gain", [P, HD])
        tab = sb("rope_all", [P, 2, 8, HD])
        k_ps = ctx.enter_context(nc.psum_tensor("k_ps", [P, 1536], F32))
        v_ps = ctx.enter_context(nc.psum_tensor("v_ps", [P, 1536], F32))
        t_ps = [ctx.enter_context(nc.psum_tensor(f"kt_ps{n}", [P, 512], F32)) for n in range(2)]
        loaded, turned, a_step, v_step, kt_done, k_hi, k_lo, cache_out = (
            sem(n) for n in ("kv_in", "kv_turned", "ka_step", "kv_step", "kt_done", "k_hi", "k_lo", "cache_out"))
        block = ctx.enter_context(nc.Block())
        by_head = lambda a: a.rearrange("p j (g d) -> p j g d", g=2)

        @block.gpsimd
        def _(pool):
            nc.gpsimd.sem_clear(range(keep["first_sem"].num + 1, doubled.num))

        @block.sync
        def _(sp):
            sp.dma_start(kvt[:], io["proj_t"][4:6].rearrange("m p n -> p m n")).then_inc(loaded, 16)
            sp.dma_start(k[:, 2:6], io["cache_k"].rearrange("(j p) n -> p j n", p=P)).then_inc(loaded, 16)
            sp.dma_start(v[:, 2:6], io["cache_v"].rearrange("(j p) n -> p j n", p=P)).then_inc(loaded, 16)
            sp.dma_start(kg[:], io["k_gain"]).then_inc(loaded, 16)
            sp.dma_start(tab[:], io["rope_rows"]).then_inc(loaded, 16)
            sp.wait_ge(v_step, 5)
            sp.dma_start(io["new_k"].rearrange("(j p) n -> p j n", p=P), k[:, 0:2]).then_inc(cache_out, 16)
            sp.wait_ge(a_step, 4)
            sp.dma_start(io["new_v"].rearrange("(j p) n -> p j n", p=P), v[:, 0:2]).then_inc(cache_out, 16)
            sp.wait_ge(cache_out, 32)

        @block.tensor
        def _(pe):
            pe.wait_ge(loaded, 80)
            for j in range(NT):
                nc.tensor.transpose(k_ps[:, j * P:(j + 1) * P], kvt[:, 0, j * P:(j + 1) * P], keep["ident"][:])
            for j in range(NT):
                last = nc.tensor.transpose(v_ps[:, j * P:(j + 1) * P], kvt[:, 1, j * P:(j + 1) * P], keep["ident"][:])
            last.then_inc(turned, 1)
            pe.wait_ge(doubled, 2)
            n = 0
            for g in range(2):
                for j0 in range(0, KTILES, 4):
                    if n >= 2:
                        pe.wait_ge(k_lo, n - 1)
                    for j in range(j0, min(j0 + 4, KTILES)):
                        last = nc.tensor.transpose(t_ps[n % 2][:, (j - j0) * P:(j - j0 + 1) * P], k2[:, g, j], keep["ident"][:])
                    last.then_inc(kt_done, 1)
                    n += 1

        @block.scalar
        def _(act):
            cp = lambda o, s: nc.scalar.activation(o, s, ACT.Copy)
            act.wait_ge(turned, 1)
            nc.scalar.activation(sq[:].rearrange("p j n -> p (j n)"), k_ps[:, 0:T], ACT.Square).then_inc(a_step, 1)
            act.wait_ge(v_step, 2)
            nc.scalar.activation(ss[:, 2], ss[:, 1], ACT.Sqrt).then_inc(a_step, 1)
            cp(v[:, 0:2], v_ps[:, 0:CTX].rearrange("p (j n) -> p j n", n=P)).then_inc(a_step, 1)
            cp(v[:, 6:14], v_ps[:, CTX:T].rearrange("p (j n) -> p j n", n=P)).then_inc(a_step, 1)
            act.wait_ge(a_step, 4)
            cp(Vs[:, :, :, 0:HD], by_head(v[:])).then_inc(a_step, 1)
            act.wait_ge(v_step, 12)
            for g in range(2):
                head = k[:, :, g * HD:(g + 1) * HD].unsqueeze(2).to_broadcast([P, KTILES, 2, HD])
                cp(k2[:, g].rearrange("p j (r d) -> p j r d", r=2), head).then_inc(doubled, 1)
            n = 0
            for g in range(2):
                for j0 in range(0, KTILES, 4):
                    w = min(4, KTILES - j0) * P
                    act.wait_ge(kt_done, n + 1)
                    cp(K2[:, g, j0 * P:j0 * P + w], t_ps[n % 2][:, 0:w]).then_inc(k_hi, 1)
                    n += 1

        @block.vector
        def _(dve):
            n = [0]

            def step(ins):
                n[0] += 1
                ins.then_inc(v_step, 1)
                dve.wait_ge(v_step, n[0])

            dve.wait_ge(a_step, 1)
            step(nc.vector.tensor_reduce(ss[:, 0], by_head(sq[:]), AX_X, ALU.add))
            step(nc.vector.tensor_scalar(ss[:, 1], ss[:, 0], 1.0 / HD, EPS, ALU.mult, ALU.add))
            dve.wait_ge(a_step, 2)
            step(nc.vector.reciprocal(ss[:, 0], ss[:, 2]))
            step(nc.vector.tensor_tensor(by_head(kn[:]), k_ps[:, 0:T].rearrange("p (j g d) -> p j g d", g=2, d=HD),
                                         ss[:, 0].unsqueeze(3).to_broadcast([P, NT, 2, HD]), ALU.mult))
            gain = kg[:].unsqueeze(1).unsqueeze(1)
            step(nc.vector.tensor_tensor(by_head(k[:, 0:2]), by_head(kn[:, 0:2]), gain.to_broadcast([P, 2, 2, HD]), ALU.mult))
            step(nc.vector.tensor_tensor(by_head(kn[:, 2:NT]), by_head(kn[:, 2:NT]), gain.to_broadcast([P, 8, 2, HD]), ALU.mult))
            cos = tab[:, 0].unsqueeze(2).to_broadcast([P, 8, 2, HD])
            step(nc.vector.tensor_tensor(by_head(k[:, 6:14]), by_head(kn[:, 2:NT]), cos, ALU.mult))
            for g in range(2):
                for part in range(2):
                    pick = lambda a, at: a.rearrange("p j (x i) -> p j x i", x=2)[:, :, :, at:at + 16]
                    own = lambda a: a[:, :, g * HD:(g + 1) * HD]
                    ins = nc.vector.tensor_tensor(pick(own(sq[:, 2:NT]), 16 * part), pick(own(kn[:, 2:NT]), 16 - 16 * part), pick(tab[:, 1], 16 * part), ALU.mult)
                    step(ins)
            step(nc.vector.tensor_tensor(k[:, 6:14], k[:, 6:14], sq[:, 2:NT], ALU.add))
            dve.wait_ge(a_step, 5)
            step(nc.vector.tensor_tensor(Vs[:, :, :, HD:P], by_head(v[:]), Vs[:, :, :, 0:HD].bitcast(F32), ALU.subtract))
            n = 0
            for g in range(2):
                for j0 in range(0, KTILES, 4):
                    w = min(4, KTILES - j0) * P
                    dve.wait_ge(k_hi, n + 1)
                    low = K2[64:128, g, j0 * P:j0 * P + w]
                    nc.vector.tensor_tensor(low, t_ps[n % 2][64:128, 0:w], low.bitcast(F32), ALU.subtract).then_inc(k_lo, 1)
                    n += 1


def attend(nc, io, keep, K2, Vs, tag, tile0, tiles, nb, w, key0, rotary):
    with ExitStack() as ctx:
        sb = lambda n, s, d=F32: ctx.enter_context(nc.sbuf_tensor(tag + n, s, d))
        sem = lambda n: ctx.enter_context(nc.semaphore(tag + n))
        wt = w // P
        qin = sb("q_t", [P, 4, P])
        rt = sb("rope_tile", [P, 2, HD])
        q1, q2, qt = (sb(n, [P, NH, HD]) for n in ("q1", "q2", "q_tmp"))
        qd = sb("q_twice", [P, NH, P])
        st = sb("q_stats", [P, 4, NH])
        qg = sb("q_gain", [P, HD])
        Qh = sb("q_hi2", [P, NH, P], F32R)
        Ql = sb("q_lo2", [P, NH, P], F32R)
        pr = sb("probs", [P, 2, nb * w])
        pmax = sb("block_max", [P, NH, 3])
        negm = sb("neg_max", [P, NH])
        sums = sb("block_sums", [P, NH, nb])
        rinv = sb("inv_sums", [P, 2, NH])
        PTh = sb("probs_t_hi", [P, 2, nb * wt, 4, P], F32R)
        PTl = sb("probs_t_lo", [P, 2, nb * wt, 4, P], F32R)
        tmp = sb("o_low", [64, 4, P])
        bc = sb("inv_bcast", [64, 4, P])
        u = sb("o_sum", [64, 4, P])
        oT = sb("o_t", [P, 4, P])
        s_ps = [ctx.enter_context(nc.psum_tensor(f"{tag}s_ps{n}", [P, 512], F32)) for n in range(4)]
        t_ps = [ctx.enter_context(nc.psum_tensor(f"{tag}t_ps{n}", [P, 512], F32)) for n in range(2)]
        o_ps = ctx.enter_context(nc.psum_tensor(tag + "o_ps", [P, 512], F32))
        m_ps = ctx.enter_context(nc.psum_tensor(tag + "m_ps", [P, 512], F32))
        names = ("gain_in q_in stored q_rows q_squared q_mean q_root q_step dup_done q_hi q_lo scores_done block_maxed max_ready "
                 "exp_done turned hi_ready lo_ready sums_ready inv_ready pv_done tmp_ready inv_ps inv_copied u_ready out_ready").split()
        e = {n: sem(n) for n in names}
        block = ctx.enter_context(nc.Block())
        QS = 6 if rotary else 2

        def each_tile(eng, body):
            body(0, True)
            with eng.Fori(1, tiles) as n:
                body(n, False)

        def rows_of(n):
            return bass.ds(n * P + tile0 * P, P)

        @block.sync
        def _(sp):
            sp.dma_start(qg[:], io["q_gain"]).then_inc(e["gain_in"], 16)

            def body(n, first):
                if not first:
                    sp.wait_ge(e["q_rows"], n)
                sp.dma_start(qin[:], io["proj_t"][0:4, :, rows_of(n)].rearrange("m p n -> p m n")).then_inc(e["q_in"], 16)
                if rotary:
                    if not first:
                        sp.wait_ge(e["q_step"], QS * n)
                    sp.dma_start(rt[:], io["rope_tiles"][bass.ds(n, 1)].rearrange("o p a d -> p (o a) d")).then_inc(e["q_in"], 16)
                sp.wait_ge(e["out_ready"], 2 * n + 2)
                sp.dma_start(io["oa_t"][:, :, rows_of(n)].rearrange("m p n -> p m n"), oT[:]).then_inc(e["stored"], 16)
            each_tile(sp, body)
            sp.wait_ge(e["stored"], 16 * tiles)

        @block.tensor
        def _(pe):
            def scores(n, h):
                for kb in range(nb):
                    G = nb * h + kb
                    if not (isinstance(n, int) and n == 0 and G < 4):
                        pe.wait_ge(e["exp_done"], nb * NH * n + G - 3)
                    keys = K2[:, h // 4, key0 + kb * w:key0 + (kb + 1) * w]
                    o = s_ps[G % 4][:, 0:w]
                    nc.tensor.matmul(o, Qh[:, h], keys, start=True, stop=False)
                    nc.tensor.matmul(o, Ql[:, h], keys, start=False, stop=True).then_inc(e["scores_done"], 1)

            def turn(n, h, first):
                for c in range(nb):
                    G = nb * h + c
                    pe.wait_ge(e["exp_done"], nb * NH * n + G + 1)
                    if G >= 2:
                        pe.wait_ge(e["lo_ready"], nb * NH * n + G - 1)
                    else:
                        pe.wait_ge(e["q_lo"], 2 * n + G + 1)
                    for b in range(wt):
                        last = nc.tensor.transpose(t_ps[G % 2][:, b * P:(b + 1) * P], pr[:, h % 2, c * w + b * P:c * w + (b + 1) * P], keep["ident"][:])
                    last.then_inc(e["turned"], 1)

            def values(n, g, first):
                pe.wait_ge(e["lo_ready"], nb * NH * n + nb * (4 * g + 4))
                if not (first and g == 0):
                    pe.wait_ge(e["u_ready"], 2 * n + g)
                for kt in range(nb * wt):
                    lhs = Vs[:, key0 // P + kt, g]
                    nc.tensor.matmul(o_ps[:], lhs, PTh[:, g, kt].rearrange("p h q -> p (h q)"), start=(kt == 0), stop=False)
                    last = nc.tensor.matmul(o_ps[:], lhs, PTl[:, g, kt].rearrange("p h q -> p (h q)"), start=False, stop=(kt == nb * wt - 1))
                last.then_inc(e["pv_done"], 1)
                pe.wait_ge(e["inv_ready"], 2 * n + g + 1)
                if not (first and g == 0):
                    pe.wait_ge(e["inv_copied"], 2 * n + g)
                for m in range(4):
                    last = nc.tensor.matmul(m_ps[0:64, m * P:(m + 1) * P], rinv[:, 1, 4 * g + m:4 * g + m + 1].to_broadcast([P, 64]), keep["ident"][:], start=True, stop=True)
                last.then_inc(e["inv_ps"], 1)

            def body(n, first):
                pe.wait_ge(e["q_in"], (32 if rotary else 16) * n + (32 if rotary else 16))
                if not first:
                    pe.wait_ge(e["inv_copied"], 2 * n)
                for m in range(4):
                    last = nc.tensor.transpose(m_ps[:, m * P:(m + 1) * P], qin[:, m], keep["ident"][:])
                last.then_inc(e["q_rows"], 1)
                for c in range(2):
                    pe.wait_ge(e["q_step"], QS * n + QS)
                    if not first:
                        pe.wait_ge(e["lo_ready"], nb * NH * n)
                    for m in range(4):
                        last = nc.tensor.transpose(t_ps[c][:, m * P:(m + 1) * P], qd[:, 4 * c + m], keep["ident"][:])
                    last.then_inc(e["dup_done"], 1)
                pe.wait_ge(e["q_lo"], 2 * n + 2)
                for h in range(NH + 1):
                    if h < NH:
                        scores(n, h)
                    if h:
                        turn(n, h - 1, first)
                    if h == 5:
                        values(n, 0, first)
                values(n, 1, first)
            each_tile(pe, body)

        @block.scalar
        def _(act):
            cp = lambda o, s: nc.scalar.activation(o, s, ACT.Copy)

            def body(n, first):
                act.wait_ge(e["q_rows"], n + 1)
                nc.scalar.activation(qt[:].rearrange("p h d -> p (h d)"), m_ps[:], ACT.Square).then_inc(e["q_squared"], 1)
                act.wait_ge(e["q_mean"], 2 * n + 2)
                nc.scalar.activation(st[:, 2], st[:, 1], ACT.Ln).then_inc(e["q_root"], 1)
                act.wait_ge(e["q_root"], 2 * n + 1)
                nc.scalar.activation(st[:, 3], st[:, 2], ACT.Exp, scale=-0.5).then_inc(e["q_root"], 1)
                for c in range(2):
                    act.wait_ge(e["dup_done"], 2 * n + c + 1)
                    cp(Qh[:, 4 * c:4 * c + 4].rearrange("p h n -> p (h n)"), t_ps[c][:]).then_inc(e["q_hi"], 1)

                def finish(g):
                    act.wait_ge(e["pv_done"], 2 * n + g + 1)
                    if not (first and g == 0):
                        act.wait_ge(e["u_ready"], 2 * n + g)
                    cp(tmp[:].rearrange("p h q -> p (h q)"), o_ps[64:128, :]).then_inc(e["tmp_ready"], 1)
                    act.wait_ge(e["inv_ps"], 2 * n + g + 1)
                    if not (first and g == 0):
                        act.wait_ge(e["out_ready"], 2 * n + g)
                    cp(bc[:].rearrange("p h q -> p (h q)"), m_ps[0:64, :]).then_inc(e["inv_copied"], 1)

                for h in range(NH + 1):
                    if h < NH:
                        act.wait_ge(e["max_ready"], NH * n + h + 1)
                        if not (first and h < 2):
                            act.wait_ge(e["turned"], nb * (NH * n + h - 1))
                        for kb in range(nb):
                            G = nb * h + kb
                            nc.scalar.activation(pr[:, h % 2, kb * w:(kb + 1) * w], s_ps[G % 4][:, 0:w], ACT.Exp, bias=negm[:, h:h + 1],
                                                 accum_out=sums[:, h, kb:kb + 1]).then_inc(e["exp_done"], 1)
                    if h:
                        g, hh = (h - 1) // 4, (h - 1) % 4
                        if not first:
                            act.wait_ge(e["pv_done"], 2 * n - 1 + g)
                        for c in range(nb):
                            G = nb * (h - 1) + c
                            act.wait_ge(e["turned"], nb * NH * n + G + 1)
                            cp(PTh[:, g, c * wt:(c + 1) * wt, hh], t_ps[G % 2][:, 0:w].rearrange("p (b q) -> p b q", b=wt)).then_inc(e["hi_ready"], 1)
                    if h == 6:
                        finish(0)
                finish(1)
            each_tile(act, body)

        @block.vector
        def _(dve):
            dve.wait_ge(e["gain_in"], 16)
            over_heads = lambda a: a.unsqueeze(1).to_broadcast([P, NH, HD])

            def body(n, first):
                qs = [0]

                def step(ins, wait=True):
                    qs[0] += 1
                    ins.then_inc(e["q_step"], 1)
                    if wait:
                        dve.wait_ge(e["q_step"], QS * n + qs[0])

                dve.wait_ge(e["q_squared"], n + 1)
                nc.vector.tensor_reduce(st[:, 0], qt[:], AX_X, ALU.add).then_inc(e["q_mean"], 1)
                dve.wait_ge(e["q_mean"], 2 * n + 1)
                nc.vector.tensor_scalar(st[:, 1], st[:, 0], HD * EPS, None, ALU.add).then_inc(e["q_mean"], 1)
                dve.wait_ge(e["q_root"], 2 * n + 2)
                step(nc.vector.tensor_tensor(q1[:], m_ps[:].rearrange("p (h d) -> p h d", d=HD), st[:, 3].unsqueeze(2).to_broadcast([P, NH, HD]), ALU.mult))
                twice = lambda a: a.unsqueeze(2).to_broadcast([P, NH, 2, HD])
                both = qd[:].rearrange("p h (r d) -> p h r d", r=2)
                gained = nc.vector.tensor_tensor(q1[:], q1[:], over_heads(qg[:]), ALU.mult) if rotary else \
                    nc.vector.tensor_tensor(both, twice(q1[:]), qg[:].unsqueeze(1).unsqueeze(1).to_broadcast([P, NH, 2, HD]), ALU.mult)
                step(gained)
                if rotary:
                    dve.wait_ge(e["q_in"], 32 * n + 32)
                    step(nc.vector.tensor_tensor(q2[:], q1[:], over_heads(rt[:, 0]), ALU.mult), False)
                    pick = lambda a, at: a.rearrange("p h (x i) -> p h x i", x=2)[:, :, :, at:at + 16]
                    for part in range(2):
                        sin = rt[:, 1].rearrange("p (x i) -> p x i", x=2)[:, :, 16 * part:16 * part + 16].unsqueeze(1).to_broadcast([P, NH, 2, 16])
                        step(nc.vector.tensor_tensor(pick(qt[:], 16 * part), pick(q1[:], 16 - 16 * part), sin, ALU.mult), part == 1)
                    step(nc.vector.tensor_tensor(both, twice(q2[:]), twice(qt[:]), ALU.add))
                for c in range(2):
                    dve.wait_ge(e["q_hi"], 2 * n + c + 1)
                    nc.vector.tensor_tensor(Ql[:, 4 * c:4 * c + 4].rearrange("p h n -> p (h n)"), t_ps[c][:], Qh[:, 4 * c:4 * c + 4].rearrange("p h n -> p (h n)").bitcast(F32), ALU.subtract).then_inc(e["q_lo"], 1)

                def inverse(g):
                    dve.wait_ge(e["exp_done"], nb * (NH * n + 4 * g + 4))
                    nc.vector.tensor_reduce(rinv[:, 0, 4 * g:4 * g + 4], sums[:, 4 * g:4 * g + 4], AX_X, ALU.add).then_inc(e["sums_ready"], 1)
                    dve.wait_ge(e["sums_ready"], 2 * n + g + 1)
                    nc.vector.reciprocal(rinv[:, 1, 4 * g:4 * g + 4], rinv[:, 0, 4 * g:4 * g + 4]).then_inc(e["inv_ready"], 1)

                def finish(g):
                    dve.wait_ge(e["tmp_ready"], 2 * n + g + 1)
                    nc.vector.tensor_tensor(u[:].rearrange("p h q -> p (h q)"), o_ps[0:64, :], tmp[:].rearrange("p h q -> p (h q)"), ALU.add).then_inc(e["u_ready"], 1)
                    dve.wait_ge(e["u_ready"], 2 * n + g + 1)
                    dve.wait_ge(e["inv_copied"], 2 * n + g + 1)
                    if not first:
                        dve.wait_ge(e["stored"], 16 * n)
                    for par in range(2):
                        last = nc.vector.tensor_tensor(oT[64 * par:64 * par + 64, 2 * g:2 * g + 2], u[:, par::2], bc[:, par::2], ALU.mult)
                    last.then_inc(e["out_ready"], 1)

                for h in range(NH + 1):
                    if h < NH:
                        for kb in range(nb):
                            G = nb * h + kb
                            dve.wait_ge(e["scores_done"], nb * NH * n + G + 1)
                            nc.vector.tensor_reduce(pmax[:, h, kb:kb + 1], s_ps[G % 4][:, 0:w], AX_X, ALU.max).then_inc(e["block_maxed"], 1)
                        dve.wait_ge(e["block_maxed"], nb * (NH * n + h + 1))
                        nc.vector.tensor_reduce(negm[:, h:h + 1], pmax[:, h, 0:nb], AX_X, ALU.max, negate=True).then_inc(e["max_ready"], 1)
                    if h:
                        g, hh = (h - 1) // 4, (h - 1) % 4
                        for c in range(nb):
                            G = nb * (h - 1) + c
                            dve.wait_ge(e["hi_ready"], nb * NH * n + G + 1)
                            dst = slice(c * wt, (c + 1) * wt)
                            nc.vector.tensor_tensor(PTl[:, g, dst, hh], t_ps[G % 2][:, 0:w].rearrange("p (b q) -> p b q", b=wt), PTh[:, g, dst, hh].bitcast(F32), ALU.subtract).then_inc(e["lo_ready"], 1)
                    if h == 4:
                        inverse(0)
                    if h == 6:
                        finish(0)
                inverse(1)
                finish(1)
            each_tile(dve, body)


def attention(nc, io, keep):
    with ExitStack() as ctx:
        K2 = ctx.enter_context(nc.sbuf_tensor("keys_hi_lo", [P, 2, KEYS], F32R))
        Vs = ctx.enter_context(nc.sbuf_tensor("values_hi_lo", [P, KTILES, 2, P], F32R))
        attention_keys(nc, io, keep, K2, Vs)
        attend(nc, io, keep, K2, Vs, "c_", 0, 2, 1, CTX, 0, False)
        attend(nc, io, keep, K2, Vs, "l_", 2, 8, 3, 512, CTX, True)


HT = T // 2
HJ = HT // P


def half_segments(half, lo, hi):
    return [(a - half * HT, b - half * HT, s) for a, b, s in segments(half * HT + lo, half * HT + hi)]


def mix_out(nc, io, keep, half, x1, h_hi, h_lo):
    with ExitStack() as ctx:
        tag = f"m{half}_"
        sb = lambda n, s, d=F32: ctx.enter_context(nc.sbuf_tensor(tag + n, s, d))
        sem = lambda n: ctx.enter_context(nc.semaphore(tag + n))
        raw = sb("w_raw", [P, 2, KT, P])
        whi = sb("w_hi", [P, 2, KT, P], F32R)
        wlo = sb("w_lo", [P, 2, KT, P], F32R)
        o_raw = sb("o_raw", [P, KT, HT])
        o_hi = sb("o_hi", [P, KT, HT], F32R)
        o_lo = sb("o_lo", [P, KT, HT], F32R)
        gate = sb("gates", [P, 2, 2, HT])
        rows = sb("x_rows2", [P, HJ, D])
        rstd = sb("rstd", [P, 2, HT])
        ps = [ctx.enter_context(nc.psum_tensor(f"{tag}ps{p}", [P, 4, 512], F32)) for p in range(2)]
        w_in = [sem(f"w_in{p}") for p in range(2)]
        g_in = [sem(f"g_in{p}") for p in range(2)]
        names = ("o_in x_in hi lo o_split o_split_lo done sig weighted summed m_hi m_lo xt_ps xt x1_ready x1_sq total norm scaled h_hi").split()
        e = {n: sem(n) for n in names}
        block = ctx.enter_context(nc.Block())
        N = 2 * KT
        tok = slice(half * HT, (half + 1) * HT)
        mod, mod_s = keep["mod"], keep["mod_scale"]
        cp = lambda o, s: nc.scalar.activation(o, s, ACT.Copy)
        groups = lambda p, a: ps[p][:, a:a + 2, 0:GN]
        two = lambda a: a.rearrange("p (g n) -> p g n", g=2)

        @block.sync
        def _(sp):
            for m in range(4):
                sp.dma_start(o_raw[:, m], io["oa_t"][m, :, tok]).then_inc(e["o_in"], 16)
                sp.dma_start(o_raw[:, 4 + m], io["od_t"][m, :, tok]).then_inc(e["o_in"], 16)
            for t in range(N):
                if t >= 2:
                    sp.wait_ge(e["lo"], t - 1)
                sp.dma_start(raw[:, t % 2], io["w_mix"][t]).then_inc(w_in[t % 2], 16)
                if t < KT:
                    if t >= 2:
                        sp.wait_ge(e["m_lo"], t - 1)
                    sp.dma_start(gate[:, t % 2, 0], io["proj_t"][10 + t, :, tok]).then_inc(g_in[t % 2], 16)
                    sp.dma_start(gate[:, t % 2, 1], io["proj_t"][18 + t, :, tok]).then_inc(g_in[t % 2], 16)

        @block.gpsimd
        def _(pool):
            for t in range(KT):
                pool.wait_ge(e["weighted"], 2 * t + 2)
                nc.gpsimd.tensor_tensor(gate[:, t % 2, 0], gate[:, t % 2, 0], gate[:, t % 2, 1], ALU.add).then_inc(e["summed"], 1)
                pool.wait_ge(e["m_hi"], t + 1)
                nc.gpsimd.tensor_tensor(h_lo[:, t], gate[:, t % 2, 0], h_hi[:, t].bitcast(F32), ALU.subtract).then_inc(e["m_lo"], 1)

        @block.scalar
        def _(act):
            act.dma_start(rows[:], io["x"][tok, :].rearrange("(j p) n -> p j n", p=P)).then_inc(e["x_in"], 16)

            def split_hi(t):
                act.wait_ge(w_in[t % 2], 16 * (t // 2 + 1))
                if t >= 2:
                    act.wait_ge(e["done"], t - 1)
                cp(whi[:, t % 2], raw[:, t % 2]).then_inc(e["hi"], 1)

            split_hi(0)
            act.wait_ge(e["o_in"], 128)
            for k in range(KT):
                cp(o_hi[:, k], o_raw[:, k]).then_inc(e["o_split"], 1)
            for t in range(N):
                if t + 1 < N:
                    split_hi(t + 1)
                if t < KT:
                    act.wait_ge(g_in[t % 2], 32 * (t // 2 + 1))
                    nc.scalar.activation(gate[:, t % 2], gate[:, t % 2], ACT.Sigmoid).then_inc(e["sig"], 1)
                    act.wait_ge(e["summed"], t + 1)
                    cp(h_hi[:, t], gate[:, t % 2, 0]).then_inc(e["m_hi"], 1)
                else:
                    m = t - KT
                    act.wait_ge(e["xt_ps"], m + 1)
                    cp(x1[:, m, 0:512], ps[t % 2][:, 2])
                    cp(x1[:, m, 512:HT], ps[t % 2][:, 3, 0:P]).then_inc(e["xt"], 1)
            for m in range(KT):
                act.wait_ge(e["x1_ready"], m + 1)
                nc.scalar.activation(o_raw[:, m], x1[:, m], ACT.Square).then_inc(e["x1_sq"], 1)
            act.wait_ge(e["norm"], 1)
            nc.scalar.activation(rstd[:, 1], rstd[:, 0], ACT.Sqrt).then_inc(e["norm"], 1)
            for m in range(KT):
                act.wait_ge(e["scaled"], m + 1)
                for lo, hi, seg in half_segments(half, 0, HT):
                    last = nc.scalar.activation(h_hi[:, m, lo:hi], o_raw[:, m, lo:hi], ACT.Identity, bias=mod[:, 24 + m, seg:seg + 1])
                last.then_inc(e["h_hi"], 1)

        @block.vector
        def _(dve):
            def split_lo(t):
                dve.wait_ge(e["hi"], t + 1)
                if t >= 2:
                    dve.wait_ge(e["done"], t - 1)
                nc.vector.tensor_tensor(wlo[:, t % 2], raw[:, t % 2], whi[:, t % 2].bitcast(F32), ALU.subtract).then_inc(e["lo"], 1)

            split_lo(0)
            for k in range(KT):
                dve.wait_ge(e["o_split"], k + 1)
                nc.vector.tensor_tensor(o_lo[:, k], o_raw[:, k], o_hi[:, k].bitcast(F32), ALU.subtract).then_inc(e["o_split_lo"], 1)
            for t in range(N):
                if t + 1 < N:
                    split_lo(t + 1)
                dve.wait_ge(e["done"], t + 1)
                if t < KT:
                    dve.wait_ge(e["sig"], t + 1)
                    for s in range(2):
                        nc.vector.tensor_tensor(two(gate[:, t % 2, s]), groups(t % 2, 2 * s), two(gate[:, t % 2, s]), ALU.mult).then_inc(e["weighted"], 1)
                else:
                    m = t - KT
                    dve.wait_ge(e["xt"], m + 1)
                    for g in range(2):
                        for lo, hi, seg in half_segments(half, g * GN, (g + 1) * GN):
                            last = nc.vector.scalar_tensor_tensor(x1[:, m, lo:hi], ps[t % 2][:, g, lo - g * GN:hi - g * GN], mod[:, 16 + m, seg:seg + 1], x1[:, m, lo:hi], ALU.mult, ALU.add)
                    last.then_inc(e["x1_ready"], 1)
            dve.wait_ge(e["total"], 1)
            nc.vector.tensor_scalar(two(rstd[:, 0]), groups(0, 0), 1.0 / D, EPS, ALU.mult, ALU.add).then_inc(e["norm"], 1)
            dve.wait_ge(e["norm"], 2)
            nc.vector.reciprocal(rstd[:, 0], rstd[:, 1]).then_inc(e["norm"], 1)
            dve.wait_ge(e["norm"], 3)
            for m in range(KT):
                for lo, hi, seg in half_segments(half, 0, HT):
                    last = nc.vector.scalar_tensor_tensor(o_raw[:, m, lo:hi], x1[:, m, lo:hi], mod_s[:, 1, m, seg:seg + 1], rstd[:, 0, lo:hi], ALU.mult, ALU.mult)
                last.then_inc(e["scaled"], 1)
            for m in range(KT):
                dve.wait_ge(e["h_hi"], m + 1)
                for lo, hi, seg in half_segments(half, 0, HT):
                    nc.vector.scalar_tensor_tensor(h_lo[:, m, lo:hi], o_raw[:, m, lo:hi], mod[:, 24 + m, seg:seg + 1], h_hi[:, m, lo:hi].bitcast(F32), ALU.add, ALU.subtract)

        @block.tensor
        def _(pe):
            part = lambda a, g: lambda k: a[:, k, g * GN:(g + 1) * GN]
            w = lambda a, p: lambda k: a[:, p, k]
            pe.wait_ge(e["o_split_lo"], KT)
            for t in range(N):
                p = t % 2
                pe.wait_ge(e["lo"], t + 1)
                if t < KT:
                    if t >= 2:
                        pe.wait_ge(e["weighted"], 2 * t - 2)
                    for s in range(2):
                        for g in range(2):
                            last = split_product(nc, ps[p][:, 2 * s + g, 0:GN], w(whi, p), w(wlo, p), part(o_hi, g), part(o_lo, g), range(4 * s, 4 * s + 4))
                else:
                    m = t - KT
                    if m < 2:
                        pe.wait_ge(e["weighted"], 2 * (t - 2) + 2)
                    else:
                        pe.wait_ge(e["x1_ready"], m - 1)
                    if m == 0:
                        pe.wait_ge(e["x_in"], 16)
                    for j in range(HJ):
                        last = nc.tensor.transpose(ps[p][:, 2 + j // 4, (j % 4) * P:(j % 4 + 1) * P], rows[:, j, m * P:(m + 1) * P], keep["ident"][:])
                    last.then_inc(e["xt_ps"], 1)
                    pe.wait_ge(e["m_lo"], KT)
                    for g in range(2):
                        last = split_product(nc, ps[p][:, g, 0:GN], w(whi, p), w(wlo, p), part(h_hi, g), part(h_lo, g), range(KT))
                last.then_inc(e["done"], 1)
            pe.wait_ge(e["x1_ready"], KT)
            pe.wait_ge(e["x1_sq"], KT)
            for g in range(2):
                for m in range(KT):
                    last = nc.tensor.matmul(ps[0][:, g, 0:GN], keep["ones"][:], o_raw[:, m, g * GN:(g + 1) * GN], start=(m == 0), stop=(m == KT - 1))
            last.then_inc(e["total"], 1)


def feed_forward(nc, io, keep, half, x1, h_hi, h_lo):
    with ExitStack() as ctx:
        tag = f"f{half}_"
        sb = lambda n, s, d=F32: ctx.enter_context(nc.sbuf_tensor(tag + n, s, d))
        sem = lambda n: ctx.enter_context(nc.semaphore(tag + n))
        raw = sb("w_raw", [P, 2, KT, P])
        whi = sb("w_hi", [P, 2, KT, P], F32R)
        wlo = sb("w_lo", [P, 2, KT, P], F32R)
        f_hi = sb("ff_hi", [P, FT, HT], F32R)
        f_lo = sb("ff_lo", [P, FT, HT], F32R)
        sg = sb("silu_gate", [P, 2, HT])
        hf = sb("ff_f32", [P, 2, HT])
        ps = [ctx.enter_context(nc.psum_tensor(f"{tag}ps{p}", [P, 4, 512], F32)) for p in range(2)]
        w_in = [sem(f"w_in{p}") for p in range(2)]
        names = "hi lo done sig prod f_hi f_lo y_t yt_ps y_rows".split()
        e = {n: sem(n) for n in names}
        stored = [sem(f"stored{p}") for p in range(2)]
        block = ctx.enter_context(nc.Block())
        mod = keep["mod"]
        NU = 2 * FT
        PARTS = ((0, 8), (8, 15), (15, 22))
        tok0 = half * HT
        cp = lambda o, s: nc.scalar.activation(o, s, ACT.Copy)
        two = lambda a: a.rearrange("p (g n) -> p g n", g=2)

        def phases(eng, up, down):
            up(0, True, False)
            with eng.Fori(1, FT // 2 - 1) as i:
                up(i, False, False)
            up(FT // 2 - 1, False, True)
            for i in range(KT // 2):
                down(i, i == 0, i == KT // 2 - 1)

        @block.sync
        def _(sp):
            for t in range(2):
                sp.dma_start(raw[:, t], io["w_up"][t]).then_inc(w_in[t], 16)

            def up(i, first, last):
                for r in range(4):
                    t = 4 * i + r + 2
                    sp.wait_ge(e["lo"], t - 1)
                    if last and r >= 2:
                        load_part(0, r - 2, r - 2, r % 2)
                    else:
                        sp.dma_start(raw[:, r % 2], io["w_up"][bass.ds(t, 1)].rearrange("o p k n -> p (o k) n")).then_inc(w_in[r % 2], 16)

            def load_part(m, c, seq, slot):
                a, b = PARTS[c]
                src = io["w_down"][bass.ds(m, 1)].rearrange("o p k n -> p (o k) n")
                sp.dma_start(raw[:, slot, 0:b - a], src[:, a:b]).then_inc(w_in[slot], 16)

            def down(i, first, last):
                for q in range(2):
                    for c in range(3):
                        s = 3 * q + c + 2
                        if not (last and s >= 6):
                            sp.wait_ge(e["lo"], NU + 6 * i + s - 1)
                            load_part(2 * i + s // 3, s % 3, s, s % 2)
                    if not (first and q == 0):
                        store_rows(2 * i + q - 1, 1 - q)

            def store_rows(m, q):
                sp.wait_ge(e["y_rows"], m + 1)
                sp.dma_start(io["y"][tok0:tok0 + HT, bass.ds(m * P, P)].rearrange("(j p) n -> p j n", p=P), sg[:, q].rearrange("p (j n) -> p j n", n=P)).then_inc(stored[q], 16)

            phases(sp, up, down)
            store_rows(KT - 1, 1)
            for p in range(2):
                sp.wait_ge(stored[p], 16 * (KT // 2))

        @block.gpsimd
        def _(pool):
            def up(i, first, last):
                for q in range(2):
                    f = 2 * i + q
                    pool.wait_ge(e["f_hi"], f + 1)
                    nc.gpsimd.tensor_tensor(f_lo[:, bass.ds(f, 1)].rearrange("p o n -> p (o n)"), hf[:, q], f_hi[:, bass.ds(f, 1)].rearrange("p o n -> p (o n)").bitcast(F32), ALU.subtract).then_inc(e["f_lo"], 1)

            up(0, True, False)
            with pool.Fori(1, FT // 2) as i:
                up(i, False, False)

        @block.scalar
        def _(act):
            def split_hi(t, slot, arrivals, nk=KT, wait=True):
                act.wait_ge(w_in[slot], 16 * arrivals)
                if wait:
                    act.wait_ge(e["done"], t - 1)
                cp(whi[:, slot, 0:nk], raw[:, slot, 0:nk]).then_inc(e["hi"], 1)

            split_hi(0, 0, 1, wait=False)

            def up(i, first, last):
                for q in range(2):
                    f = 2 * i + q
                    split_hi(2 * f + 1, 1, f + 1, wait=not (first and q == 0))
                    act.wait_ge(e["done"], 2 * f + 1)
                    if not first:
                        act.wait_ge(e["prod"], f - 1)
                    nc.scalar.activation(two(sg[:, q]), ps[q][:, 0:2, 0:GN], ACT.Silu).then_inc(e["sig"], 1)
                    split_hi(2 * f + 2, 0, f + 2)
                    act.wait_ge(e["prod"], f + 1)
                    cp(f_hi[:, bass.ds(f, 1)].rearrange("p o n -> p (o n)"), hf[:, q]).then_inc(e["f_hi"], 1)

            def down(i, first, last):
                for q in range(2):
                    m = 2 * i + q
                    for c in range(3):
                        s = 3 * q + c + 1
                        if not (last and s == 6):
                            a, b = PARTS[s % 3]
                            split_hi(NU + 6 * i + s, s % 2, FT + 3 * i + s // 2 + 1, b - a)
                    if not (first and q == 0):
                        copy_rows(m - 1, 1 - q)

            def copy_rows(m, q):
                act.wait_ge(e["yt_ps"], m + 1)
                if m >= 2:
                    act.wait_ge(stored[q], 16 * (m // 2))
                cp(sg[:, q, 0:512], ps[q][:, 2])
                cp(sg[:, q, 512:HT], ps[q][:, 3, 0:P]).then_inc(e["y_rows"], 1)

            phases(act, up, down)
            copy_rows(KT - 1, 1)

        @block.vector
        def _(dve):
            def split_lo(t, slot, nk=KT, wait=True):
                dve.wait_ge(e["hi"], t + 1)
                if wait:
                    dve.wait_ge(e["done"], t - 1)
                nc.vector.tensor_tensor(wlo[:, slot, 0:nk], raw[:, slot, 0:nk], whi[:, slot, 0:nk].bitcast(F32), ALU.subtract).then_inc(e["lo"], 1)

            split_lo(0, 0, wait=False)

            def up(i, first, last):
                for q in range(2):
                    f = 2 * i + q
                    split_lo(2 * f + 1, 1, wait=not (first and q == 0))
                    split_lo(2 * f + 2, 0)
                    dve.wait_ge(e["sig"], f + 1)
                    dve.wait_ge(e["done"], 2 * f + 2)
                    if not first:
                        dve.wait_ge(e["f_lo"], f - 1)
                    nc.vector.tensor_tensor(two(hf[:, q]), ps[q][:, 2:4, 0:GN], two(sg[:, q]), ALU.mult).then_inc(e["prod"], 1)

            def down(i, first, last):
                for q in range(2):
                    m = 2 * i + q
                    for c in range(3):
                        s = 3 * q + c + 1
                        if not (last and s == 6):
                            a, b = PARTS[s % 3]
                            split_lo(NU + 6 * i + s, s % 2, b - a)
                    dve.wait_ge(e["done"], NU + 3 * m + 3)
                    if first:
                        dve.wait_ge(e["f_lo"], FT)
                    else:
                        dve.wait_ge(e["yt_ps"], m - 1)
                    for g in range(2):
                        for lo, hi, seg in half_segments(half, g * GN, (g + 1) * GN):
                            x1m = x1[:, bass.ds(m, 1), lo:hi].rearrange("p o n -> p (o n)")
                            gain = gate2[:, bass.ds(m, 1), seg].rearrange("p o -> p o")
                            last_ = nc.vector.scalar_tensor_tensor(hf[:, q, lo:hi], ps[q][:, g, lo - g * GN:hi - g * GN], gain, x1m, ALU.mult, ALU.add)
                    last_.then_inc(e["y_t"], 1)

            gate2 = mod[:, 40:48]
            phases(dve, up, down)

        @block.tensor
        def _(pe):
            part = lambda a, g: lambda k: a[:, k, g * GN:(g + 1) * GN]
            w = lambda a, p, k0=0: lambda k: a[:, p, k - k0]

            def up(i, first, last):
                for q in range(2):
                    f = 2 * i + q
                    for u in range(2):
                        pe.wait_ge(e["lo"], 2 * f + u + 1)
                        if not first:
                            pe.wait_ge(e["sig"] if u == 0 else e["prod"], f - 1)
                        for g in range(2):
                            ins = split_product(nc, ps[q][:, 2 * u + g, 0:GN], w(whi, u), w(wlo, u), part(h_hi, g), part(h_lo, g), range(KT))
                        ins.then_inc(e["done"], 1)

            def turn_y(m, q):
                pe.wait_ge(e["y_t"], m + 1)
                if m >= 2:
                    pe.wait_ge(e["y_rows"], m - 1)
                for j in range(HJ):
                    ins = nc.tensor.transpose(ps[q][:, 2 + j // 4, (j % 4) * P:(j % 4 + 1) * P], hf[:, q, j * P:(j + 1) * P], keep["ident"][:])
                ins.then_inc(e["yt_ps"], 1)

            def down(i, first, last):
                for q in range(2):
                    m = 2 * i + q
                    if first and q == 0:
                        pe.wait_ge(e["f_lo"], FT)
                    for c, (a, b) in enumerate(PARTS):
                        s = 3 * q + c
                        pe.wait_ge(e["lo"], NU + 6 * i + s + 1)
                        if c == 0:
                            if first:
                                pe.wait_ge(e["prod"], FT - 1 + q)
                            else:
                                pe.wait_ge(e["y_t"], m - 1)
                        for g in range(2):
                            ins = split_product(nc, ps[q][:, g, 0:GN], w(whi, s % 2, a), w(wlo, s % 2, a), part(f_hi, g), part(f_lo, g), range(a, b), first=(c == 0), last=(c == 2))
                        ins.then_inc(e["done"], 1)
                    if not (first and q == 0):
                        turn_y(m - 1, 1 - q)

            phases(pe, up, down)
            turn_y(KT - 1, 1)


def merge_and_ffn(nc, io, keep):
    for half in range(2):
        with ExitStack() as ctx:
            x1 = ctx.enter_context(nc.sbuf_tensor(f"x1_{half}", [P, KT, HT], F32))
            h_hi = ctx.enter_context(nc.sbuf_tensor(f"h2_hi{half}", [P, KT, HT], F32R))
            h_lo = ctx.enter_context(nc.sbuf_tensor(f"h2_lo{half}", [P, KT, HT], F32R))
            mix_out(nc, io, keep, half, x1, h_hi, h_lo)
            feed_forward(nc, io, keep, half, x1, h_hi, h_lo)


def build(nc, io):
    with ExitStack() as ctx:
        sb = lambda n, s, d=F32: ctx.enter_context(nc.sbuf_tensor(n, s, d))
        keep = {
            "ident": sb("ident_sb", [P, P]),
            "mod": sb("mod", [P, 48, 2]),
            "mod_scale": sb("mod_scale", [P, 2, KT, 2]),
            "bg": sb("beta_gate_cols", [P, NT, 32]),
            "ones": sb("ones_sb", [P, P]),
        }
        keep["first_sem"] = ctx.enter_context(nc.semaphore("first_sem"))
        with ExitStack() as c1:
            h_hi = c1.enter_context(nc.sbuf_tensor("h_hi", [P, KT, T], F32R))
            h_lo = c1.enter_context(nc.sbuf_tensor("h_lo", [P, KT, T], F32R))
            keep["c_act"] = c1.enter_context(nc.sbuf_tensor("c_silu", [P, KT, 2], F32))
            keep["b_ada"] = c1.enter_context(nc.sbuf_tensor("b_ada_sb", [P, 48], F32))
            keep["gains"] = c1.enter_context(nc.sbuf_tensor("norm_gains", [P, 2, KT], F32))
            ada_and_norm(nc, io, keep, h_hi, h_lo)
            in_projection(nc, io, keep, h_hi, h_lo)
        with ExitStack() as c2:
            sb2 = lambda n, s, d=F32: c2.enter_context(nc.sbuf_tensor(n, s, d))
            keep["tri"] = sb2("tri_sb", [P, 2, P])
            keep["offdiag"] = sb2("offdiag_sb", [P, P])
            keep["maskneg"] = sb2("maskneg_sb", [P, 2, P])
            keep["levels"] = sb2("levels_sb", [P, LEVELS, 2, P])
            tab = sb2("scalar_table", [P, 2, NT, SCW])
            o_rows = sb2("o_rows", [P, 2, NT, 512])
            delta_rows(nc, io, keep)
            delta_scalars(nc, io, keep, tab)
            delta_scan(nc, io, keep, tab, o_rows)
            delta_gate(nc, io, keep, o_rows)
        attention(nc, io, keep)
        merge_and_ffn(nc, io, keep)


def tiles_of(w):
    k, n = w.shape
    return np.ascontiguousarray(w.reshape(k // P, P, n // P, P).transpose(2, 1, 0, 3))


def constants():
    i = np.arange(P)
    tri = (i[:, None] <= i[None, :]).astype(np.float32)
    tri = np.stack([tri, tri.T], 1)
    levels = np.zeros((P, LEVELS, 2, P), np.float32)
    for lv in range(LEVELS):
        s = 2 ** lv
        b = i // s
        low = (b[:, None] // 2 == b[None, :] // 2) & (b[:, None] % 2 == 1) & (b[None, :] % 2 == 0)
        levels[:, lv, 0], levels[:, lv, 1] = low, low.T
    t = np.arange(LAT)
    inv = (np.float32(10000.0) ** (-np.arange(16, dtype=np.float32) / 16)).astype(np.float32)
    ang = np.stack([t // 64, t % 64], 1).astype(np.float32)[:, :, None] * inv
    cos = np.concatenate([np.cos(ang), np.cos(ang)], 2).reshape(LAT, HD)
    sin = np.concatenate([-np.sin(ang), np.sin(ang)], 2).reshape(LAT, HD)
    rope = np.stack([cos, sin], 1).astype(np.float32).reshape(8, P, 2, HD)
    return {
        "ident": np.eye(P, dtype=np.float32),
        "ones": np.ones((P, P), np.float32),
        "tri": tri,
        "offdiag": 1 - np.eye(P, dtype=np.float32),
        "maskneg": (1 - tri) * np.float32(-1e30),
        "levels": levels,
        "rope_tiles": rope,
        "rope_rows": rope.transpose(1, 2, 0, 3),
    }


def laid_out(inp):
    a = {k: np.asarray(v) for k, v in inp.items()}
    w = a["w_in"][0]
    cols = np.concatenate([np.arange(768, 2304), np.arange(0, 768), np.arange(2304, 2816), np.arange(2848, 4896)])
    paired = lambda s: s.reshape(4, 2, HD, HD).transpose(1, 2, 0, 3).reshape(P, 4, HD)
    out = constants() | {
        "x": np.concatenate([a["x_prompt"][0], a["x_sample"][0]], 0),
        "c_t": np.stack([a["c_ctx"].reshape(KT, P).T, a["c"][0].reshape(KT, P).T], -1),
        "w_ada": tiles_of(a["w_ada"][0]),
        "b_ada": a["b_ada"][0].reshape(48, P).T,
        "gains": np.stack([a["norm1_g"][0].reshape(KT, P).T, a["norm2_g"][0].reshape(KT, P).T], 1),
        "w_in": tiles_of(w[:, cols]),
        "w_bg": w[:, 2816:2848].reshape(KT, P, 32).transpose(1, 0, 2),
        "conv_w": a["conv_w"][0].T.reshape(CONV_TILES, P, CONV).transpose(1, 0, 2),
        "decay_params": np.broadcast_to(np.stack([a["a_log"][0].reshape(16), a["dt_bias"][0].reshape(16)]), (P, 2, 16)),
        "dn_g": np.tile(a["dn_norm_g"][0], 2).reshape(P, 1),
        "cache_k": a["cache_k"][0, 0].reshape(PAST, P),
        "cache_v": a["cache_v"][0, 0].reshape(PAST, P),
        "k_gain": np.broadcast_to(a["k_norm_g"][0], (P, HD)),
        "q_gain": np.broadcast_to(a["q_norm_g"][0], (P, HD)),
        "w_mix": np.concatenate([tiles_of(np.concatenate([a["w_pa"][0], a["w_pb"][0]], 0)), tiles_of(a["w_o"][0])], 0),
        "w_up": np.stack([tiles_of(a["w_gate"][0]), tiles_of(a["w_up"][0])], 1).reshape(2 * FT, P, KT, P),
        "w_down": tiles_of(a["w_down"][0]),
        "state_in": np.stack([paired(a["state_fwd"][0, 0]), paired(a["state_bwd"][0, 0])]),
    }
    return {k: np.ascontiguousarray(v) for k, v in out.items()}


SCRATCH = {"conv_t": (CONV_TILES, P, T), "proj_t": (REST_TILES, P, T), "delta_t": (NT, P, TW), "od_t": (4, P, T), "oa_t": (4, P, T)}
RESULTS = {"state_out": (2, P, 4, HD), "new_k": (CTX, P), "new_v": (CTX, P), "y": (T, D)}


def kernel(**inputs):
    import concourse.bacc as bacc
    from concourse.bass_utils import run_bass_kernel_spmd

    nc = bacc.Bacc("TRN2", target_bir_lowering=False, num_devices=1)
    data = laid_out(inputs)
    io = {n: nc.dram_tensor(f"{n}_dram", a.shape, mybir.dt.from_np(a.dtype), kind="ExternalInput").ap() for n, a in data.items()}
    for n, shape in SCRATCH.items():
        io[n] = nc.dram_tensor(n, shape, F32, kind="Internal").ap()
    for n, shape in RESULTS.items():
        io[n] = nc.dram_tensor(f"{n}_out", shape, F32, kind="ExternalOutput").ap()
    build(nc, io)
    res = run_bass_kernel_spmd(nc, [{f"{n}_dram": a for n, a in data.items()}], core_ids=[0]).results[0]
    y = res["y_out"]
    kv = lambda a: a.reshape(1, CTX, 1, 2, HD).transpose(0, 2, 1, 3, 4)
    state = res["state_out_out"].reshape(2, 2, HD, 4, HD).transpose(0, 3, 1, 2, 4).reshape(2, 1, 1, NH, HD, HD)
    return y[None, :CTX], y[None, CTX:], kv(res["new_k_out"]), kv(res["new_v_out"]), state[0], state[1]
```
